# Optimizing a Trainium2 kernel written in Bass

```python
import math
import jax, jax.numpy as jnp
from jax import lax
import numpy as np

D_MODEL = 1024
BATCH = 1
SEQ = 512
DEPTH = 1

HG_HEADS = 8
HG_DK = 128
HG_DV = D_MODEL // HG_HEADS
HG_KWIDTH = HG_HEADS * HG_DK
HG_VWIDTH = HG_HEADS * HG_DV
HG_CHUNK = 64

AT_Q_HEADS = 16
AT_KV_HEADS = 4
AT_HEAD_DIM = D_MODEL // AT_Q_HEADS
AT_GROUP = AT_Q_HEADS // AT_KV_HEADS
WINDOW = 128
AT_BLOCK = WINDOW
AT_QWIDTH = AT_Q_HEADS * AT_HEAD_DIM
AT_KVWIDTH = AT_KV_HEADS * AT_HEAD_DIM

N_EXPERTS = 32
TOP_K = 4
D_FF_EXPERT = D_MODEL
SWIGLU_LIMIT = 7.0
SWIGLU_ALPHA = 1.702
MOE_BLOCK = 128

NORM_EPS = 1e-5

IN_SIZES = (HG_KWIDTH, HG_KWIDTH, HG_KWIDTH, HG_VWIDTH, HG_VWIDTH, AT_QWIDTH, AT_KVWIDTH, AT_KVWIDTH, D_MODEL, D_MODEL)
IN_WIDTH = sum(IN_SIZES)
IN_SPLITS = tuple(int(c) for c in np.cumsum(IN_SIZES)[:-1])

kernel_name = 'hybrid_hgrn2_swa_moe_encoder_block'

def rms_norm(x, gain):
    xf = x.astype(jnp.float32)
    y = xf * lax.rsqrt(jnp.mean(xf * xf, axis=-1, keepdims=True) + NORM_EPS)
    return (y * gain.astype(jnp.float32)).astype(x.dtype)

def gla_chunkwise(q, k, v, log_f):
    bsz, seqlen, nh, dk = q.shape
    dv = v.shape[-1]
    n_chunks = seqlen // HG_CHUNK

    def chunks(t):
        return t.reshape(bsz, n_chunks, HG_CHUNK, nh, t.shape[-1]).transpose(0, 3, 1, 2, 4)

    qc = chunks(q).astype(jnp.float32)
    kc = chunks(k).astype(jnp.float32)
    vc = chunks(v).astype(jnp.float32)
    cum = jnp.cumsum(chunks(log_f).astype(jnp.float32), axis=3)
    last = cum[:, :, :, -1:, :]
    q_dec = qc * jnp.exp(cum)
    k_inv = kc * jnp.exp(-cum)
    k_end = kc * jnp.exp(last - cum)
    decay = jnp.exp(last[:, :, :, 0, :])
    tri = jnp.tril(jnp.ones((HG_CHUNK, HG_CHUNK), dtype=bool))
    scores = jnp.where(tri, jnp.einsum('bhncd,bhnsd->bhncs', q_dec, k_inv), 0.0)
    o_intra = jnp.einsum('bhncs,bhnsv->bhncv', scores, vc)

    def step(state, inp):
        qd, ke, vv, dec = inp
        o_inter = jnp.einsum('bhcd,bhdv->bhcv', qd, state)
        state = dec[..., None] * state + jnp.einsum('bhcd,bhcv->bhdv', ke, vv)
        return state, o_inter

    s0 = jnp.zeros((bsz, nh, dk, dv), jnp.float32)
    xs = (jnp.moveaxis(q_dec, 2, 0), jnp.moveaxis(k_end, 2, 0), jnp.moveaxis(vc, 2, 0), jnp.moveaxis(decay, 2, 0))
    _, o_inter = lax.scan(step, s0, xs)
    o = o_intra + jnp.moveaxis(o_inter, 0, 2)
    return o.transpose(0, 2, 3, 1, 4).reshape(bsz, seqlen, nh, dv)

def hgrn2_mixer(q_pre, f_fwd_pre, f_bwd_pre, i_val, g_pre, lb_fwd, lb_bwd, gnorm_gain):
    bsz, seqlen, _ = q_pre.shape

    def heads(t, d):
        return t.reshape(bsz, seqlen, HG_HEADS, d)

    q = heads(jax.nn.silu(q_pre), HG_DK)
    v = heads(i_val, HG_DV)

    def gate(f_pre, lb):
        f = lb + (1.0 - lb) * jax.nn.sigmoid(f_pre.astype(jnp.float32))
        return heads(1.0 - f, HG_DK), heads(jnp.log(f), HG_DK)

    k_fwd, logf_fwd = gate(f_fwd_pre, lb_fwd)
    k_bwd, logf_bwd = gate(f_bwd_pre, lb_bwd)
    flip = lambda t: jnp.flip(t, axis=1)
    o = gla_chunkwise(q, k_fwd, v, logf_fwd) + flip(gla_chunkwise(flip(q), flip(k_bwd), flip(v), flip(logf_bwd)))
    o = o * lax.rsqrt(jnp.mean(o * o, axis=-1, keepdims=True) + NORM_EPS) * gnorm_gain.astype(jnp.float32)
    o = o.reshape(bsz, seqlen, HG_VWIDTH) * jax.nn.silu(g_pre.astype(jnp.float32))
    return o.astype(q_pre.dtype)

def window_attention(q_pre, k_pre, v_pre, sink):
    bsz, seqlen, _ = q_pre.shape
    nb = seqlen // AT_BLOCK
    span = 3 * AT_BLOCK
    q = q_pre.reshape(bsz, nb, AT_BLOCK, AT_KV_HEADS, AT_GROUP, AT_HEAD_DIM)

    def band(t):
        t = t.reshape(bsz, seqlen, AT_KV_HEADS, AT_HEAD_DIM)
        t = jnp.pad(t, ((0, 0), (AT_BLOCK, AT_BLOCK), (0, 0), (0, 0)))
        t = t.reshape(bsz, nb + 2, AT_BLOCK, AT_KV_HEADS, AT_HEAD_DIM)
        return jnp.concatenate([t[:, :-2], t[:, 1:-1], t[:, 2:]], axis=2)

    kb, vb = band(k_pre), band(v_pre)
    s = jnp.einsum('bnqkgd,bnskd->bnkgqs', q, kb).astype(jnp.float32) * (AT_HEAD_DIM ** -0.5)
    rel = (jnp.arange(AT_BLOCK)[:, None] + AT_BLOCK) - jnp.arange(span)[None, :]
    key_pos = jnp.arange(nb)[:, None] * AT_BLOCK - AT_BLOCK + jnp.arange(span)[None, :]
    valid = (jnp.abs(rel) <= WINDOW)[None] & ((key_pos >= 0) & (key_pos < seqlen))[:, None, :]
    slopes = jnp.exp2(-8.0 * jnp.arange(1, AT_Q_HEADS + 1, dtype=jnp.float32) / AT_Q_HEADS)
    alibi = (-slopes[:, None, None] * jnp.abs(rel).astype(jnp.float32)).reshape(AT_KV_HEADS, AT_GROUP, AT_BLOCK, span)
    s = jnp.where(valid[None, :, None, None], s + alibi, -jnp.inf)
    sink_l = sink.astype(jnp.float32).reshape(1, 1, AT_KV_HEADS, AT_GROUP, 1, 1)
    m = jnp.maximum(jnp.max(s, axis=-1, keepdims=True), sink_l)
    p = jnp.exp(s - m)
    p = p / (jnp.sum(p, axis=-1, keepdims=True) + jnp.exp(sink_l - m))
    o = jnp.einsum('bnkgqs,bnskd->bnqkgd', p.astype(vb.dtype), vb)
    return o.reshape(bsz, seqlen, AT_QWIDTH)

def moe_ffn(xn, w_router, b_router, w_up_gate, b_up_gate, w_down, b_down):
    bsz, seqlen, d = xn.shape
    n_tok = bsz * seqlen
    n_assign = n_tok * TOP_K
    n_pad = n_assign + N_EXPERTS * MOE_BLOCK
    n_blocks = n_pad // MOE_BLOCK
    xt = xn.reshape(n_tok, d)
    logits = xt.astype(jnp.float32) @ w_router.astype(jnp.float32) + b_router.astype(jnp.float32)
    top_val, top_idx = lax.top_k(logits, TOP_K)
    gates = jax.nn.softmax(top_val, axis=-1)
    flat_e = top_idx.reshape(-1).astype(jnp.int32)
    flat_tok = jnp.repeat(jnp.arange(n_tok, dtype=jnp.int32), TOP_K)
    order = jnp.argsort(flat_e)
    sorted_e = flat_e[order]
    counts = jnp.bincount(flat_e, length=N_EXPERTS).astype(jnp.int32)
    padded = (counts + MOE_BLOCK - 1) // MOE_BLOCK * MOE_BLOCK
    grp_start = jnp.cumsum(counts) - counts
    pad_end = jnp.cumsum(padded)
    pad_start = pad_end - padded
    dest = (pad_start[sorted_e] + jnp.arange(n_assign, dtype=jnp.int32) - grp_start[sorted_e]).astype(jnp.int32)
    rows_tok = jnp.zeros((n_pad,), jnp.int32).at[dest].set(flat_tok[order])
    block_expert = jnp.minimum(jnp.searchsorted(pad_end, jnp.arange(n_blocks, dtype=jnp.int32) * MOE_BLOCK, side='right'), N_EXPERTS - 1)
    xb = xt[rows_tok].reshape(n_blocks, MOE_BLOCK, d)

    def expert_block(args):
        xblk, e = args
        hu = xblk @ w_up_gate[e] + b_up_gate[e]
        g, u = hu[:, :D_FF_EXPERT], hu[:, D_FF_EXPERT:]
        g = jnp.minimum(g, SWIGLU_LIMIT)
        u = jnp.clip(u, -SWIGLU_LIMIT, SWIGLU_LIMIT)
        act = g * jax.nn.sigmoid(SWIGLU_ALPHA * g) * (u + 1.0)
        return act @ w_down[e] + b_down[e]

    yb = lax.map(expert_block, (xb, block_expert)).reshape(n_pad, d)
    dest_of_assign = jnp.zeros((n_assign,), jnp.int32).at[order].set(dest)
    y = yb[dest_of_assign].reshape(n_tok, TOP_K, d)
    out = jnp.einsum('tk,tkd->td', gates.astype(y.dtype), y)
    return out.reshape(bsz, seqlen, d)

def setup_inputs(seed: int = 0) -> dict:
    key = jax.random.key(seed)
    ks = jax.random.split(key, 16)
    f32 = jnp.float32

    def nrm(k, shape, scale):
        return scale * jax.random.normal(k, shape, f32)

    x = jax.random.normal(ks[0], (BATCH, SEQ, D_MODEL), f32)
    norm_mix_gain = 1.0 + nrm(ks[1], (DEPTH, D_MODEL), 0.01)
    w_in = nrm(ks[2], (DEPTH, D_MODEL, IN_WIDTH), D_MODEL ** -0.5)
    hg_lb_fwd = nrm(ks[3], (DEPTH + 1, HG_KWIDTH), 0.1)
    hg_lb_bwd = nrm(ks[4], (DEPTH + 1, HG_KWIDTH), 0.1)
    hg_norm_gain = 1.0 + nrm(ks[5], (DEPTH, HG_DV), 0.01)
    attn_sink = nrm(ks[6], (DEPTH, AT_Q_HEADS), 0.5)
    w_out = nrm(ks[7], (DEPTH, D_MODEL, D_MODEL), D_MODEL ** -0.5)
    norm_ffn_gain = 1.0 + nrm(ks[8], (DEPTH, D_MODEL), 0.01)
    w_router = nrm(ks[9], (DEPTH, D_MODEL, N_EXPERTS), D_MODEL ** -0.5)
    b_router = nrm(ks[10], (DEPTH, N_EXPERTS), 0.01)
    w_up_gate = nrm(ks[11], (DEPTH, N_EXPERTS, D_MODEL, 2 * D_FF_EXPERT), D_MODEL ** -0.5)
    b_up_gate = nrm(ks[12], (DEPTH, N_EXPERTS, 2 * D_FF_EXPERT), 0.01)
    w_down = nrm(ks[13], (DEPTH, N_EXPERTS, D_FF_EXPERT, D_MODEL), D_FF_EXPERT ** -0.5)
    b_down = nrm(ks[14], (DEPTH, N_EXPERTS, D_MODEL), 0.01)
    final_norm_gain = 1.0 + nrm(ks[15], (D_MODEL,), 0.01)
    return {'x': x, 'norm_mix_gain': norm_mix_gain, 'w_in': w_in, 'hg_lb_fwd': hg_lb_fwd,
            'hg_lb_bwd': hg_lb_bwd, 'hg_norm_gain': hg_norm_gain, 'attn_sink': attn_sink,
            'w_out': w_out, 'norm_ffn_gain': norm_ffn_gain, 'w_router': w_router,
            'b_router': b_router, 'w_up_gate': w_up_gate, 'b_up_gate': b_up_gate,
            'w_down': w_down, 'b_down': b_down, 'final_norm_gain': final_norm_gain}

def reference(x, norm_mix_gain, w_in, hg_lb_fwd, hg_lb_bwd, hg_norm_gain, attn_sink, w_out,
              norm_ffn_gain, w_router, b_router, w_up_gate, b_up_gate, w_down, b_down,
              final_norm_gain):
    lb_fwd_all = jnp.cumsum(jax.nn.softmax(hg_lb_fwd.astype(jnp.float32), axis=0), axis=0)
    lb_bwd_all = jnp.cumsum(jax.nn.softmax(hg_lb_bwd.astype(jnp.float32), axis=0), axis=0)
    h = x
    for layer in range(DEPTH):
        xn = rms_norm(h, norm_mix_gain[layer])
        proj = xn @ w_in[layer]
        hq, hf_fwd, hf_bwd, hi, hg, aq, ak, av, gate_a, gate_b = jnp.split(proj, IN_SPLITS, axis=-1)
        y_rec = hgrn2_mixer(hq, hf_fwd, hf_bwd, hi, hg, lb_fwd_all[layer], lb_bwd_all[layer], hg_norm_gain[layer])
        y_att = window_attention(aq, ak, av, attn_sink[layer])
        merged = jax.nn.sigmoid(gate_a) * y_rec + jax.nn.sigmoid(gate_b) * y_att
        h = h + merged @ w_out[layer]
        h = h + moe_ffn(rms_norm(h, norm_ffn_gain[layer]), w_router[layer], b_router[layer],
                        w_up_gate[layer], b_up_gate[layer], w_down[layer], b_down[layer])
    return rms_norm(h, final_norm_gain)


_drawn_inputs = setup_inputs


def setup_inputs(seed=0):
    import zlib

    import numpy as np

    out = dict(_drawn_inputs(seed))
    spreads = {}
    factors = {'hg_lb_fwd': 3.345,
     'hg_lb_bwd': 3.364,
     'hg_norm_gain': 2.938,
     'b_up_gate': 8.0,
     'b_down': 8.0,
     'final_norm_gain': 5.719}
    for name, (base, spread) in spreads.items():
        noise = np.random.default_rng([zlib.crc32(name.encode()), seed]).standard_normal(out[name].shape)
        drawn = base * np.exp(spread * noise) if base else spread * noise
        out[name] = __import__('jax').numpy.asarray(drawn.astype(out[name].dtype))
    for name, factor in factors.items():
        out[name] = (out[name] * factor).astype(out[name].dtype)
    return out
```

```python
from contextlib import ExitStack

import numpy as np

import concourse.bass as bass
from concourse import mybir

F32, F32R, BF16 = mybir.dt.float32, mybir.dt.float32r, mybir.dt.bfloat16
I32, U32 = mybir.dt.int32, mybir.dt.uint32
ALU, ACT, AX = mybir.AluOpType, mybir.ActivationFunctionType, mybir.AxisListType

P = 128
T, D = 512, 1024
NT, KD = T // P, D // P
NH = 8
CH = 64
NCH = T // CH
QH, KVH, DH = 16, 4, 64
WIN = 128
NE, TOPK, FF = 32, 4, 1024
RS_MAX = 1 + NT + NT + 2
BIAS_STEPS = 9
BLK = 128
NB = T // BLK
MAXOVER = T * TOPK // BLK - 1
LIMIT, ALPHA = 7.0, 1.702
EPS = 1e-5
NONE = 1 << 20
SCALE = DH ** -0.5

C_Q, C_FF, C_FB, C_V, C_G = 0, D, 2 * D, 3 * D, 4 * D
C_AQ = 5 * D
C_AK = C_AQ + QH * DH
C_AV = C_AK + KVH * DH
C_GA = C_AV + KVH * DH
C_GB = C_GA + D

K_ID, K_TF, K_TB, K_KF, K_KB, K_REL, K_SL, K_IO, K_LT, K_ON, K_CD, K_P1, K_END = np.cumsum(
    [0, P, P, P, T, T, 3 * P, QH, NE, P, P, 3 * NE, 1]).tolist()
R_LF, R_LB, R_NG, R_FG, R_END = 0, 16, 32, 40, 48


def constants():
    c = np.zeros((P, K_END), np.float32)
    i, s = np.arange(P), np.arange(P)[:, None]
    c[:, K_ID:K_TF] = np.eye(P)
    same = (i[None] // CH) == (s // CH)
    c[:, K_TF:K_TB] = same & (s <= i[None])
    c[:, K_TB:K_KF] = same & (s >= i[None])
    t = np.arange(T)
    c[:, K_KF:K_KB] = t % CH != 0
    c[:, K_KB:K_REL] = t % CH != CH - 1
    rel = np.abs(s + WIN - np.arange(3 * P)[None])
    c[:, K_REL:K_SL] = np.where(rel <= WIN, -rel, -1e30)
    c[:, K_SL:K_IO] = 2.0 ** (-8.0 * np.arange(1, QH + 1) / QH) / SCALE
    c[:, K_IO:K_LT] = np.arange(NE)
    c[:, K_LT:K_ON] = s < i[None]
    c[:, K_ON:K_CD] = 1.0
    c[:, K_CD:K_P1] = (np.arange(NE)[:, None] * NB + np.arange(1, NB)[None]).ravel()
    c[:, K_P1] = np.arange(P) + 1
    return c


def bias_selectors():
    one = 0x3F80
    sel = np.zeros((NE, 3 * NE, P), np.uint16)
    for part in range(3):
        sel[np.arange(NE), part * NE + np.arange(NE)] = one
    return sel


def build(nc, x, norm_mix_gain, w_in, hg_lb_fwd, hg_lb_bwd, hg_norm_gain, attn_sink, w_out,
          norm_ffn_gain, w_router, b_router, w_up_gate, b_up_gate, w_down, b_down,
          final_norm_gain, consts, selectors, out):
    w_in, w_out = w_in[0], w_out[0]
    slots = nc.dram_tensor("slots", [P * NE * NB, 2], I32, kind="Internal").ap()
    over_list = nc.dram_tensor("over_list", [P, 1], I32, kind="Internal").ap()
    x2d = nc.dram_tensor("x2d", [T, D], F32, kind="Internal").ap()
    yd = nc.dram_tensor("yd", [TOPK * T, D], F32, kind="Internal").ap()

    BASE = 16512
    at = [BASE]

    def sb(name, shape, dt=F32):
        size = int(np.prod(shape[1:])) * (2 if dt == BF16 else 4)
        t = nc.alloc_sbuf_tensor_at(name, shape, dt, offset=at[0])
        at[0] += -(-size // 32) * 32
        return t

    cst = sb("cst", [P, K_END])
    vecs = sb("vecs", [P, R_END])
    rows = sb("rows", [R_END, P])
    lbs = sb("lbs", [P, 8, 16])
    fa = sb("fa", [P, 16])
    fb_ = sb("fb_", [P, 16])
    fn = sb("fn", [P, 16])
    fk = sb("fk", [P, 16])
    stat = sb("stat", [P, 64])
    small_top = at[0]

    xnH = sb("xnH", [P, KD, T], F32R)
    xnL = sb("xnL", [P, KD, T], F32R)
    fraw = sb("fraw", [P, 4, KD, P])
    tsH = sb("tsH", [P, KD, 4, P], F32R)
    tsL = sb("tsL", [P, KD, 4, P], F32R)
    wsH = sb("wsH", [P, 2, KD, P], F32R)
    wsL = sb("wsL", [P, 2, KD, P], F32R)
    front_w_top = at[0]
    merged = sb("merged", [P, NT, D])
    front_work = at[0]
    thF = sb("thF", [P, T]); thB = sb("thB", [P, T])
    qp = sb("qp", [P, T])
    fF = sb("fF", [P, T]); fB = sb("fB", [P, T])
    kF = sb("kF", [P, T]); kB = sb("kB", [P, T])
    qdF = sb("qdF", [P, T]); qdB = sb("qdB", [P, T])
    kiF = sb("kiF", [P, T]); kiB = sb("kiB", [P, T])
    dcF = sb("dcF", [P, NCH]); dcB = sb("dcB", [P, NCH])
    ktF = sb("ktF", [P, NT, P]); ktB = sb("ktB", [P, NT, P])
    scF = sb("scF", [P, NT, P]); scB = sb("scB", [P, NT, P])
    SF = sb("SF", [P, NCH, P]); SB = sb("SB", [P, NCH, P])
    vv = sb("vv", [P, NT, P])
    vab = sb("vab", [P, NT, 2, P])
    tht = sb("tht", [P, NT, 3, P])
    G1 = sb("G1", [P, NT, P])
    aqT = sb("aqT", [P, T])
    kdup = sb("kdup", [P, KVH, T])
    kcur = sb("kcur", [P, T])
    av = sb("av", [P, NT, KVH * DH])
    vcur = sb("vcur", [P, NT, DH])
    sbuf_s = sb("sbuf_s", [P, 2, 3 * P])
    sbuf_p = sb("sbuf_p", [P, 2, 3 * P])
    pTs = sb("pTs", [P, 2, 3, P])
    gainq = sb("gainq", [P, P])
    sinkb = sb("sinkb", [P, QH])
    nsink = sb("nsink", [P, QH])
    att = sb("att", [P, 64])
    orow = sb("orow", [P, 16])
    ogt = sb("ogt", [P, NT, P])
    attn1 = sb("attn1", [P, NT, P])
    assert at[0] <= 229368, at[0]
    at[0] = front_work
    xt = sb("xt", [P, NT, D])
    junk = sb("junk", [P, D])

    at[0] = small_top
    uraw = sb("uraw", [P, 4, 2 * FF])
    draw = sb("draw", [P, 2, 2, D])
    uH = sb("uH", [P, 2, 2 * FF], F32R)
    uL = sb("uL", [P, 2, 2 * FF], F32R)
    dH = sb("dH", [P, 2, 2, D], F32R)
    dL = sb("dL", [P, 2, 2, D], F32R)
    moe_w_top = at[0]
    at[0] = max(moe_w_top, front_w_top)
    at[0] = max(at[0], front_work)
    hres = sb("hres", [P, NT, D])
    bias = sb("bias", [3 * NE, 3 * D], BF16)
    tab = sb("tab", [P, NE * NB, 2], I32)
    sel = sb("sel", [3 * NE, 2, P], BF16)
    ixg = sb("ixg", [P, 2], I32)
    ixs = sb("ixs", [P, 2], I32)
    gates = sb("gates", [P, NT, TOPK])
    regs_in = sb("regs_in", [P, 4], I32)
    done = sb("done", [P, 1])
    fgain = sb("fgain", [P, D])
    moe_work = at[0]
    mTH = sb("mTH", [P, KD, T], F32R)
    mTL = sb("mTL", [P, KD, T], F32R)
    ngain = sb("ngain", [P, D])
    xr = sb("xr", [P, 2, D])
    mid_top = at[0]
    at[0] = moe_work
    rT = sb("rT", [P, KD, T])
    wr = sb("wr", [P, KD, NE])
    brb = sb("brb", [P, NE])
    lg = sb("lg", [P, NT, NE])
    v8 = sb("v8", [P, NT, 8])
    i8 = sb("i8", [P, NT, 8], U32)
    idf = sb("idf", [P, NT, 8])
    oh = sb("oh", [P, NT, TOPK, NE])
    msk = sb("msk", [P, NT, NE])
    msum = sb("msum", [P, NE])
    ps_ = sb("ps_", [P, NT, NE])
    pk = sb("pk", [P, NT, TOPK, NE])
    posk = sb("posk", [P, NT * TOPK])
    blk_ = sb("blk_", [P, 3, NT * TOPK])
    rowf = sb("rowf", [P, NT * TOPK])
    rowi = sb("rowi", [P, NT * TOPK], I32)
    pay = sb("pay", [P, NT * TOPK, 2], I32)
    fill = sb("fill", [P, NE * NB * 2], I32)
    gst = sb("gst", [P, NT, 8])
    ovf = sb("ovf", [P, 4, NE * (NB - 1)])
    ovc = sb("ovc", [P, 4])
    ovi = sb("ovi", [P, 2], I32)
    assert at[0] <= moe_work + 32768, at[0] - moe_work
    at[0] = moe_work
    xg = sb("xg", [P, D])
    xTH = sb("xTH", [P, KD, P], F32R)
    xTL = sb("xTL", [P, KD, P], F32R)
    gcl = sb("gcl", [P, FF]); ucl = sb("ucl", [P, FF]); sg = sb("sg", [P, FF]); actv = sb("actv", [P, FF])
    aTH = sb("aTH", [P, KD, P], F32R)
    aTL = sb("aTL", [P, KD, P], F32R)
    ysb = sb("ysb", [P, D])
    moe_top = at[0]
    at[0] = mid_top
    braw = sb("braw", [3 * NE, 3 * D])
    assert at[0] <= 229368, (at[0], 'braw')
    at[0] = small_top
    yk = sb("yk", [P, 2, TOPK, D])
    acc = sb("acc", [P, 2, D])
    fin = sb("fin", [P, 2, D])

    nc_psum = nc.alloc_psum_tensor("psum", [P, 8 * 512], F32)
    bank = [nc_psum[:, i * 512:(i + 1) * 512] for i in range(8)]

    def sem(name):
        return nc.alloc_semaphore(name)

    def sems(name, n):
        return [sem(f"{name}{i}") for i in range(n)]

    ident = cst[:, K_ID:K_TF]
    gain_mix = [vecs[:, R_NG + k:R_NG + k + 1] for k in range(KD)]

    def mm3(ps, lh, ll, rh, rl, start, stop):
        nc.tensor.matmul(ps, lh, rh, start=start, stop=False)
        nc.tensor.matmul(ps, lh, rl, start=False, stop=False)
        return nc.tensor.matmul(ps, ll, rh, start=False, stop=stop)

    cst_in, vec_in, bc_in = sem("cst_in"), sem("vec_in"), sem("bc_in")
    x_in = sems("x_in", NT)
    fraw_in, uraw_in, draw_in = sems("fraw_in", 4), sems("uraw_in", 4), sems("draw_in", 2)
    kdup_in = sem("kdup_in")
    sq0, ms0, sd0, rs0, xn0 = sem("sq0"), sem("ms0"), sem("sd0"), sem("rs0"), sem("xn0")
    xt_done, xh_done, xl_done = sem("xt_done"), sem("xh_done"), sem("xl_done")
    vecT_done, vec_ready, lb_step, lb_exp = sem("vecT_done"), sem("vec_ready"), sem("lb_step"), sem("lb_exp")
    zeroed = sem("zeroed")
    w_hi, w_lo, proj_done = sem("w_hi"), sem("w_lo"), sem("proj_done")
    kd_ready, av_ready = sem("kd_ready"), sem("av_ready")
    th_ready, f_ready, k_ready, ln_ready, cum_ready = sem("th_ready"), sem("f_ready"), sem("k_ready"), sem("ln_ready"), sem("cum_ready")
    q_ready, ec_ready, dc_ready, qk_ready = sem("q_ready"), sem("ec_ready"), sem("dc_ready"), sem("qk_ready")
    kT_done, kt_ready, sc_done, sc_ready = sem("kT_done"), sem("kt_ready"), sem("sc_done"), sem("sc_ready")
    U_done, st_ready, o_done = sem("U_done"), sem("st_ready"), sem("o_done")
    tht_ready, v_ready, ts_free, G1_step, G1_ready, vab_ready = sem("tht_ready"), sem("v_ready"), sem("ts_free"), sem("G1_step"), sem("G1_ready"), sem("vab_ready")
    osq_ready, oms_step, osd_ready, ors_ready, og_ready, mg_ready = sem("osq_ready"), sem("oms_step"), sem("osd_ready"), sem("ors_ready"), sem("og_ready"), sem("mg_ready")
    aq_ready, kcur_ready, vcur_ready = sem("aq_ready"), sem("kcur_ready"), sem("vcur_ready")
    s_done, s_ready, mx_ready, nm_ready, p_ready = sem("s_done"), sem("s_ready"), sem("mx_ready"), sem("nm_ready"), sem("p_ready")
    pT_done, pT_ready, att_done = sem("pT_done"), sem("pT_ready"), sem("att_done")
    se_ready, l_step, att_step, ma_ready = sem("se_ready"), sem("l_step"), sem("att_step"), sem("ma_ready")
    mT_done, mh_done, ml_done = sem("mT_done"), sem("mh_done"), sem("ml_done")
    wo_done, h_in, h_ready = sem("wo_done"), sem("h_in"), sem("h_ready")
    sq1, ms1, sd1, rs1, xr_ready, x2_out = sem("sq1"), sem("ms1"), sem("sd1"), sem("rs1"), sem("xr_ready"), sems("x2_out", 2)
    b_in, b_step = sem("b_in"), sem("b_step")
    rT_done, rT_ready, wr_in, lg_done, r_step, rexp_ready = sem("rT_done"), sem("rT_ready"), sem("wr_in"), sem("lg_done"), sem("r_step"), sem("rexp_ready")
    mask_ready, pos_done, row_ready, fill_ready, fill_out, slot_out = sem("mask_ready"), sem("pos_done"), sem("row_ready"), sem("fill_ready"), sem("fill_out"), sem("slot_out")
    tab_in, over_ready, over_out = sem("tab_in"), sem("over_ready"), sem("over_out")
    u_hi, u_lo, u_lop, u_used = sem("u_hi"), sem("u_lo"), sem("u_lop"), sem("u_used")
    d_hi, d_lo, d_used = sem("d_hi"), sem("d_lo"), sem("d_used")
    sel_in = sems("sel_in", 2)
    ix_ready, xg_in, xg_zero = sem("ix_ready"), sem("xg_in"), sem("xg_zero")
    xT_done, xTh_ready, xTl_ready = sem("xT_done"), sem("xTh_ready"), sem("xTl_ready")
    g_ready, ucl_ready, sg_ready, t_ready, act_ready = sem("g_ready"), sem("ucl_ready"), sem("sg_ready"), sem("t_ready"), sem("act_ready")
    aT_done, aTh_ready, aTl_ready = sem("aT_done"), sem("aTh_ready"), sem("aTl_ready")
    y_ready, y_out, experts_done = sem("y_ready"), sem("y_out"), sem("experts_done")
    yk_in, acc_step, sq2, ms2, sd2, rs2, fin_ready, out_done = sems("yk_in", 2), sem("acc_step"), sem("sq2"), sem("ms2"), sem("sd2"), sem("rs2"), sem("fin_ready"), sems("out_done", 2)
    nsink_ready, pay_ready, ixs_ready = sem("nsink_ready"), sem("pay_ready"), sem("ixs_ready")
    fg_in, ng_in = sem("fg_in"), sem("ng_in")

    PRE_B, PRE_G = 4, 6
    GROUPS = 8
    UNITS = [(n, a) for n in range(NT) for a in range(2)]

    def span(n):
        tiles = [t for t in (n - 1, n, n + 1) if 0 <= t < NT]
        return tiles, (tiles[0] - (n - 1)) * P

    block_cols = [C_AQ, C_FF, C_FB, C_Q, C_V, C_G, C_GA, C_GB]
    w_in_t = w_in.rearrange("(k p) n -> p k n", p=P)

    def at_head(fn, eng, first=True):
        fn(0, True, False)
        with eng.Fori(1, NH - 1) as h:
            fn(h, False, False)
        fn(NH - 1, False, True)

    POOL_P = (2, 5)
    VEC_P = tuple(p for p in range(8) if p not in POOL_P)

    def first(i):
        return isinstance(i, int) and i == 0

    def wait_u_split(eng, i, p):
        if p in POOL_P:
            eng.wait_ge(u_lop, len(POOL_P) * i + (POOL_P.index(p) + 1))
        else:
            eng.wait_ge(u_lo, len(VEC_P) * i + (VEC_P.index(p) + 1))

    def run_overflow(eng, item, needs_code=False):
        eng.wait_ge(over_ready, 1)
        if needs_code:
            eng.wait_ge(over_out, 16)
        n = eng.value_load(regs_in[0:1, 0:1], min_val=0, max_val=MAXOVER)
        with eng.If(n > 0):
            with eng.Fori(0, MAXOVER) as j:
                with eng.If(n > j):
                    if needs_code:
                        code = eng.value_load(over_list[bass.ds(j, 1), 0:1], min_val=0, max_val=NE * NB - 1)
                        item(j + NE, code)
                    else:
                        item(j + NE)

    hu = nc_psum[:, 0:4 * 512]
    ybank = nc_psum[:, 4 * 512:6 * 512]
    with nc.Block() as block:

        @block.sync
        def _(sp):
            for j in range(NT):
                sp.dma_start(xt[:, j, :], x[0, j * P:(j + 1) * P, :]).then_inc(x_in[j], 16)
            sp.dma_start(cst[:, :], consts).then_inc(cst_in, 16)
            for r, a in ((R_LF, hg_lb_fwd), (R_LB, hg_lb_bwd)):
                sp.dma_start(rows[r:r + 16, :], a.rearrange("a (k p) -> (a k) p", p=P)).then_inc(vec_in, 16)
            for r, a in ((R_NG, norm_mix_gain), (R_FG, norm_ffn_gain)):
                sp.dma_start(rows[r:r + 8, :], a.rearrange("a (k p) -> (a k) p", p=P)).then_inc(vec_in, 16)
            sp.dma_start(gainq[:, :], hg_norm_gain.to_broadcast([P, P])).then_inc(bc_in, 16)
            sp.dma_start(sinkb[:, :], attn_sink.to_broadcast([P, QH])).then_inc(bc_in, 16)

            def load_block(slot, col, free):
                src = w_in_t[:, :, bass.ds(col, P)] if not isinstance(col, int) else w_in_t[:, :, col:col + P]
                if free is not None:
                    sp.wait_ge(fraw_in[slot], 16)
                    sp.wait_ge(w_lo, free)
                sp.dma_start(fraw[:, slot, :, :], src).then_inc(fraw_in[slot], 16)

            for b, col in enumerate((C_AK, C_AK + P, C_AV, C_AV + P)):
                load_block(b, col, None)
            for b in range(8):
                load_block(b % 4, block_cols[b], PRE_B + b - 3)
            with sp.Fori(1, NH) as h:
                for b in range(8):
                    col = sp.snap(h * P + block_cols[b])
                    load_block(b % 4, col, sp.to_reg(8 * h + (PRE_B + b - 3)))

            sp.wait_ge(w_lo, PRE_B + 8 * NH)
            sp.wait_ge(proj_done, PRE_G + 8 * NH)
            d_src0 = w_out.rearrange("(q k p) n -> q p k n", p=P, k=2)

            def load_d(slot, src, free):
                if free is not None:
                    sp.wait_ge(d_lo, free)
                sp.dma_start(draw[:, slot, :, :], src).then_inc(draw_in[slot], 16)

            def load_u(p, src, i):
                if p >= 4:
                    wait_u_split(sp, i, p - 4)
                elif not first(i):
                    wait_u_split(sp, i - 1, p + 4)
                sp.dma_start(uraw[:, p % 4, :], src).then_inc(uraw_in[p % 4], 16)

            def up_src(e, p):
                return w_up_gate[0][bass.ds(e, 1), p * P:(p + 1) * P, :].rearrange("o p n -> (o p) n")

            def down_src(e, q):
                return w_down[0][bass.ds(e, 1), q * 2 * P:(q + 1) * 2 * P, :].rearrange("o (k p) n -> p (o k) n", p=P)

            load_d(0, d_src0[0], None)
            load_d(1, d_src0[1], None)
            for p in range(4):
                load_u(p, up_src(0, p), 0)
            sp.wait_ge(mg_ready, NH)
            for j in range(NT):
                sp.dma_start(hres[:, j, :], x[0, j * P:(j + 1) * P, :]).then_inc(h_in, 16)
            for r in range(3):
                sp.dma_start(braw[r * NE:(r + 1) * NE, 0:2 * FF], b_up_gate[0]).then_inc(b_in, 16)
                sp.dma_start(braw[r * NE:(r + 1) * NE, 2 * FF:], b_down[0]).then_inc(b_in, 16)
            sp.dma_start(fgain[:, :], final_norm_gain.rearrange("(a n) -> a n", a=1).to_broadcast([P, D])).then_inc(fg_in, 16)
            sp.dma_start(ngain[:, :], norm_ffn_gain.to_broadcast([P, D])).then_inc(ng_in, 16)
            load_d(0, d_src0[2], 1)
            load_d(1, d_src0[3], 2)
            for p in range(4, 6):
                load_u(p, up_src(0, p), 0)
            for j in range(NT):
                sp.wait_ge(xr_ready, j + 1)
                sp.dma_start(x2d[j * P:(j + 1) * P, :], xr[:, j % 2, :]).then_inc(x2_out[j % 2], 16)
            sp.wait_ge(rT_done, NT * 2)
            sp.dma_start(wr[:, :, :], w_router[0].rearrange("(k p) n -> p k n", p=P)).then_inc(wr_in, 16)
            sp.dma_start(brb[:, :], b_router.to_broadcast([P, NE])).then_inc(wr_in, 16)
            sp.wait_ge(fill_ready, 1)
            sp.dma_start(slots.rearrange("(p c) t -> p (c t)", p=P), fill[:, :]).then_inc(fill_out, 16)
            sp.wait_ge(slot_out, 16 * NT * TOPK)
            sp.dma_start(tab[:, :, :], slots.rearrange("(p c) t -> p c t", p=P)).then_inc(tab_in, 16)
            sp.wait_ge(over_ready, 1)
            sp.dma_start(over_list[:, :], ovi[:, 0:1]).then_inc(over_out, 16)

            def load_sel(s, e, used, n):
                row = selectors[bass.ds(e, 1), :, :].rearrange("o p n -> (o p) n")
                if n is not None:
                    sp.wait_ge(used, n)
                sp.dma_start(sel[:, s, :].bitcast(mybir.dt.uint16), row).then_inc(sel_in[s], 16)

            def load_down(i, e):
                load_sel(1, e, d_used, None if first(i) else 4 * i + 1)
                for q in range(4):
                    load_d(q % 2, down_src(e, q), 4 * i + (4 + q - 1))

            def load_up(i, e):
                load_sel(0, e, u_used, None if first(i) else 8 * i - 7)
                for p in range(8):
                    load_u(p, up_src(e, p), i)

            load_sel(0, 0, None, None)
            for p in range(6, 8):
                load_u(p, up_src(0, p), 0)
            with sp.Fori(1, NE) as e:
                load_up(e, e)
                load_down(e - 1, e - 1)
            load_down(NE - 1, NE - 1)

            def overflow(i, code):
                e = nc.s_assert_within(code >> 2, 0, NE - 1, skip_runtime_bounds_check_because="codes are below NE * NB")
                load_up(i, e)
                load_down(i, e)
            run_overflow(sp, overflow, needs_code=True)

            sp.wait_ge(experts_done, 1)
            for j in range(NT):
                if j >= 2:
                    sp.wait_ge(acc_step, 4 * (j - 1))
                for k in range(TOPK):
                    r = k * T + j * P
                    sp.dma_start(yk[:, j % 2, k, :], yd[r:r + P, :]).then_inc(yk_in[j % 2], 16)
            for j in range(NT):
                sp.wait_ge(fin_ready, j + 1)
                sp.dma_start(out[0, j * P:(j + 1) * P, :], fin[:, j % 2, :]).then_inc(out_done[j % 2], 16)
            sp.wait_ge(out_done[0], 32)
            sp.wait_ge(out_done[1], 32)
            for s_, n_ in ((x2_out[0], 32), (x2_out[1], 32), (over_out, 16)):
                sp.wait_ge(s_, n_)

        @block.tensor
        def _(pe):
            pe.wait_ge(cst_in, 16)
            pe.wait_ge(vec_in, 64)
            nc.tensor.transpose(bank[0][:, 0:R_END], rows[:, :], cst[0:R_END, K_ID:K_ID + R_END]).then_inc(vecT_done, 1)
            pe.wait_ge(vec_ready, 1)
            for k in range(KD):
                for j in range(NT):
                    if k == 0:
                        pe.wait_ge(xn0, j + 1)
                    last = nc.tensor.transpose(bank[k][:, j * P:(j + 1) * P], xt[:, j, k * P:(k + 1) * P], ident)
                last.then_inc(xt_done, 1)

            def project_cols(g, slot, split, ready, bank_sem, bank_n):
                pe.wait_ge(w_lo, ready)
                if bank_sem is not None:
                    pe.wait_ge(bank_sem, bank_n)
                for k in range(KD):
                    last = mm3(bank[g % 2], wsH[:, slot, k, :], wsL[:, slot, k, :], xnH[:, k, :], xnL[:, k, :],
                               k == 0, k == KD - 1)
                last.then_inc(proj_done, 1)

            def project_tokens(g, j, nblk, ready, bank_sem, bank_n):
                pe.wait_ge(w_lo, ready)
                pe.wait_ge(bank_sem, bank_n)
                ps = bank[g % 2][:, 0:nblk * P].rearrange("p (b n) -> p b n", b=nblk)
                tok = slice(j * P, (j + 1) * P)
                for k in range(KD):
                    last = mm3(ps, xnH[:, k, tok], xnL[:, k, tok], tsH[:, k, 0:nblk, :], tsL[:, k, 0:nblk, :],
                               k == 0, k == KD - 1)
                last.then_inc(proj_done, 1)

            pe.wait_ge(xl_done, KD)
            project_cols(0, 0, None, 1, None, None)
            project_cols(1, 1, None, 2, None, None)
            for j, (s_, n_) in enumerate(((kd_ready, 2), (kd_ready, 4), (av_ready, 1), (av_ready, 2))):
                project_tokens(2 + j, j, 2, 4, s_, n_)

            U4 = nc_psum[:, 4 * 512:6 * 512].rearrange("p (n v) -> p n v", n=NCH)
            U6 = nc_psum[:, 6 * 512:8 * 512].rearrange("p (n v) -> p n v", n=NCH)

            def updates(h):
                pe.wait_ge(vab_ready, 2 * h + 2)
                for d, (kt, U) in enumerate(((ktF, U4), (ktB, U6))):
                    pe.wait_ge(kt_ready, 2 * h + d + 1)
                    if d == 0:
                        pe.wait_ge(s_ready, 8 * h + 8)
                    else:
                        pe.wait_ge(att_step, 2 * h + 1)
                        if not first(h):
                            pe.wait_ge(og_ready, 4 * h)
                    for j in range(NT):
                        last = nc.tensor.matmul(U[:, 2 * j:2 * j + 2, :], kt[:, j, :], vab[:, j, :, :],
                                                start=True, stop=True)
                    last.then_inc(U_done, 1)

            def output(h):
                pe.wait_ge(st_ready, 14 * h + 14)
                pe.wait_ge(sc_ready, 2 * h + 2)
                for j in range(NT):
                    ps = bank[6][:, j * P:(j + 1) * P]
                    nc.tensor.matmul(ps, scF[:, j, :], vv[:, j, :], start=True, stop=False, skip_group_check=True)
                    nc.tensor.matmul(ps, scB[:, j, :], vv[:, j, :], start=False, stop=False, skip_group_check=True)
                    for c in range(2):
                        n = 2 * j + c
                        tok, half = slice(n * CH, (n + 1) * CH), bank[6][c * CH:(c + 1) * CH, j * P:(j + 1) * P]
                        for qd, S, has in ((qdF, SF, n > 0), (qdB, SB, n < NCH - 1)):
                            if has:
                                last = nc.tensor.matmul(half, qd[:, tok], S[:, n, :], start=False, stop=True,
                                                        skip_group_check=True)
                last.then_inc(o_done, 1)

            def scores(h, us):
                if us[0] == 0:
                    pe.wait_ge(aq_ready, h + 1)
                    pe.wait_ge(kcur_ready, h + 1)
                for u in us:
                    n, a = UNITS[u]
                    if u >= 2:
                        pe.wait_ge(s_ready, 8 * h + (u - 1))
                    elif not first(h):
                        pe.wait_ge(st_ready, 14 * (h - 1) + 1)
                    tiles, c0 = span(n)
                    half = slice(a * DH, (a + 1) * DH)
                    nc.tensor.matmul(bank[4 + a][:, 0:len(tiles) * P], aqT[half, n * P:(n + 1) * P],
                                     kcur[half, tiles[0] * P:(tiles[-1] + 1) * P], start=True, stop=True).then_inc(s_done, 1)

            def attend(h, us):
                for u in us:
                    n, a = UNITS[u]
                    tiles, _ = span(n)
                    pe.wait_ge(p_ready, 8 * h + u + 1)
                    if u >= 2:
                        pe.wait_ge(pT_ready, 8 * h + (u - 1))
                    elif not first(h):
                        pe.wait_ge(kt_ready, 2 * h)
                        pe.wait_ge(sc_ready, 2 * h)
                    for i in range(len(tiles)):
                        last = nc.tensor.transpose(bank[2 + a][:, i * P:(i + 1) * P], sbuf_p[:, a, i * P:(i + 1) * P], ident)
                    last.then_inc(pT_done, 1)
                for u in us:
                    n, a = UNITS[u]
                    tiles, _ = span(n)
                    pe.wait_ge(pT_ready, 8 * h + u + 1)
                    if u == 0:
                        pe.wait_ge(vcur_ready, h + 1)
                        if not first(h):
                            pe.wait_ge(st_ready, 14 * h)
                    for i, t in enumerate(tiles):
                        last = nc.tensor.matmul(bank[7][:, n * P + a * DH:n * P + (a + 1) * DH], pTs[:, a, i, :],
                                                vcur[:, t, :], start=i == 0, stop=i == len(tiles) - 1)
                    last.then_inc(att_done, 1)

            def keys_and_chunk_scores(h, d):
                ki, qd = ((kiF, qdF), (kiB, qdB))[d]
                pe.wait_ge(qk_ready, 4 * h + 2 * d + 2)
                if d == 0:
                    pe.wait_ge(pT_ready, 8 * h + 8)
                else:
                    pe.wait_ge(kt_ready, 2 * h + 1)
                for j in range(NT):
                    last = nc.tensor.transpose(bank[2][:, j * P:(j + 1) * P], ki[:, j * P:(j + 1) * P], ident)
                last.then_inc(kT_done, 1)
                if d == 1:
                    pe.wait_ge(sc_ready, 2 * h + 1)
                for j in range(NT):
                    tok = slice(j * P, (j + 1) * P)
                    last = nc.tensor.matmul(bank[3][:, tok], ki[:, tok], qd[:, tok], start=True, stop=True)
                last.then_inc(sc_done, 1)

            def head(h, is_first, is_last):
                pg, pb = 8 * h + PRE_G, 8 * h + PRE_B
                if is_first:
                    project_cols(0, 0, None, pb + 1, av_ready, 3)
                else:
                    project_cols(0, 0, None, pb + 1, ts_free, 4 * h - 1)
                    updates(h - 1)
                project_cols(1, 1, None, pb + 2, av_ready if is_first else ts_free, 4 if is_first else 4 * h)
                scores(h, (0, 1))
                project_cols(2, 0, None, pb + 3, aq_ready, h + 1)
                if not is_first:
                    output(h - 1)
                attend(h, (0, 1))
                scores(h, (2, 3))
                project_cols(3, 1, None, pb + 4, th_ready, 3 * h + 1)
                attend(h, (2, 3))
                scores(h, (4, 5))
                project_tokens(4, 0, 4, pb + 8, th_ready, 3 * h + 2)
                attend(h, (4, 5))
                scores(h, (6, 7))
                project_tokens(5, 1, 4, pb + 8, q_ready, h + 1)
                attend(h, (6, 7))
                project_tokens(6, 2, 4, pb + 8, ts_free, 4 * h + 1)
                keys_and_chunk_scores(h, 0)
                project_tokens(7, 3, 4, pb + 8, ts_free, 4 * h + 2)
                keys_and_chunk_scores(h, 1)

            at_head(head, pe)
            updates(NH - 1)
            output(NH - 1)

            for k in range(KD):
                b_ = k % 6
                if k >= 6:
                    pe.wait_ge(ml_done, k - 5)
                elif k == 0:
                    pe.wait_ge(mg_ready, NH)
                for j in range(NT):
                    last = nc.tensor.transpose(bank[b_][:, j * P:(j + 1) * P], merged[:, j, k * P:(k + 1) * P], ident)
                last.then_inc(mT_done, 1)
            pe.wait_ge(ml_done, KD)
            for q in range(4):
                pe.wait_ge(d_lo, q + 1)
                for kk in range(2):
                    k = 2 * q + kk
                    for j in range(NT):
                        for n in range(2):
                            last = mm3(bank[2 * j + n], mTH[:, k, j * P:(j + 1) * P], mTL[:, k, j * P:(j + 1) * P],
                                       dH[:, q % 2, kk, n * 512:(n + 1) * 512], dL[:, q % 2, kk, n * 512:(n + 1) * 512],
                                       k == 0, k == KD - 1)
                last.then_inc(d_used, 1)

            for j in range(NT):
                pe.wait_ge(xr_ready, j + 1)
                for half in range(2):
                    b_ = 2 * (j % 2) + half
                    if j >= 2:
                        pe.wait_ge(rT_ready, 2 * (j - 2) + half + 1)
                    else:
                        pe.wait_ge(h_ready, 8)
                    for k in range(4 * half, 4 * half + 4):
                        last = nc.tensor.transpose(bank[b_][:, (k % 4) * P:(k % 4 + 1) * P], xr[:, j % 2, k * P:(k + 1) * P], ident)
                    last.then_inc(rT_done, 1)
            pe.wait_ge(rT_ready, 2 * NT)
            pe.wait_ge(wr_in, 32)
            for j in range(NT):
                for k in range(KD):
                    last = nc.tensor.matmul(bank[4][:, j * NE:(j + 1) * NE], rT[:, k, j * P:(j + 1) * P], wr[:, k, :],
                                            start=k == 0, stop=k == KD - 1)
                last.then_inc(lg_done, 1)
            pe.wait_ge(mask_ready, NT)
            for j in range(NT + 1):
                tiles = list(range(min(j, NT)))
                ps = bank[5][:, j * NE:(j + 1) * NE]
                for n_, t in enumerate(tiles):
                    last = nc.tensor.matmul(ps, cst[:, K_ON:K_ON + P], msk[:, t, :], start=n_ == 0,
                                            stop=j == NT and n_ == NT - 1)
                if j < NT:
                    last = nc.tensor.matmul(ps, cst[:, K_LT:K_LT + P], msk[:, j, :], start=not tiles, stop=True)
            last.then_inc(pos_done, 1)

            def x_part(i):
                pe.wait_ge(xg_in, 16 * i + 16)
                if first(i):
                    pe.wait_ge(xg_zero, 1)
                for b_ in range(2):
                    for k in range(4 * b_, 4 * b_ + 4):
                        last = nc.tensor.transpose(bank[6 + b_][:, (k % 4) * P:(k % 4 + 1) * P], xg[:, k * P:(k + 1) * P], ident)
                    last.then_inc(xT_done, 1)

            def up_part(i):
                if not first(i):
                    pe.wait_ge(ucl_ready, i)
                pe.wait_ge(sel_in[0], 16 * i + 16)
                if first(i):
                    pe.wait_ge(b_step, BIAS_STEPS)
                for n in range(4):
                    nc.tensor.matmul(bank[n], sel[:, 0, :], bias[:, n * 512:(n + 1) * 512], start=True, stop=False)
                pe.wait_ge(xTl_ready, 2 * i + 2)
                for p in range(8):
                    wait_u_split(pe, i, p)
                    for n in range(4):
                        cols = slice(n * 512, (n + 1) * 512)
                        last = mm3(bank[n], xTH[:, p, :], xTL[:, p, :], uH[:, p % 2, cols], uL[:, p % 2, cols], False, p == 7)
                    last.then_inc(u_used, 1)

            def a_part(i, x_before):
                pe.wait_ge(act_ready, i + 1)
                pe.wait_ge(xTl_ready, x_before)
                for b_ in range(2):
                    for k in range(4 * b_, 4 * b_ + 4):
                        last = nc.tensor.transpose(bank[6 + b_][:, (k % 4) * P:(k % 4 + 1) * P], actv[:, k * P:(k + 1) * P], ident)
                    last.then_inc(aT_done, 1)

            def down_part(i):
                if not first(i):
                    pe.wait_ge(y_ready, i)
                pe.wait_ge(sel_in[1], 16 * i + 16)
                for n in range(2):
                    nc.tensor.matmul(bank[4 + n], sel[:, 1, :], bias[:, (4 + n) * 512:(5 + n) * 512], start=True, stop=False)
                pe.wait_ge(aTl_ready, 2 * i + 2)
                for q in range(4):
                    pe.wait_ge(d_lo, 4 * i + (4 + q + 1))
                    for kk in range(2):
                        k = 2 * q + kk
                        for n in range(2):
                            cols = slice(n * 512, (n + 1) * 512)
                            last = mm3(bank[4 + n], aTH[:, k, :], aTL[:, k, :], dH[:, q % 2, kk, cols], dL[:, q % 2, kk, cols],
                                       False, k == KD - 1)
                    last.then_inc(d_used, 1)

            x_part(0)
            up_part(0)
            x_part(1)
            a_part(0, 4)
            with pe.Fori(1, NE - 1) as i:
                up_part(i)
                pe.wait_ge(aTl_ready, 2 * i)
                x_part(i + 1)
                down_part(i - 1)
                a_part(i, 2 * i + 4)
            up_part(NE - 1)
            down_part(NE - 2)
            a_part(NE - 1, 2 * NE)
            down_part(NE - 1)

            def overflow(i):
                pe.wait_ge(aTl_ready, 2 * i)
                x_part(i)
                up_part(i)
                a_part(i, 2 * i + 2)
                down_part(i)
            run_overflow(pe, overflow)

        @block.scalar
        def _(act):
            A = nc.scalar.activation
            for j in range(NT):
                act.wait_ge(x_in[j], 16)
                if j:
                    act.wait_ge(sq0, j)
                A(junk[:, :], xt[:, j, :], ACT.Square, accum_out=stat[:, j:j + 1]).then_inc(sq0, 1)
            for j in range(NT):
                act.wait_ge(ms0, j + 1)
                A(stat[:, 8 + j:9 + j], stat[:, 4 + j:5 + j], ACT.Sqrt).then_inc(sd0, 1)
            act.wait_ge(lb_step, 2)
            A(lbs[:, 2:4, :], lbs[:, 0:2, :], ACT.Exp).then_inc(lb_exp, 1)
            for k in range(KD):
                act.wait_ge(xt_done, k + 1)
                A(xnH[:, k, :], bank[k], ACT.Copy, scale=gain_mix[k]).then_inc(xh_done, 1)

            def split_ws(b, slot, raw_slot, raw_n, used):
                act.wait_ge(fraw_in[raw_slot], raw_n)
                if used is not None:
                    act.wait_ge(proj_done, used)
                A(wsH[:, slot, :, :], fraw[:, raw_slot, :, :], ACT.Copy).then_inc(w_hi, 1)

            def split_ts(b, col, raw_slot, raw_n, used):
                act.wait_ge(fraw_in[raw_slot], raw_n)
                if used is not None:
                    act.wait_ge(proj_done, used)
                A(tsH[:, :, col, :], fraw[:, raw_slot, :, :], ACT.Copy).then_inc(w_hi, 1)

            split_ws(0, 0, 0, 16, None)
            split_ws(1, 1, 1, 16, None)
            split_ts(2, 0, 2, 16, None)
            split_ts(3, 1, 3, 16, None)

            def split(h, b):
                raw_n = 16 * 2 * h + 16 * (2 + b // 4)
                if b < 4:
                    split_ws(b, b % 2, b % 4, raw_n, 8 * h + (1, 2, 7, 8)[b])
                else:
                    split_ts(b, b - 4, b % 4, raw_n, 8 * h + 6)

            def exps(h, us):
                for u in us:
                    tiles, _ = span(UNITS[u][0])
                    w = len(tiles) * P
                    act.wait_ge(nm_ready, 8 * h + u + 1)
                    if u >= 2:
                        act.wait_ge(pT_done, 8 * h + (u - 1))
                    elif not first(h):
                        act.wait_ge(pT_done, 8 * h)
                    a = UNITS[u][1]
                    A(sbuf_p[:, a, 0:w], sbuf_s[:, a, 0:w], ACT.Exp, bias=att[:, 8 + u:9 + u], scale=SCALE,
                      accum_out=att[:, 16 + u:17 + u]).then_inc(p_ready, 1)

            def evac_pT(h, us):
                for u in us:
                    tiles, _ = span(UNITS[u][0])
                    a = UNITS[u][1]
                    act.wait_ge(pT_done, 8 * h + u + 1)
                    if u >= 2:
                        act.wait_ge(att_done, 8 * h + (u - 1))
                    elif not first(h):
                        act.wait_ge(att_done, 8 * h)
                    A(pTs[:, a, 0:len(tiles), :], bank[2 + a][:, 0:len(tiles) * P].rearrange("p (i s) -> p i s", s=P),
                      ACT.Copy).then_inc(pT_ready, 1)

            def token_gates(h, j):
                act.wait_ge(proj_done, 8 * h + (PRE_G + 4 + j + 1))
                if j == 0 and not first(h):
                    act.wait_ge(att_step, 2 * h)
                A(tht[:, j, :, :], bank[j % 2][:, P:4 * P].rearrange("p (b n) -> p b n", b=3), ACT.Tanh,
                  scale=0.5).then_inc(tht_ready, 1)

            def norm_square(h):
                act.wait_ge(o_done, h + 1)
                A(ogt[:, :, :], bank[6].rearrange("p (j v) -> p j v", j=NT), ACT.Square).then_inc(osq_ready, 1)

            def norm_sqrt(h):
                act.wait_ge(oms_step, 2 * h + 2)
                A(orow[:, 4:8], orow[:, 0:4], ACT.Sqrt).then_inc(osd_ready, 1)

            def exp_cum(h, d):
                cum, qd, ki = ((thF, qdF, kiF), (thB, qdB, kiB))[d]
                act.wait_ge(cum_ready, 2 * h + d + 1)
                A(qd[:, :], cum[:, :], ACT.Exp).then_inc(ec_ready, 1)
                A(ki[:, :], cum[:, :], ACT.Exp, scale=-1.0).then_inc(ec_ready, 1)

            def evac_kT(h, d):
                act.wait_ge(kT_done, 2 * h + d + 1)
                if d == 0 and not first(h):
                    act.wait_ge(U_done, 2 * h)
                A((ktF, ktB)[d][:, :, :], bank[2].rearrange("p (j s) -> p j s", j=NT), ACT.Copy).then_inc(kt_ready, 1)

            def head(h, is_first, is_last):
                pg = 8 * h + PRE_G
                if is_first:
                    split(h, 0)
                    split(h, 1)
                act.wait_ge(proj_done, pg + 1)
                if not is_first:
                    act.wait_ge(s_done, 8 * h)
                A(aqT[:, :], bank[0], ACT.Copy).then_inc(aq_ready, 1)
                split(h, 2)
                act.wait_ge(proj_done, pg + 2)
                if not is_first:
                    act.wait_ge(ec_ready, 4 * h)
                A(thF[:, :], bank[1], ACT.Tanh, scale=0.5).then_inc(th_ready, 1)
                split(h, 3)
                split(h, 4)
                split(h, 5)
                exps(h, (0, 1))
                act.wait_ge(proj_done, pg + 3)
                A(thB[:, :], bank[0], ACT.Tanh, scale=0.5).then_inc(th_ready, 1)
                split(h, 6)
                split(h, 7)
                if not is_first:
                    norm_square(h - 1)
                evac_pT(h, (0, 1))
                exps(h, (2, 3))
                if not is_first:
                    norm_sqrt(h - 1)
                act.wait_ge(proj_done, pg + 4)
                if not is_first:
                    act.wait_ge(qk_ready, 4 * h)
                A(qp[:, :], bank[1], ACT.Tanh, scale=0.5).then_inc(th_ready, 1)
                evac_pT(h, (2, 3))
                exps(h, (4, 5))
                act.wait_ge(f_ready, 2 * h + 2)
                act.wait_ge(k_ready, 2 * h + 2)
                A(fF[:, :], fF[:, :], ACT.Ln).then_inc(ln_ready, 1)
                A(fB[:, :], fB[:, :], ACT.Ln).then_inc(ln_ready, 1)
                token_gates(h, 0)
                if not is_last:
                    split(h + 1, 0)
                evac_pT(h, (4, 5))
                exps(h, (6, 7))
                if not is_first:
                    act.wait_ge(o_done, h)
                    act.wait_ge(dc_ready, 2 * h)
                exp_cum(h, 0)
                token_gates(h, 1)
                if not is_last:
                    split(h + 1, 1)
                evac_pT(h, (6, 7))
                exp_cum(h, 1)
                act.wait_ge(nm_ready, 8 * h + 8)
                act.wait_ge(l_step, 3 * h + 1)
                A(att[:, 32:40], att[:, 24:32], ACT.Exp).then_inc(se_ready, 1)
                token_gates(h, 2)
                evac_kT(h, 0)
                token_gates(h, 3)
                evac_kT(h, 1)

            at_head(head, act)
            norm_square(NH - 1)
            norm_sqrt(NH - 1)

            for k in range(KD):
                act.wait_ge(mT_done, k + 1)
                A(mTH[:, k, :], bank[k % 6], ACT.Copy).then_inc(mh_done, 1)
            act.wait_ge(mT_done, KD)
            for q in range(4):
                act.wait_ge(draw_in[q % 2], 16 * (q // 2) + 16)
                if q >= 2:
                    act.wait_ge(d_used, q - 1)
                A(dH[:, q % 2, :, :], draw[:, q % 2, :, :], ACT.Copy).then_inc(d_hi, 1)

            def split_u(i, p):
                act.wait_ge(uraw_in[p % 4], 32 * i + 16 * (p // 4 + 1))
                if not (first(i) and p < 2):
                    act.wait_ge(u_used, 8 * i + (p - 1))
                A(uH[:, p % 2, :], uraw[:, p % 4, :], ACT.Copy).then_inc(u_hi, 1)

            def split_d(i, q):
                act.wait_ge(draw_in[q % 2], 32 * i + 16 * (q // 2 + 3))
                act.wait_ge(d_used, 4 * i + (4 + q - 1))
                A(dH[:, q % 2, :, :], draw[:, q % 2, :, :], ACT.Copy).then_inc(d_hi, 1)

            split_u(0, 0)
            split_u(0, 1)
            for j in range(NT):
                act.wait_ge(h_ready, 2 * j + 2)
                if j >= 2:
                    act.wait_ge(x2_out[j % 2], 16)
                    act.wait_ge(rT_done, 2 * (j - 2) + 2)
                A(xr[:, j % 2, :], hres[:, j, :], ACT.Square, accum_out=stat[:, 16 + j:17 + j]).then_inc(sq1, 1)
                act.wait_ge(ms1, j + 1)
                A(stat[:, 24 + j:25 + j], stat[:, 20 + j:21 + j], ACT.Sqrt).then_inc(sd1, 1)
            for j in range(NT):
                for half in range(2):
                    n = 2 * j + half
                    act.wait_ge(rT_done, n + 1)
                    A(rT[:, 4 * half:4 * half + 4, j * P:(j + 1) * P],
                      bank[2 * (j % 2) + half].rearrange("p (k t) -> p k t", k=4), ACT.Copy).then_inc(rT_ready, 1)
            act.wait_ge(r_step, RS_MAX)
            for j in range(NT):
                A(gst[:, j, 0:4], v8[:, j, 0:4], ACT.Exp, bias=gst[:, j, 4:5], accum_out=gst[:, j, 5:6]).then_inc(rexp_ready, 1)

            def x_high(i):
                for b_ in range(2):
                    act.wait_ge(xT_done, 2 * i + b_ + 1)
                    if b_ == 0 and not first(i):
                        act.wait_ge(u_used, 8 * i)
                    A(xTH[:, 4 * b_:4 * b_ + 4, :], bank[6 + b_].rearrange("p (k s) -> p k s", k=4), ACT.Copy).then_inc(xTh_ready, 1)

            def a_high(i):
                for b_ in range(2):
                    act.wait_ge(aT_done, 2 * i + b_ + 1)
                    if b_ == 0 and not first(i):
                        act.wait_ge(d_used, 4 * i + 4)
                    A(aTH[:, 4 * b_:4 * b_ + 4, :], bank[6 + b_].rearrange("p (k s) -> p k s", k=4), ACT.Copy).then_inc(aTh_ready, 1)

            def sigmoid(i):
                act.wait_ge(g_ready, i + 1)
                if not first(i):
                    act.wait_ge(act_ready, i)
                A(sg[:, :], gcl[:, :], ACT.Sigmoid, scale=ALPHA).then_inc(sg_ready, 1)

            def y_evac(i):
                act.wait_ge(d_used, 4 * i + 8)
                if not first(i):
                    act.wait_ge(y_out, 16 * i)
                A(ysb[:, :], ybank, ACT.Copy).then_inc(y_ready, 1)

            x_high(0)
            for p in range(2, 8):
                split_u(0, p)
            x_high(1)
            sigmoid(0)
            split_u(1, 0)
            split_u(1, 1)
            a_high(0)

            def main(i, prefetch):
                for p in range(2, 8):
                    split_u(i, p)
                split_d(i - 1, 0)
                split_d(i - 1, 1)
                if prefetch:
                    x_high(i + 1)
                sigmoid(i)
                split_d(i - 1, 2)
                split_d(i - 1, 3)
                if prefetch:
                    split_u(i + 1, 0)
                    split_u(i + 1, 1)
                y_evac(i - 1)
                a_high(i)

            with act.Fori(1, NE - 1) as i:
                main(i, True)
            main(NE - 1, False)
            for q in range(4):
                split_d(NE - 1, q)
            y_evac(NE - 1)

            def overflow(i):
                x_high(i)
                for p in range(8):
                    split_u(i, p)
                sigmoid(i)
                a_high(i)
                for q in range(4):
                    split_d(i, q)
                y_evac(i)
            run_overflow(act, overflow)

            for j in range(NT):
                act.wait_ge(acc_step, 4 * j + 4)
                if j >= 2:
                    act.wait_ge(out_done[j % 2], 16)
                A(fin[:, j % 2, :], acc[:, j % 2, :], ACT.Square, accum_out=stat[:, 32 + j:33 + j]).then_inc(sq2, 1)
                act.wait_ge(ms2, j + 1)
                A(stat[:, 40 + j:41 + j], stat[:, 36 + j:37 + j], ACT.Sqrt).then_inc(sd2, 1)

        @block.vector
        def _(dve):
            V = nc.vector
            dve.wait_ge(vecT_done, 1)
            V.tensor_copy(vecs[:, :], bank[0][:, 0:R_END]).then_inc(vec_ready, 1)
            dve.wait_ge(vec_ready, 1)
            lbv = vecs[:, 0:32].rearrange("p (d l h) -> p d l h", d=2, l=2)
            mx = lbs[:, 4, :].rearrange("p (d h) -> p d h", d=2)
            V.tensor_tensor(mx, lbv[:, :, 0, :], lbv[:, :, 1, :], ALU.max).then_inc(vec_ready, 1)
            dve.wait_ge(vec_ready, 2)
            for l in range(2):
                V.tensor_tensor(lbs[:, l, :].rearrange("p (d h) -> p d h", d=2), lbv[:, :, l, :], mx, ALU.subtract).then_inc(lb_step, 1)
            for j in range(NT):
                dve.wait_ge(sq0, j + 1)
                V.tensor_scalar(stat[:, 4 + j:5 + j], stat[:, j:j + 1], 1.0 / D, EPS, ALU.mult, ALU.add).then_inc(ms0, 1)
            for j in range(NT):
                dve.wait_ge(sd0, j + 1)
                V.reciprocal(stat[:, 12 + j:13 + j], stat[:, 8 + j:9 + j]).then_inc(rs0, 1)
                dve.wait_ge(rs0, j + 1)
                V.tensor_scalar(xt[:, j, :], xt[:, j, :], stat[:, 12 + j:13 + j], None, ALU.mult).then_inc(xn0, 1)
            dve.wait_ge(lb_exp, 1)
            V.tensor_tensor(lbs[:, 5, :], lbs[:, 2, :], lbs[:, 3, :], ALU.add).then_inc(lb_step, 1)
            dve.wait_ge(lb_step, 3)
            V.reciprocal(lbs[:, 6, :], lbs[:, 5, :]).then_inc(lb_step, 1)
            dve.wait_ge(lb_step, 4)
            V.tensor_tensor(lbs[:, 7, :], lbs[:, 2, :], lbs[:, 6, :], ALU.mult).then_inc(lb_step, 1)
            dve.wait_ge(lb_step, 5)
            for t, (m, a) in ((fa, (-0.5, 0.5)), (fb_, (0.5, 0.5)), (fn, (0.25, -0.25)), (fk, (-0.25, 0.25))):
                V.tensor_scalar(t[:, :], lbs[:, 7, :], m, a, ALU.mult, ALU.add).then_inc(lb_step, 1)
            dve.wait_ge(bc_in, 32)
            V.tensor_scalar(gainq[:, :], gainq[:, :], 0.25, None, ALU.mult).then_inc(lb_step, 1)
            for k in range(KD):
                dve.wait_ge(xh_done, k + 1)
                V.scalar_tensor_tensor(out=xnL[:, k, :], in0=bank[k], scalar=gain_mix[k], in1=xnH[:, k, :].bitcast(F32),
                                       op0=ALU.mult, op1=ALU.subtract).then_inc(xl_done, 1)

            def low(n, out_, raw, high):
                dve.wait_ge(w_hi, n)
                V.tensor_tensor(out_, raw, high.bitcast(F32), ALU.subtract).then_inc(w_lo, 1)

            low(1, wsL[:, 0, :, :], fraw[:, 0, :, :], wsH[:, 0, :, :])
            low(2, wsL[:, 1, :, :], fraw[:, 1, :, :], wsH[:, 1, :, :])
            low(3, tsL[:, :, 0, :], fraw[:, 2, :, :], tsH[:, :, 0, :])
            low(4, tsL[:, :, 1, :], fraw[:, 3, :, :], tsH[:, :, 1, :])

            def split(h, b):
                n = 8 * h + (PRE_B + b + 1)
                if b < 4:
                    low(n, wsL[:, b % 2, :, :], fraw[:, b % 4, :, :], wsH[:, b % 2, :, :])
                else:
                    low(n, tsL[:, :, b - 4, :], fraw[:, b % 4, :, :], tsH[:, :, b - 4, :])

            split(0, 0)
            for kt_ in range(2):
                dve.wait_ge(proj_done, kt_ + 1)
                V.tensor_copy(kdup[0:DH, 2 * kt_, :], bank[kt_][0:DH, :]).then_inc(kd_ready, 1)
                V.tensor_copy(kdup[DH:P, 2 * kt_ + 1, :], bank[kt_][DH:P, :]).then_inc(kd_ready, 1)
            split(0, 1)
            for j in range(NT):
                dve.wait_ge(proj_done, 2 + j + 1)
                V.tensor_scalar(av[:, j, :], bank[j % 2][:, 0:KVH * DH], 0.5, None, ALU.mult).then_inc(av_ready, 1)

            def states(h, d):
                U, S, dc = ((nc_psum[:, 4 * 512:6 * 512], SF, dcF), (nc_psum[:, 6 * 512:8 * 512], SB, dcB))[d]
                U = U.rearrange("p (n v) -> p n v", n=NCH)
                n0 = 14 * h + 7 * d
                dve.wait_ge(U_done, 2 * h + d + 1)
                if not first(h):
                    dve.wait_ge(o_done, h)
                src, dst = ((0, 7), (1, 8)) if d == 0 else ((1, 8), (0, 7))
                V.tensor_tensor(S[:, dst[0]:dst[1], :], U[:, src[0]:src[1], :],
                                dc[:, src[0]:src[1]].unsqueeze(2).to_broadcast([P, 7, P]), ALU.mult).then_inc(st_ready, 1)
                for s in range(6):
                    n, b = (2 + s, 1 + s) if d == 0 else (5 - s, 6 - s)
                    dve.wait_ge(st_ready, n0 + (s + 1))
                    V.scalar_tensor_tensor(out=S[:, n, :], in0=S[:, b, :], scalar=dc[:, b:b + 1], in1=S[:, n, :],
                                           op0=ALU.mult, op1=ALU.add).then_inc(st_ready, 1)

            def softmax_front(h, us):
                for u in us:
                    n, a = UNITS[u]
                    tiles, c0 = span(n)
                    w = len(tiles) * P
                    dve.wait_ge(s_done, 8 * h + u + 1)
                    if u >= 2:
                        dve.wait_ge(p_ready, 8 * h + (u - 1))
                    elif not first(h):
                        dve.wait_ge(p_ready, 8 * h)
                    V.scalar_tensor_tensor(out=sbuf_s[:, a, 0:w], in0=cst[:, K_REL + c0:K_REL + c0 + w],
                                           scalar=cst[:, bass.ds(2 * h + (K_SL + a), 1)], in1=bank[4 + a][:, 0:w],
                                           op0=ALU.mult, op1=ALU.add).then_inc(s_ready, 1)
                for u in us:
                    n, a = UNITS[u]
                    w = len(span(n)[0]) * P
                    dve.wait_ge(s_ready, 8 * h + u + 1)
                    V.tensor_reduce(att[:, u:u + 1], sbuf_s[:, a, 0:w], AX.X, ALU.max).then_inc(mx_ready, 1)
                for u in us:
                    a = UNITS[u][1]
                    dve.wait_ge(mx_ready, 8 * h + u + 1)
                    if u == 0 and not first(h):
                        dve.wait_ge(l_step, 3 * h)
                    V.tensor_scalar(att[:, 8 + u:9 + u], att[:, u:u + 1], -SCALE, nsink[:, bass.ds(2 * h + a, 1)],
                                    ALU.mult, ALU.min).then_inc(nm_ready, 1)

            def gate(h, d):
                th, f, k = ((thF, fF, kF), (thB, fB, kB))[d]
                dve.wait_ge(th_ready, 3 * h + d + 1)
                if d == 0 and not first(h):
                    dve.wait_ge(qk_ready, 4 * h)
                col = bass.ds(h + 8 * d, 1)
                V.tensor_scalar(f[:, :], th[:, :], fa[:, col], fb_[:, col], ALU.mult, ALU.add).then_inc(f_ready, 1)
                V.tensor_scalar(k[:, :], th[:, :], fn[:, col], fk[:, col], ALU.mult, ALU.add).then_inc(k_ready, 1)

            def cumulate(h, d):
                th, f, keep = ((thF, fF, K_KF), (thB, fB, K_KB))[d]
                dve.wait_ge(ln_ready, 2 * h + d + 1)
                dve.wait_ge(f_ready, 2 * h + 2)
                dve.wait_ge(k_ready, 2 * h + 2)
                step = 1 if d == 0 else -1
                V.tensor_tensor_scan(th[:, ::step], cst[:, K_KF:K_KB] if d == 0 else cst[:, K_KB:K_REL][:, ::-1],
                                     f[:, ::step], 0.0, ALU.mult, ALU.add).then_inc(cum_ready, 1)

            def chunk_decay(h, d):
                qd, dc, c = ((qdF, dcF, CH - 1), (qdB, dcB, 0))[d]
                dve.wait_ge(ec_ready, 4 * h + 2 * d + 2)
                V.tensor_copy(dc[:, :], qd[:, :].rearrange("p (n c) -> p n c", c=CH)[:, :, c]).then_inc(dc_ready, 1)

            def token_tile(h, j):
                dve.wait_ge(tht_ready, 4 * h + j + 1)
                if j == 0 and not first(h):
                    dve.wait_ge(mg_ready, h)
                    dve.wait_ge(U_done, 2 * h)
                V.tensor_copy(vv[:, j, :], bank[j % 2][:, 0:P]).then_inc(v_ready, 1)
                V.scalar_tensor_tensor(out=G1[:, j, :], in0=tht[:, j, 0, :], scalar=1.0, in1=bank[j % 2][:, P:2 * P],
                                       op0=ALU.add, op1=ALU.mult).then_inc(ts_free, 1)
                dve.wait_ge(ts_free, 4 * h + j + 1)
                V.scalar_tensor_tensor(out=G1[:, j, :], in0=tht[:, j, 1, :], scalar=1.0, in1=G1[:, j, :],
                                       op0=ALU.add, op1=ALU.mult).then_inc(G1_step, 1)

            def mask_scores(h, d):
                sc, m = ((scF, K_TF), (scB, K_TB))[d]
                dve.wait_ge(zeroed, 3)
                dve.wait_ge(sc_done, 2 * h + d + 1)
                V.copy_predicated(sc[:, :, :], cst[:, m:m + P].bitcast(I32).unsqueeze(1).to_broadcast([P, NT, P]),
                                  bank[3].rearrange("p (j c) -> p j c", j=NT)).then_inc(sc_ready, 1)

            def norm_stats(h):
                dve.wait_ge(osq_ready, h + 1)
                V.tensor_reduce(orow[:, 8:12], ogt[:, :, :], AX.X, ALU.add).then_inc(oms_step, 1)
                dve.wait_ge(oms_step, 2 * h + 1)
                V.tensor_scalar(orow[:, 0:4], orow[:, 8:12], 1.0 / P, EPS, ALU.mult, ALU.add).then_inc(oms_step, 1)

            def gated_output(h):
                dve.wait_ge(osd_ready, h + 1)
                V.reciprocal(orow[:, 12:16], orow[:, 4:8]).then_inc(ors_ready, 1)
                dve.wait_ge(ors_ready, h + 1)
                dve.wait_ge(G1_ready, 4 * h + 4)
                for j in range(NT):
                    V.scalar_tensor_tensor(out=ogt[:, j, :], in0=bank[6][:, j * P:(j + 1) * P], scalar=orow[:, 12 + j:13 + j],
                                           in1=G1[:, j, :], op0=ALU.mult, op1=ALU.mult).then_inc(og_ready, 1)
                dve.wait_ge(og_ready, 4 * h + 4)
                dve.wait_ge(ma_ready, h + 1)
                m = merged[:, :, bass.ds(h * P, P)]
                V.tensor_tensor(m, m, ogt[:, :, :], ALU.add).then_inc(mg_ready, 1)

            def sink_sum(h, part):
                if part == 0:
                    dve.wait_ge(nm_ready, 8 * h + 8)
                    V.tensor_tensor(att[:, 24:32].rearrange("p (n a) -> p n a", a=2),
                                    att[:, 8:16].rearrange("p (n a) -> p n a", a=2),
                                    sinkb[:, bass.ds(2 * h, 2)].unsqueeze(1).to_broadcast([P, NT, 2]), ALU.add).then_inc(l_step, 1)
                else:
                    dve.wait_ge(se_ready, h + 1)
                    dve.wait_ge(p_ready, 8 * h + 8)
                    V.tensor_tensor(att[:, 40:48], att[:, 32:40], att[:, 16:24], ALU.add).then_inc(l_step, 1)
                    dve.wait_ge(l_step, 3 * h + 2)
                    V.reciprocal(att[:, 48:56], att[:, 40:48]).then_inc(l_step, 1)

            def gated_attention(h):
                dve.wait_ge(l_step, 3 * h + 3)
                dve.wait_ge(att_done, 8 * h + 8)
                V.tensor_tensor(attn1[:, :, :].rearrange("p j (a d) -> p (j a) d", a=2),
                                bank[7].rearrange("p (g d) -> p g d", d=DH),
                                att[:, 48:56].unsqueeze(2).to_broadcast([P, 8, DH]), ALU.mult).then_inc(att_step, 1)
                dve.wait_ge(att_step, 2 * h + 1)
                dve.wait_ge(tht_ready, 4 * h + 4)
                V.scalar_tensor_tensor(out=attn1[:, :, :], in0=tht[:, :, 2, :], scalar=1.0, in1=attn1[:, :, :],
                                       op0=ALU.add, op1=ALU.mult).then_inc(att_step, 1)
                dve.wait_ge(att_step, 2 * h + 2)
                V.tensor_copy(merged[:, :, bass.ds(h * P, P)], attn1[:, :, :]).then_inc(ma_ready, 1)

            def head(h, is_first, is_last):
                split(h, 2)
                if not is_first:
                    states(h - 1, 0)
                    states(h - 1, 1)
                split(h, 3)
                softmax_front(h, (0, 1))
                gate(h, 0)
                split(h, 4)
                split(h, 5)
                if not is_first:
                    norm_stats(h - 1)
                softmax_front(h, (2, 3))
                gate(h, 1)
                split(h, 6)
                split(h, 7)
                if not is_first:
                    gated_output(h - 1)
                dve.wait_ge(th_ready, 3 * h + 3)
                V.scalar_tensor_tensor(out=qp[:, :], in0=qp[:, :], scalar=1.0, in1=bank[1], op0=ALU.add,
                                       op1=ALU.mult).then_inc(q_ready, 1)
                softmax_front(h, (4, 5))
                cumulate(h, 0)
                cumulate(h, 1)
                token_tile(h, 0)
                if not is_last:
                    split(h + 1, 0)
                softmax_front(h, (6, 7))
                sink_sum(h, 0)
                chunk_decay(h, 0)
                token_tile(h, 1)
                if not is_last:
                    split(h + 1, 1)
                chunk_decay(h, 1)
                sink_sum(h, 1)
                token_tile(h, 2)
                mask_scores(h, 0)
                token_tile(h, 3)
                gated_attention(h)
                mask_scores(h, 1)

            dve.wait_ge(nsink_ready, 1)
            at_head(head, dve)
            states(NH - 1, 0)
            states(NH - 1, 1)
            norm_stats(NH - 1)
            gated_output(NH - 1)

            for k in range(KD):
                dve.wait_ge(mh_done, k + 1)
                V.tensor_tensor(mTL[:, k, :], bank[k % 6], mTH[:, k, :].bitcast(F32), ALU.subtract).then_inc(ml_done, 1)
            for q in range(4):
                dve.wait_ge(d_hi, q + 1)
                V.tensor_tensor(dL[:, q % 2, :, :], draw[:, q % 2, :, :], dH[:, q % 2, :, :].bitcast(F32), ALU.subtract).then_inc(d_lo, 1)

            def low_u(i, p):
                dve.wait_ge(u_hi, 8 * i + (p + 1))
                V.tensor_tensor(uL[:, p % 2, :], uraw[:, p % 4, :], uH[:, p % 2, :].bitcast(F32), ALU.subtract).then_inc(u_lo, 1)

            def low_d(i, q):
                dve.wait_ge(d_hi, 4 * i + (4 + q + 1))
                V.tensor_tensor(dL[:, q % 2, :, :], draw[:, q % 2, :, :], dH[:, q % 2, :, :].bitcast(F32), ALU.subtract).then_inc(d_lo, 1)

            low_u(0, 0)
            low_u(0, 1)
            dve.wait_ge(h_in, 16 * NT)
            dve.wait_ge(d_used, 4)
            for j in range(NT):
                for n in range(2):
                    hs = hres[:, j, n * 512:(n + 1) * 512]
                    V.tensor_tensor(hs, hs, bank[2 * j + n], ALU.add).then_inc(h_ready, 1)
            for j in range(NT):
                dve.wait_ge(sq1, j + 1)
                V.tensor_scalar(stat[:, 20 + j:21 + j], stat[:, 16 + j:17 + j], 1.0 / D, EPS, ALU.mult, ALU.add).then_inc(ms1, 1)
                dve.wait_ge(sd1, j + 1)
                V.reciprocal(stat[:, 28 + j:29 + j], stat[:, 24 + j:25 + j]).then_inc(rs1, 1)
                dve.wait_ge(rs1, j + 1)
                dve.wait_ge(ng_in, 16)
                if j >= 2:
                    dve.wait_ge(rT_done, 2 * (j - 2) + 2)
                V.scalar_tensor_tensor(out=xr[:, j % 2, :], in0=hres[:, j, :], scalar=stat[:, 28 + j:29 + j], in1=ngain[:, :],
                                       op0=ALU.mult, op1=ALU.mult).then_inc(xr_ready, 1)

            step = [0]

            def chain(ins):
                ins.then_inc(r_step, 1)
                step[0] += 1
                dve.wait_ge(r_step, step[0])

            dve.wait_ge(wr_in, 32)
            dve.wait_ge(lg_done, NT)
            chain(V.tensor_tensor(lg[:, :, :], bank[4][:, 0:NT * NE].rearrange("p (j e) -> p j e", j=NT),
                                  brb[:, :].unsqueeze(1).to_broadcast([P, NT, NE]), ALU.add))
            for j in range(NT):
                chain(V.max(v8[:, j, :], lg[:, j, :]))
            for j in range(NT):
                chain(V.max_index(i8[:, j, :], v8[:, j, :], lg[:, j, :]))
            chain(V.tensor_scalar(gst[:, :, 4], v8[:, :, 0], -1.0, None, ALU.mult))
            chain(V.tensor_copy(idf[:, :, :], i8[:, :, :]))
            assert step[0] == RS_MAX
            for j in range(NT):
                chain(V.tensor_tensor(oh[:, j, :, :], cst[:, K_IO:K_IO + NE].unsqueeze(1).to_broadcast([P, TOPK, NE]),
                                      idf[:, j, 0:TOPK].unsqueeze(2).to_broadcast([P, TOPK, NE]), ALU.is_equal))
            for j in range(NT):
                V.tensor_reduce(msk[:, j, :], oh[:, j, :, :].rearrange("p k e -> p e k"), AX.X, ALU.add).then_inc(mask_ready, 1)
            dve.wait_ge(pos_done, 1)
            chain(V.tensor_copy(ps_[:, :, :], bank[5][:, 0:NT * NE].rearrange("p (j e) -> p j e", j=NT)))
            chain(V.tensor_copy(msum[:, :], bank[5][:, NT * NE:(NT + 1) * NE]))
            for j in range(NT):
                chain(V.tensor_tensor(pk[:, j, :, :], oh[:, j, :, :], ps_[:, j, :].unsqueeze(1).to_broadcast([P, TOPK, NE]), ALU.mult))
            chain(V.tensor_reduce(posk[:, :], pk[:, :, :, :].rearrange("p j k e -> p (j k) e"), AX.X, ALU.add))
            for b in range(1, NB):
                chain(V.tensor_scalar(blk_[:, b - 1, :], posk[:, :], float(BLK * b), None, ALU.is_ge))
            chain(V.tensor_tensor(blk_[:, 0, :], blk_[:, 0, :], blk_[:, 1, :], ALU.add))
            chain(V.tensor_tensor(blk_[:, 0, :], blk_[:, 0, :], blk_[:, 2, :], ALU.add))
            chain(V.tensor_scalar(rowf[:, :], posk[:, :], float(NE * NB), None, ALU.mult))
            chain(V.scalar_tensor_tensor(out=rowf[:, :], in0=blk_[:, 0, :], scalar=float(1 - BLK * NE * NB), in1=rowf[:, :],
                                         op0=ALU.mult, op1=ALU.add))
            chain(V.scalar_tensor_tensor(out=rowf[:, :].rearrange("p (j k) -> p j k", j=NT), in0=idf[:, :, 0:TOPK], scalar=float(NB),
                                         in1=rowf[:, :].rearrange("p (j k) -> p j k", j=NT), op0=ALU.mult, op1=ALU.add))
            V.tensor_copy(rowi[:, :], rowf[:, :]).then_inc(row_ready, 1)
            for j in range(NT):
                dve.wait_ge(rexp_ready, j + 1)
            chain(V.reciprocal(gst[:, :, 6], gst[:, :, 5]))
            chain(V.tensor_tensor(gates[:, :, :], gst[:, :, 0:4], gst[:, :, 6:7].to_broadcast([P, NT, TOPK]), ALU.mult))
            for b in range(1, NB):
                chain(V.tensor_scalar(ovf[:, 0, :].rearrange("p (e b) -> p e b", b=NB - 1)[:, :, b - 1], msum[:, :],
                                      float(BLK * b), None, ALU.is_gt))
            chain(V.memset(ovf[:, 1, :], 1.0))
            chain(V.tensor_tensor_scan(ovf[:, 2, :], ovf[:, 1, :], ovf[:, 0, :], 0.0, ALU.mult, ALU.add))
            chain(V.tensor_copy(ovc[:, 0:1], ovf[:, 2, NE * (NB - 1) - 1:]))
            chain(V.scalar_tensor_tensor(out=ovf[:, 3, :], in0=ovf[:, 2, :], scalar=cst[:, K_P1:K_P1 + 1], in1=ovf[:, 0, :],
                                         op0=ALU.is_equal, op1=ALU.mult))
            chain(V.tensor_tensor(ovf[:, 1, :], ovf[:, 3, :], cst[:, K_CD:K_CD + NE * (NB - 1)], ALU.mult))
            chain(V.tensor_reduce(ovc[:, 1:2], ovf[:, 1, :], AX.X, ALU.add))
            chain(V.tensor_copy(ovi[:, 0:1], ovc[:, 1:2]))
            V.tensor_copy(regs_in[:, 0:1], ovc[:, 0:1]).then_inc(over_ready, 1)

            def x_low(i):
                for b_ in range(2):
                    dve.wait_ge(xTh_ready, 2 * i + b_ + 1)
                    V.tensor_tensor(xTL[:, 4 * b_:4 * b_ + 4, :], bank[6 + b_].rearrange("p (k s) -> p k s", k=4),
                                    xTH[:, 4 * b_:4 * b_ + 4, :].bitcast(F32), ALU.subtract).then_inc(xTl_ready, 1)

            def a_low(i):
                for b_ in range(2):
                    dve.wait_ge(aTh_ready, 2 * i + b_ + 1)
                    V.tensor_tensor(aTL[:, 4 * b_:4 * b_ + 4, :], bank[6 + b_].rearrange("p (k s) -> p k s", k=4),
                                    aTH[:, 4 * b_:4 * b_ + 4, :].bitcast(F32), ALU.subtract).then_inc(aTl_ready, 1)

            def clamp(i):
                dve.wait_ge(u_used, 8 * i + 8)
                if not first(i):
                    dve.wait_ge(act_ready, i)
                V.tensor_scalar(gcl[:, :], hu[:, 0:FF], LIMIT, None, ALU.min).then_inc(g_ready, 1)
                V.tensor_scalar(ucl[:, :], hu[:, FF:2 * FF], LIMIT, -LIMIT, ALU.min, ALU.max).then_inc(ucl_ready, 1)

            def swiglu(i):
                dve.wait_ge(g_ready, i + 1)
                dve.wait_ge(ucl_ready, i + 1)
                V.scalar_tensor_tensor(out=ucl[:, :], in0=ucl[:, :], scalar=1.0, in1=gcl[:, :], op0=ALU.add,
                                       op1=ALU.mult).then_inc(t_ready, 1)
                dve.wait_ge(t_ready, i + 1)
                dve.wait_ge(sg_ready, i + 1)
                if not first(i):
                    dve.wait_ge(aT_done, 2 * i)
                V.tensor_tensor(actv[:, :], ucl[:, :], sg[:, :], ALU.mult).then_inc(act_ready, 1)

            x_low(0)
            for p in VEC_P[2:]:
                low_u(0, p)
            clamp(0)
            x_low(1)
            swiglu(0)
            low_u(1, 0)
            low_u(1, 1)
            a_low(0)

            def main(i, prefetch):
                for p in VEC_P[2:]:
                    low_u(i, p)
                low_d(i - 1, 0)
                low_d(i - 1, 1)
                clamp(i)
                if prefetch:
                    x_low(i + 1)
                swiglu(i)
                low_d(i - 1, 2)
                low_d(i - 1, 3)
                if prefetch:
                    low_u(i + 1, 0)
                    low_u(i + 1, 1)
                a_low(i)

            with dve.Fori(1, NE - 1) as i:
                main(i, True)
            main(NE - 1, False)
            for q in range(4):
                low_d(NE - 1, q)

            def overflow(i):
                x_low(i)
                for p in VEC_P:
                    low_u(i, p)
                clamp(i)
                swiglu(i)
                a_low(i)
                for q in range(4):
                    low_d(i, q)
            run_overflow(dve, overflow)

            for j in range(NT):
                if j >= 2:
                    dve.wait_ge(fin_ready, j - 1)
                dve.wait_ge(yk_in[j % 2], 64 * (j // 2 + 1))
                for k in range(TOPK):
                    if k:
                        dve.wait_ge(acc_step, 4 * j + k)
                    V.scalar_tensor_tensor(out=acc[:, j % 2, :], in0=yk[:, j % 2, k, :], scalar=gates[:, j, k:k + 1],
                                           in1=acc[:, j % 2, :] if k else hres[:, j, :], op0=ALU.mult, op1=ALU.add).then_inc(acc_step, 1)
                dve.wait_ge(sq2, j + 1)
                V.tensor_scalar(stat[:, 36 + j:37 + j], stat[:, 32 + j:33 + j], 1.0 / D, EPS, ALU.mult, ALU.add).then_inc(ms2, 1)
                dve.wait_ge(sd2, j + 1)
                V.reciprocal(stat[:, 44 + j:45 + j], stat[:, 40 + j:41 + j]).then_inc(rs2, 1)
                dve.wait_ge(rs2, j + 1)
                dve.wait_ge(fg_in, 16)
                V.scalar_tensor_tensor(out=fin[:, j % 2, :], in0=acc[:, j % 2, :], scalar=stat[:, 44 + j:45 + j], in1=fgain[:, :],
                                       op0=ALU.mult, op1=ALU.mult).then_inc(fin_ready, 1)

        @block.gpsimd
        def _(gp):
            G = nc.gpsimd
            G.memset(scF[:, :, :], 0.0).then_inc(zeroed, 1)
            G.memset(scB[:, :, :], 0.0).then_inc(zeroed, 1)
            G.memset(vab[:, :, :, :], 0.0).then_inc(zeroed, 1)
            gp.wait_ge(bc_in, 32)
            G.tensor_scalar(nsink[:, :], sinkb[:, :], -1.0, None, ALU.mult).then_inc(nsink_ready, 1)
            for kv in range(KVH):
                src, dst = (slice(0, DH), slice(DH, P)) if kv % 2 == 0 else (slice(DH, P), slice(0, DH))
                gp.wait_ge(kd_ready, 2 * (kv // 2) + 2)
                gp.dma_start(kdup[dst, kv, :], kdup[src, kv, :]).then_inc(kdup_in, 16)
            gp.wait_ge(kdup_in, 16 * KVH)
            gp.wait_ge(av_ready, NT)

            def decayed(h, d):
                qd, ki, k = ((qdF, kiF, kF), (qdB, kiB, kB))[d]
                gp.wait_ge(ec_ready, 4 * h + 2 * d + 2)
                gp.wait_ge(dc_ready, 2 * h + d + 1)
                gp.wait_ge(q_ready, h + 1)
                gp.wait_ge(k_ready, 2 * h + 2)
                G.tensor_tensor(qd[:, :], qp[:, :], qd[:, :], ALU.mult).then_inc(qk_ready, 1)
                G.tensor_tensor(ki[:, :], k[:, :], ki[:, :], ALU.mult).then_inc(qk_ready, 1)

            def kv_of(h):
                kv = h // 2
                if not first(h):
                    gp.wait_ge(s_done, 8 * h)
                src = kdup[:, kv, :] if isinstance(h, int) else kdup[:, bass.ds(kv, 1), :].rearrange("p o t -> p (o t)")
                G.tensor_copy(kcur[:, :], src).then_inc(kcur_ready, 1)
                if not first(h):
                    gp.wait_ge(att_done, 8 * h)
                G.tensor_copy(vcur[:, :, :], av[:, :, bass.ds(kv * DH, DH)]).then_inc(vcur_ready, 1)

            def head(h, is_first, is_last):
                decayed(h, 0)
                decayed(h, 1)
                for j in range(NT):
                    gp.wait_ge(G1_step, 4 * h + j + 1)
                    G.tensor_tensor(G1[:, j, :], G1[:, j, :], gainq[:, :], ALU.mult).then_inc(G1_ready, 1)
                gp.wait_ge(zeroed, 3)
                gp.wait_ge(v_ready, 4 * h + 4)
                if not is_first:
                    gp.wait_ge(U_done, 2 * h)
                gp.wait_ge(G1_ready, 4 * h + 4)
                G.tensor_copy(vab[0:CH, :, 0, :], vv[0:CH, :, :]).then_inc(vab_ready, 1)
                gp.wait_ge(zeroed, 3)
                gp.wait_ge(vab_ready, 2 * h + 1)
                G.tensor_copy(vab[CH:P, :, 1, :], vv[CH:P, :, :]).then_inc(vab_ready, 1)
                if not is_last:
                    gp.wait_ge(vab_ready, 2 * h + 2)
                    kv_of(h + 1)

            gp.wait_ge(zeroed, 3)
            gp.wait_ge(lb_step, 10)
            kv_of(0)
            at_head(head, gp)

            gp.wait_ge(b_in, 16 * 6)
            step = [0]

            def chain(ins):
                ins.then_inc(b_step, 1)
                step[0] += 1
                gp.wait_ge(b_step, step[0])

            for part in range(3):
                own = slice(part * NE, (part + 1) * NE)
                chain(G.tensor_copy(bias[own, :], braw[own, :]))
                for later in range(part + 1, 3):
                    own2 = slice(later * NE, (later + 1) * NE)
                    chain(G.tensor_copy(bias[own2, :], braw[own2, :]))
                    chain(G.tensor_tensor(braw[own2, :], braw[own2, :], bias[own2, :], ALU.subtract))
            assert step[0] == BIAS_STEPS
            gp.wait_ge(rT_done, 2 * NT)
            G.memset(fill[:, :], NONE).then_inc(fill_ready, 1)
            for k in range(TOPK):
                pv = pay[:, :, :].rearrange("p (j k) c -> p j k c", k=TOPK)
                G.iota(pv[:, :, k, 0], pattern=[[P, NT]], base=0, channel_multiplier=1).then_inc(pay_ready, 1)
                G.iota(pv[:, :, k, 1], pattern=[[P, NT]], base=k * T, channel_multiplier=1).then_inc(pay_ready, 1)
            gp.wait_ge(pay_ready, 2 * TOPK)
            gp.wait_ge(fill_out, 16)
            gp.wait_ge(row_ready, 1)
            for n in range(NT * TOPK):
                gp.indirect_dma_start(slots, bass.IndirectOffsetOnAxis(ap=rowi[:, n:n + 1], axis=0),
                                      pay[:, n, :], None).then_inc(slot_out, 16)
            gp.wait_ge(lg_done, NT)
            gp.wait_ge(rT_ready, 2 * NT)
            G.memset(xg[:, :], 0.0).then_inc(xg_zero, 1)
            gp.wait_ge(xg_zero, 1)
            gp.wait_ge(tab_in, 16)
            gp.wait_ge(x2_out[0], 32)
            gp.wait_ge(x2_out[1], 32)
            gp.wait_ge(over_ready, 1)

            last_token, last_assignment = gp.to_reg(T - 1), gp.to_reg(TOPK * T - 1)

            def gather(i, code):
                if not first(i):
                    gp.wait_ge(xT_done, 2 * i)
                src = tab[:, code, :] if isinstance(code, int) else tab[:, bass.ds(code, 1), :].rearrange("p o c -> p (o c)")
                G.tensor_copy(ixg[:, :], src).then_inc(ix_ready, 1)
                n = i + 1 if isinstance(i, int) else gp.to_reg(i + 1)
                gp.wait_ge(x2_out[0], 32)
                gp.wait_ge(ix_ready, n)
                gp.indirect_dma_start(xg[:, :], None, x2d, bass.IndirectOffsetOnAxis(ap=ixg[:, 0:1], axis=0),
                                      bounds_check=last_token, oob_is_err=False).then_inc(xg_in, 16)

            def scatter(i, code):
                src = tab[:, code, :] if isinstance(code, int) else tab[:, bass.ds(code, 1), :].rearrange("p o c -> p (o c)")
                gp.wait_ge(tab_in, 16)
                gp.wait_ge(y_ready, i + 1)
                G.tensor_copy(ixs[:, :], src).then_inc(ixs_ready, 1)
                gp.wait_ge(tab_in, 16)
                gp.wait_ge(ixs_ready, i + 1)
                gp.indirect_dma_start(yd, bass.IndirectOffsetOnAxis(ap=ixs[:, 1:2], axis=0), ysb[:, :], None,
                                      bounds_check=last_assignment, oob_is_err=False).then_inc(y_out, 16)
                gp.wait_ge(y_out, 16 * i + 16)

            def low_u(i, p):
                gp.wait_ge(u_hi, 8 * i + (p + 1))
                G.tensor_tensor(uL[:, p % 2, :], uraw[:, p % 4, :], uH[:, p % 2, :].bitcast(F32), ALU.subtract).then_inc(u_lop, 1)

            gather(0, 0)
            for p in POOL_P:
                low_u(0, p)
            gather(1, NB)

            def main(i, prefetch):
                for p in POOL_P:
                    low_u(i, p)
                if prefetch:
                    gather(i + 1, NB * (i + 1))
                scatter(i - 1, NB * (i - 1))

            with gp.Fori(1, NE - 1) as i:
                main(i, True)
            main(NE - 1, False)
            scatter(NE - 1, NB * (NE - 1))

            def overflow(i, code):
                code = gp.snap(code)
                gather(i, code)
                for p in POOL_P:
                    low_u(i, p)
                scatter(i, code)
            run_overflow(gp, overflow, needs_code=True)
            G.memset(done[:, :], 0.0).then_inc(experts_done, 1)


_INS = ['x', 'norm_mix_gain', 'w_in', 'hg_lb_fwd', 'hg_lb_bwd', 'hg_norm_gain', 'attn_sink', 'w_out',
        'norm_ffn_gain', 'w_router', 'b_router', 'w_up_gate', 'b_up_gate', 'w_down', 'b_down', 'final_norm_gain']


def kernel(**inputs):
    import concourse.bacc as bacc
    from concourse.bass_utils import run_bass_kernel_spmd

    nc = bacc.Bacc("TRN2", target_bir_lowering=False, num_devices=1)
    arrays = {n: np.ascontiguousarray(inputs[n]) for n in _INS}
    arrays["consts"] = constants()
    arrays["selectors"] = bias_selectors()
    args = [nc.dram_tensor(f"in_{n}", a.shape, mybir.dt.from_np(a.dtype), kind="ExternalInput").ap()
            for n, a in arrays.items()]
    out = nc.dram_tensor("out_0", (1, T, D), F32, kind="ExternalOutput").ap()
    build(nc, *args, out)
    r = run_bass_kernel_spmd(nc, [{f"in_{n}": a for n, a in arrays.items()}], core_ids=[0])
    return r.results[0]["out_0"]
```

```python
from contextlib import ExitStack

import numpy as np

import concourse.bass as bass
from concourse import mybir

F32, F32R, BF16 = mybir.dt.float32, mybir.dt.float32r, mybir.dt.bfloat16
I32, U32 = mybir.dt.int32, mybir.dt.uint32
ALU, ACT, AX = mybir.AluOpType, mybir.ActivationFunctionType, mybir.AxisListType

P = 128
T, D = 512, 1024
NT, KD = T // P, D // P
NH = 8
CH = 64
NCH = T // CH
QH, KVH, DH = 16, 4, 64
WIN = 128
NE, TOPK, FF = 32, 4, 1024
RS_MAX = 2 * NT + 2
RAW, SPLIT = 6, 4
BODY = 12
BIAS_STEPS = 5
BLK = 128
NB = T // BLK
MAXOVER = T * TOPK // BLK - 1
LIMIT, ALPHA = 7.0, 1.702
EPS = 1e-5
NONE = 1 << 20
SCALE = DH ** -0.5

C_Q, C_FF, C_FB, C_V, C_G = 0, D, 2 * D, 3 * D, 4 * D
C_AQ = 5 * D
C_AK = C_AQ + QH * DH
C_AV = C_AK + KVH * DH
C_GA = C_AV + KVH * DH
C_GB = C_GA + D

K_ID, K_TF, K_TB, K_KF, K_KB, K_REL, K_SL, K_IO, K_LT, K_ON, K_CD, K_P1, K_EPS, K_END = np.cumsum(
    [0, P, P, P, T, T, 3 * P, QH, NE, P, P, 3 * NE, 1, 1]).tolist()
R_LF, R_LB, R_NG, R_END = 0, 16, 32, 40


def constants():
    c = np.zeros((P, K_END), np.float32)
    i, s = np.arange(P), np.arange(P)[:, None]
    c[:, K_ID:K_TF] = np.eye(P)
    same = (i[None] // CH) == (s // CH)
    c[:, K_TF:K_TB] = same & (s <= i[None])
    c[:, K_TB:K_KF] = same & (s >= i[None])
    t = np.arange(T)
    c[:, K_KF:K_KB] = t % CH != 0
    c[:, K_KB:K_REL] = t % CH != CH - 1
    rel = np.abs(s + WIN - np.arange(3 * P)[None])
    c[:, K_REL:K_SL] = np.where(rel <= WIN, -rel, -1e30)
    c[:, K_SL:K_IO] = 2.0 ** (-8.0 * np.arange(1, QH + 1) / QH) / SCALE
    c[:, K_IO:K_LT] = np.arange(NE)
    c[:, K_LT:K_ON] = s < i[None]
    c[:, K_ON:K_CD] = 1.0
    c[:, K_CD:K_P1] = (np.arange(NE)[:, None] * NB + np.arange(1, NB)[None]).ravel()
    c[:, K_P1] = np.arange(P) + 1
    c[:, K_EPS] = EPS
    return c


def bias_selectors():
    one = 0x3F80
    sel = np.zeros((NE, 3 * NE, P), np.uint16)
    for part in range(3):
        sel[np.arange(NE), part * NE + np.arange(NE)] = one
    return sel


def build(nc, x, norm_mix_gain, w_in, hg_lb_fwd, hg_lb_bwd, hg_norm_gain, attn_sink, w_out,
          norm_ffn_gain, w_router, b_router, w_up_gate, b_up_gate, w_down, b_down,
          final_norm_gain, consts, selectors, out):
    w_in, w_out = w_in[0], w_out[0]
    slots = nc.dram_tensor("slots", [P * NE * NB, 2], I32, kind="Internal").ap()
    over_list = nc.dram_tensor("over_list", [P, 1], I32, kind="Internal").ap()
    x2d = nc.dram_tensor("x2d", [T, D], F32, kind="Internal").ap()
    yd = nc.dram_tensor("yd", [TOPK * T, D], F32, kind="Internal").ap()

    BASE = 16512
    at = [BASE]

    def sb(name, shape, dt=F32):
        size = int(np.prod(shape[1:])) * (2 if dt == BF16 else 4)
        t = nc.alloc_sbuf_tensor_at(name, shape, dt, offset=at[0])
        at[0] += -(-size // 32) * 32
        return t

    cst = sb("cst", [P, K_END])
    vecs = sb("vecs", [P, R_END])
    rows = sb("rows", [R_END, P])
    lbs = sb("lbs", [P, 8, 16])
    fa = sb("fa", [P, 16])
    fb_ = sb("fb_", [P, 16])
    fn = sb("fn", [P, 16])
    fk = sb("fk", [P, 16])
    stat = sb("stat", [P, 64])
    small_top = at[0]

    xnH = sb("xnH", [P, KD, T], F32R)
    xnL = sb("xnL", [P, KD, T], F32R)
    fraw = sb("fraw", [P, 4, KD, P])
    tsH = sb("tsH", [P, KD, 4, P], F32R)
    tsL = sb("tsL", [P, KD, 4, P], F32R)
    wsH = sb("wsH", [P, 2, KD, P], F32R)
    wsL = sb("wsL", [P, 2, KD, P], F32R)
    front_w_top = at[0]
    merged = sb("merged", [P, NT, D])
    front_work = at[0]
    thF = sb("thF", [P, T]); thB = sb("thB", [P, T])
    qp = sb("qp", [P, T])
    fF = sb("fF", [P, T]); fB = sb("fB", [P, T])
    kF = sb("kF", [P, T]); kB = sb("kB", [P, T])
    qdF = sb("qdF", [P, T]); qdB = sb("qdB", [P, T])
    kiF = sb("kiF", [P, T]); kiB = sb("kiB", [P, T])
    dcF = sb("dcF", [P, NCH]); dcB = sb("dcB", [P, NCH])
    ktF = sb("ktF", [P, NT, P]); ktB = sb("ktB", [P, NT, P])
    scF = sb("scF", [P, NT, P]); scB = sb("scB", [P, NT, P])
    SF = sb("SF", [P, NCH, P]); SB = sb("SB", [P, NCH, P])
    vv = sb("vv", [P, NT, P])
    vab = sb("vab", [P, NT, 2, P])
    tht = sb("tht", [P, NT, 3, P])
    G1 = sb("G1", [P, NT, P])
    aqT = sb("aqT", [P, T])
    kdup = sb("kdup", [P, KVH, T])
    kcur = sb("kcur", [P, T])
    av = sb("av", [P, NT, KVH * DH])
    vcur = sb("vcur", [P, NT, DH])
    sbuf_s = sb("sbuf_s", [P, 2, 3 * P])
    sbuf_p = sb("sbuf_p", [P, 2, 3 * P])
    pTs = sb("pTs", [P, 2, 3, P])
    gainq = sb("gainq", [P, P])
    sinkb = sb("sinkb", [P, QH])
    nsink = sb("nsink", [P, QH])
    att = sb("att", [P, 64])
    orow = sb("orow", [P, 16])
    ogt = sb("ogt", [P, NT, P])
    attn1 = sb("attn1", [P, NT, P])
    assert at[0] <= 229368, at[0]
    at[0] = front_work
    xt = sb("xt", [P, NT, D])
    junk = sb("junk", [P, D])

    at[0] = small_top
    wraw = sb("wraw", [P, RAW, 2 * FF])
    wH = sb("wH", [P, SPLIT, 2 * FF], F32R)
    wL = sb("wL", [P, SPLIT, 2 * FF], F32R)
    moe_w_top = at[0]
    at[0] = max(moe_w_top, front_w_top)
    at[0] = max(at[0], front_work)
    hres = sb("hres", [P, NT, D])
    bias = sb("bias", [3 * NE, 3 * D], BF16)
    tab = sb("tab", [P, NE * NB, 2], I32)
    sel = sb("sel", [3 * NE, 2, P], BF16)
    ixg = sb("ixg", [P, 2], I32)
    ixs = sb("ixs", [P, 2], I32)
    gates = sb("gates", [P, NT, TOPK])
    regs_in = sb("regs_in", [P, 4], I32)
    done = sb("done", [P, 1])
    fgain = sb("fgain", [P, D])
    moe_work = at[0]
    mTH = sb("mTH", [P, KD, T], F32R)
    mTL = sb("mTL", [P, KD, T], F32R)
    ngain = sb("ngain", [P, D])
    xr = sb("xr", [P, 2, D])
    mid_top = at[0]
    at[0] = moe_work
    rT = sb("rT", [P, KD, T])
    at[0] = mid_top
    wr = sb("wr", [P, KD, NE])
    brb = sb("brb", [P, NE])
    lg = sb("lg", [P, NT, NE])
    v8 = sb("v8", [P, NT, 8])
    i8 = sb("i8", [P, NT, 8], U32)
    idf = sb("idf", [P, NT, 8])
    oh = sb("oh", [P, NT, TOPK, NE])
    msk = sb("msk", [P, NT + 1, NE], BF16)
    tri = sb("tri", [P, 2, P], BF16)
    msum = sb("msum", [P, NE])
    pk = sb("pk", [P, NT, TOPK, NE])
    posk = sb("posk", [P, NT * TOPK])
    blk_ = sb("blk_", [P, 3, NT * TOPK])
    rowf = sb("rowf", [P, NT * TOPK])
    rowi = sb("rowi", [P, NT * TOPK], I32)
    pay = sb("pay", [P, NT * TOPK, 2], I32)
    fill = sb("fill", [P, NE * NB * 2], I32)
    gst = sb("gst", [P, NT, 8])
    ovf = sb("ovf", [P, 4, NE * (NB - 1)])
    ovc = sb("ovc", [P, 4])
    ovi = sb("ovi", [P, 2], I32)
    assert at[0] <= 229368, at[0]
    at[0] = moe_work
    xg = sb("xg", [P, D])
    xTH = sb("xTH", [P, KD, P], F32R)
    xTL = sb("xTL", [P, KD, P], F32R)
    gcl = sb("gcl", [P, FF]); ucl = sb("ucl", [P, FF]); sg = sb("sg", [P, FF]); actv = sb("actv", [P, FF])
    aTH = sb("aTH", [P, KD, P], F32R)
    aTL = sb("aTL", [P, KD, P], F32R)
    ysb = sb("ysb", [P, D])
    moe_top = at[0]
    at[0] = small_top + 4 * 2 * FF * 4
    braw = sb("braw", [3 * NE, 3 * D])
    assert at[0] <= small_top + RAW * 2 * FF * 4
    at[0] = small_top
    yk = sb("yk", [P, NT, TOPK, D])
    acc = sb("acc", [P, 2, D])
    fin = sb("fin", [P, 2, D])

    nc_psum = nc.alloc_psum_tensor("psum", [P, 8 * 512], F32)
    bank = [nc_psum[:, i * 512:(i + 1) * 512] for i in range(8)]

    def sem(name):
        return nc.alloc_semaphore(name)

    def sems(name, n):
        return [sem(f"{name}{i}") for i in range(n)]

    ident = cst[:, K_ID:K_TF]
    eps = cst[:, K_EPS:K_EPS + 1]
    gain_mix = [vecs[:, R_NG + k:R_NG + k + 1] for k in range(KD)]

    def mm3(ps, lh, ll, rh, rl, start, stop):
        nc.tensor.matmul(ps, lh, rh, start=start, stop=False)
        nc.tensor.matmul(ps, lh, rl, start=False, stop=False)
        return nc.tensor.matmul(ps, ll, rh, start=False, stop=stop)

    cst_in, vec_in, bc_in = sem("cst_in"), sem("vec_in"), sem("bc_in")
    x_in = sems("x_in", NT)
    fraw_in, wraw_in = sems("fraw_in", 4), sems("wraw_in", RAW)
    kdup_in = sem("kdup_in")
    sq0, sd0, rs0, xn0 = sem("sq0"), sem("sd0"), sem("rs0"), sem("xn0")
    xt_done, xh_done, xl_done = sem("xt_done"), sem("xh_done"), sem("xl_done")
    vecT_done, vec_ready, lb_step, lb_exp = sem("vecT_done"), sem("vec_ready"), sem("lb_step"), sem("lb_exp")
    zeroed = sem("zeroed")
    w_hi, w_lo, proj_done = sem("w_hi"), sem("w_lo"), sem("proj_done")
    kd_ready, av_ready = sem("kd_ready"), sem("av_ready")
    th_ready, f_ready, k_ready, ln_ready, cum_ready = sem("th_ready"), sem("f_ready"), sem("k_ready"), sem("ln_ready"), sem("cum_ready")
    q_ready, ec_ready, dc_ready, qk_ready = sem("q_ready"), sem("ec_ready"), sem("dc_ready"), sem("qk_ready")
    kT_done, kt_ready, sc_done, sc_ready = sem("kT_done"), sem("kt_ready"), sem("sc_done"), sem("sc_ready")
    U_done, st_ready, o_done = sem("U_done"), sem("st_ready"), sem("o_done")
    tht_ready, v_ready, ts_free, G1_step, G1_ready, vab_ready = sem("tht_ready"), sem("v_ready"), sem("ts_free"), sem("G1_step"), sem("G1_ready"), sem("vab_ready")
    osq_ready, oms_ready, osd_ready, ors_ready, og_ready, mg_ready = sem("osq_ready"), sem("oms_ready"), sem("osd_ready"), sem("ors_ready"), sem("og_ready"), sem("mg_ready")
    aq_ready, kcur_ready, vcur_ready = sem("aq_ready"), sem("kcur_ready"), sem("vcur_ready")
    s_done, s_ready, mx_ready, nm_ready, p_ready = sem("s_done"), sem("s_ready"), sem("mx_ready"), sem("nm_ready"), sem("p_ready")
    pT_done, pT_ready, att_done = sem("pT_done"), sem("pT_ready"), sem("att_done")
    se_ready, l_step, att_step, ma_ready = sem("se_ready"), sem("l_step"), sem("att_step"), sem("ma_ready")
    mT_done, mh_done, ml_done = sem("mT_done"), sem("mh_done"), sem("ml_done")
    wo_done, h_in, h_ready = sem("wo_done"), sem("h_in"), sem("h_ready")
    sq1, sd1, rs1, xr_ready, x2_out = sem("sq1"), sem("sd1"), sem("rs1"), sem("xr_ready"), sems("x2_out", 2)
    b_in, b_step = sem("b_in"), sem("b_step")
    mi_ready, rT_done, rT_ready, wr_in, lg_done, r_step, rexp_ready = sem("mi_ready"), sem("rT_done"), sem("rT_ready"), sem("wr_in"), sem("lg_done"), sem("r_step"), sem("rexp_ready")
    tri_ready, mask_ready, pos_done, row_ready, fill_ready, fill_out, slot_out = sem("tri_ready"), sem("mask_ready"), sem("pos_done"), sem("row_ready"), sem("fill_ready"), sem("fill_out"), sem("slot_out")
    tab_in, over_ready, over_out = sem("tab_in"), sem("over_ready"), sem("over_out")
    p_hi, p_lo, p_lop, p_used = sem("p_hi"), sem("p_lo"), sem("p_lop"), sem("p_used")
    sel_in = sems("sel_in", 2)
    ix_ready, xg_in, xg_zero = sem("ix_ready"), sem("xg_in"), sem("xg_zero")
    xT_done, xTh_ready, xTl_ready = sem("xT_done"), sem("xTh_ready"), sem("xTl_ready")
    g_ready, ucl_ready, sg_ready, t_ready, act_ready = sem("g_ready"), sem("ucl_ready"), sem("sg_ready"), sem("t_ready"), sem("act_ready")
    aT_done, aTh_ready, aTl_ready = sem("aT_done"), sem("aTh_ready"), sem("aTl_ready")
    y_ready, y_out, experts_done = sem("y_ready"), sem("y_out"), sem("experts_done")
    yk_in, acc_step, sq2, sd2, rs2, fin_ready, out_done = sems("yk_in", NT), sem("acc_step"), sem("sq2"), sem("sd2"), sem("rs2"), sem("fin_ready"), sems("out_done", 2)
    nsink_ready, pay_ready, ixs_ready = sem("nsink_ready"), sem("pay_ready"), sem("ixs_ready")
    fg_in, ng_in = sem("fg_in"), sem("ng_in")

    PRE_B, PRE_G = 4, 6
    GROUPS = 8
    UNITS = [(n, a) for n in range(NT) for a in range(2)]

    def span(n):
        tiles = [t for t in (n - 1, n, n + 1) if 0 <= t < NT]
        return tiles, (tiles[0] - (n - 1)) * P

    block_cols = [C_AQ, C_FF, C_FB, C_Q, C_V, C_G, C_GA, C_GB]
    w_in_t = w_in.rearrange("(k p) n -> p k n", p=P)

    def at_head(fn, eng, first=True):
        fn(0, True, False)
        with eng.Fori(1, NH - 1) as h:
            fn(h, False, False)
        fn(NH - 1, False, True)

    POOL_B = (1, 5, 9)
    VEC_B = tuple(b for b in range(BODY) if b not in POOL_B)

    def first(i):
        return isinstance(i, int) and i == 0

    def wait_split(eng, k, b):
        if b in POOL_B:
            eng.wait_ge(p_lop, len(POOL_B) * k + (POOL_B.index(b) + 1))
        else:
            eng.wait_ge(p_lo, len(VEC_B) * k + (VEC_B.index(b) + 1))

    def high(act, k, b):
        act.wait_ge(wraw_in[b % RAW], 16 * BODY // RAW * k + 16 * (b // RAW + 1))
        if not (first(k) and b < SPLIT):
            act.wait_ge(p_used, BODY * k + (b + 1 - SPLIT))
        nc.scalar.activation(wH[:, b % SPLIT, :], wraw[:, b % RAW, :], ACT.Copy).then_inc(p_hi, 1)

    def low_part(eng, engine, k, b, done):
        eng.wait_ge(p_hi, BODY * k + (b + 1))
        engine.tensor_tensor(wL[:, b % SPLIT, :], wraw[:, b % RAW, :], wH[:, b % SPLIT, :].bitcast(F32),
                             ALU.subtract).then_inc(done, 1)

    def up_at(i, over=False):
        return (i, 4) if over or first(i) else (i, 0)

    def down_at(i, over=False):
        return (i + 1, 0) if over or (isinstance(i, int) and i == NE - 1) else (i + 1, 8)

    def used(at_, n):
        return BODY * at_[0] + (at_[1] + n)

    def run_overflow(eng, item, needs_code=False):
        eng.wait_ge(over_ready, 1)
        if needs_code:
            eng.wait_ge(over_out, 16)
        n = eng.value_load(regs_in[0:1, 0:1], min_val=0, max_val=MAXOVER)
        with eng.If(n > 0):
            with eng.Fori(0, MAXOVER) as j:
                with eng.If(n > j):
                    if needs_code:
                        code = eng.value_load(over_list[bass.ds(j, 1), 0:1], min_val=0, max_val=NE * NB - 1)
                        item(j + NE, code)
                    else:
                        item(j + NE)

    hu = nc_psum[:, 0:4 * 512]
    ybank = nc_psum[:, 4 * 512:6 * 512]
    with nc.Block() as block:

        @block.sync
        def _(sp):
            for j in range(NT):
                sp.dma_start(xt[:, j, :], x[0, j * P:(j + 1) * P, :]).then_inc(x_in[j], 16)
            sp.dma_start(cst[:, :], consts).then_inc(cst_in, 16)
            for r, a in ((R_LF, hg_lb_fwd), (R_LB, hg_lb_bwd)):
                sp.dma_start(rows[r:r + 16, :], a.rearrange("a (k p) -> (a k) p", p=P)).then_inc(vec_in, 16)
            sp.dma_start(rows[R_NG:R_END, :], norm_mix_gain.rearrange("a (k p) -> (a k) p", p=P)).then_inc(vec_in, 16)
            sp.dma_start(gainq[:, :], hg_norm_gain.to_broadcast([P, P])).then_inc(bc_in, 16)
            sp.dma_start(sinkb[:, :], attn_sink.to_broadcast([P, QH])).then_inc(bc_in, 16)

            def load_block(slot, col, free):
                src = w_in_t[:, :, bass.ds(col, P)] if not isinstance(col, int) else w_in_t[:, :, col:col + P]
                if free is not None:
                    sp.wait_ge(fraw_in[slot], 16)
                    sp.wait_ge(w_lo, free)
                sp.dma_start(fraw[:, slot, :, :], src).then_inc(fraw_in[slot], 16)

            for b, col in enumerate((C_AK, C_AK + P, C_AV, C_AV + P)):
                load_block(b, col, None)
            for b in range(8):
                load_block(b % 4, block_cols[b], PRE_B + b - 3)
            with sp.Fori(1, NH) as h:
                for b in range(8):
                    col = sp.snap(h * P + block_cols[b])
                    load_block(b % 4, col, sp.to_reg(8 * h + (PRE_B + b - 3)))

            sp.wait_ge(w_lo, PRE_B + 8 * NH)
            sp.wait_ge(proj_done, PRE_G + 8 * NH)
            d_src0 = w_out.rearrange("(q k p) n -> q p k n", p=P, k=2)

            def load_piece(k, b, src):
                if b >= RAW:
                    wait_split(sp, k, b - RAW)
                elif not first(k):
                    wait_split(sp, k - 1, b + BODY - RAW)
                sp.dma_start(wraw[:, b % RAW, :] if len(src.shape) == 2 else
                             wraw[:, b % RAW, :].rearrange("p (k n) -> p k n", k=2), src).then_inc(wraw_in[b % RAW], 16)

            def up_src(e, p):
                return w_up_gate[0][bass.ds(e, 1), p * P:(p + 1) * P, :].rearrange("o p n -> (o p) n")

            def down_src(e, q):
                return w_down[0][bass.ds(e, 1), q * 2 * P:(q + 1) * 2 * P, :].rearrange("o (k p) n -> p (o k) n", p=P)

            for q in range(4):
                load_piece(0, q, d_src0[q])
            for r in range(3):
                sp.dma_start(braw[r * NE:(r + 1) * NE, 0:2 * FF], b_up_gate[0]).then_inc(b_in, 16)
                sp.dma_start(braw[r * NE:(r + 1) * NE, 2 * FF:], b_down[0]).then_inc(b_in, 16)
            sp.wait_ge(mg_ready, NH)
            for j in range(NT):
                sp.dma_start(hres[:, j, :], x[0, j * P:(j + 1) * P, :]).then_inc(h_in, 16)
            sp.dma_start(ngain[:, :], norm_ffn_gain.to_broadcast([P, D])).then_inc(ng_in, 16)
            sp.dma_start(wr[:, :, :], w_router[0].rearrange("(k p) n -> p k n", p=P)).then_inc(wr_in, 16)
            sp.dma_start(brb[:, :], b_router.to_broadcast([P, NE])).then_inc(wr_in, 16)
            sp.dma_start(fgain[:, :], final_norm_gain.rearrange("(a n) -> a n", a=1).to_broadcast([P, D])).then_inc(fg_in, 16)
            for p in range(2, 6):
                load_piece(0, 4 + p, up_src(0, p))
            for j in range(NT):
                sp.wait_ge(xr_ready, j + 1)
                sp.dma_start(x2d[j * P:(j + 1) * P, :], xr[:, j % 2, :]).then_inc(x2_out[j % 2], 16)
            sp.wait_ge(b_step, BIAS_STEPS)
            for p in range(2):
                load_piece(0, 4 + p, up_src(0, p))
            sp.wait_ge(fill_ready, 1)
            sp.dma_start(slots.rearrange("(p c) t -> p (c t)", p=P), fill[:, :]).then_inc(fill_out, 16)
            sp.wait_ge(slot_out, 16 * NT * TOPK)
            sp.dma_start(tab[:, :, :], slots.rearrange("(p c) t -> p c t", p=P)).then_inc(tab_in, 16)
            sp.wait_ge(over_ready, 1)
            sp.dma_start(over_list[:, :], ovi[:, 0:1]).then_inc(over_out, 16)

            def load_sel(s, e, used):
                row = selectors[bass.ds(e, 1), :, :].rearrange("o p n -> (o p) n")
                if used is not None:
                    sp.wait_ge(p_used, used)
                sp.dma_start(sel[:, s, :].bitcast(mybir.dt.uint16), row).then_inc(sel_in[s], 16)

            def load_body(e, is_first):
                load_sel(0, e, 5 if is_first else BODY * e - (BODY - 1))
                for p in range(8):
                    load_piece(e, p, up_src(e, p))
                load_sel(1, e - 1, None if is_first else BODY * e - 3)
                for q in range(4):
                    load_piece(e, 8 + q, down_src(e - 1, q))

            load_sel(0, 0, None)
            for p in range(6, 8):
                load_piece(0, 4 + p, up_src(0, p))
            load_body(1, True)
            with sp.Fori(2, NE) as e:
                load_body(e, False)
            load_sel(1, NE - 1, BODY * NE - 3)
            for q in range(4):
                load_piece(NE, q, down_src(NE - 1, q))

            def overflow(i, code):
                e = nc.s_assert_within(code >> 2, 0, NE - 1, skip_runtime_bounds_check_because="codes are below NE * NB")
                load_sel(0, e, BODY * i - 7)
                for p in range(8):
                    load_piece(i, 4 + p, up_src(e, p))
                load_sel(1, e, BODY * i + 1)
                for q in range(4):
                    load_piece(i + 1, q, down_src(e, q))
            run_overflow(sp, overflow, needs_code=True)

            sp.wait_ge(experts_done, 1)
            for j in range(NT):
                for k in range(TOPK):
                    r = k * T + j * P
                    sp.dma_start(yk[:, j, k, :], yd[r:r + P, :]).then_inc(yk_in[j], 16)
            for j in range(NT):
                sp.wait_ge(fin_ready, j + 1)
                sp.dma_start(out[0, j * P:(j + 1) * P, :], fin[:, j % 2, :]).then_inc(out_done[j % 2], 16)
            sp.wait_ge(out_done[0], 32)
            sp.wait_ge(out_done[1], 32)
            for s_, n_ in ((x2_out[0], 32), (x2_out[1], 32), (over_out, 16)):
                sp.wait_ge(s_, n_)

        @block.tensor
        def _(pe):
            pe.wait_ge(cst_in, 16)
            pe.wait_ge(vec_in, 48)
            nc.tensor.transpose(bank[0][:, 0:R_END], rows[:, :], cst[0:R_END, K_ID:K_ID + R_END]).then_inc(vecT_done, 1)
            pe.wait_ge(vec_ready, 1)
            for k in range(KD):
                for j in range(NT):
                    if k == 0:
                        pe.wait_ge(xn0, j + 1)
                    last = nc.tensor.transpose(bank[k][:, j * P:(j + 1) * P], xt[:, j, k * P:(k + 1) * P], ident)
                last.then_inc(xt_done, 1)

            def project_cols(g, slot, split, ready, bank_sem, bank_n):
                pe.wait_ge(w_lo, ready)
                if bank_sem is not None:
                    pe.wait_ge(bank_sem, bank_n)
                for k in range(KD):
                    last = mm3(bank[g % 2], wsH[:, slot, k, :], wsL[:, slot, k, :], xnH[:, k, :], xnL[:, k, :],
                               k == 0, k == KD - 1)
                last.then_inc(proj_done, 1)

            def project_tokens(g, j, nblk, ready, bank_sem, bank_n):
                pe.wait_ge(w_lo, ready)
                pe.wait_ge(bank_sem, bank_n)
                ps = bank[g % 2][:, 0:nblk * P].rearrange("p (b n) -> p b n", b=nblk)
                tok = slice(j * P, (j + 1) * P)
                for k in range(KD):
                    last = mm3(ps, xnH[:, k, tok], xnL[:, k, tok], tsH[:, k, 0:nblk, :], tsL[:, k, 0:nblk, :],
                               k == 0, k == KD - 1)
                last.then_inc(proj_done, 1)

            pe.wait_ge(xl_done, KD)
            project_cols(0, 0, None, 1, None, None)
            project_cols(1, 1, None, 2, None, None)
            for j, (s_, n_) in enumerate(((kd_ready, 2), (kd_ready, 4), (av_ready, 1), (av_ready, 2))):
                project_tokens(2 + j, j, 2, 4, s_, n_)

            U4 = nc_psum[:, 4 * 512:6 * 512].rearrange("p (n v) -> p n v", n=NCH)
            U6 = nc_psum[:, 6 * 512:8 * 512].rearrange("p (n v) -> p n v", n=NCH)

            def updates(h):
                pe.wait_ge(vab_ready, 2 * h + 2)
                for d, (kt, U) in enumerate(((ktF, U4), (ktB, U6))):
                    pe.wait_ge(kt_ready, 2 * h + d + 1)
                    if d == 0:
                        pe.wait_ge(s_ready, 8 * h + 8)
                    else:
                        pe.wait_ge(att_step, 2 * h + 1)
                        if not first(h):
                            pe.wait_ge(og_ready, 4 * h)
                    for j in range(NT):
                        last = nc.tensor.matmul(U[:, 2 * j:2 * j + 2, :], kt[:, j, :], vab[:, j, :, :],
                                                start=True, stop=True)
                    last.then_inc(U_done, 1)

            def output(h):
                pe.wait_ge(st_ready, 14 * h + 14)
                pe.wait_ge(sc_ready, 2 * h + 2)
                for j in range(NT):
                    ps = bank[6][:, j * P:(j + 1) * P]
                    nc.tensor.matmul(ps, scF[:, j, :], vv[:, j, :], start=True, stop=False, skip_group_check=True)
                    nc.tensor.matmul(ps, scB[:, j, :], vv[:, j, :], start=False, stop=False, skip_group_check=True)
                    for c in range(2):
                        n = 2 * j + c
                        tok, half = slice(n * CH, (n + 1) * CH), bank[6][c * CH:(c + 1) * CH, j * P:(j + 1) * P]
                        for qd, S, has in ((qdF, SF, n > 0), (qdB, SB, n < NCH - 1)):
                            if has:
                                last = nc.tensor.matmul(half, qd[:, tok], S[:, n, :], start=False, stop=True,
                                                        skip_group_check=True)
                last.then_inc(o_done, 1)

            def scores(h, us):
                if us[0] == 0:
                    pe.wait_ge(aq_ready, h + 1)
                    pe.wait_ge(kcur_ready, h + 1)
                for u in us:
                    n, a = UNITS[u]
                    if u >= 2:
                        pe.wait_ge(s_ready, 8 * h + (u - 1))
                    elif not first(h):
                        pe.wait_ge(st_ready, 14 * (h - 1) + 1)
                    tiles, c0 = span(n)
                    half = slice(a * DH, (a + 1) * DH)
                    nc.tensor.matmul(bank[4 + a][:, 0:len(tiles) * P], aqT[half, n * P:(n + 1) * P],
                                     kcur[half, tiles[0] * P:(tiles[-1] + 1) * P], start=True, stop=True).then_inc(s_done, 1)

            def turn(h, us):
                for u in us:
                    n, a = UNITS[u]
                    tiles, _ = span(n)
                    pe.wait_ge(p_ready, 8 * h + u + 1)
                    if u >= 2:
                        pe.wait_ge(pT_ready, 8 * h + (u - 1))
                    elif not first(h):
                        pe.wait_ge(kt_ready, 2 * h)
                        pe.wait_ge(sc_ready, 2 * h)
                    for i in range(len(tiles)):
                        last = nc.tensor.transpose(bank[2 + a][:, i * P:(i + 1) * P], sbuf_p[:, a, i * P:(i + 1) * P], ident)
                    last.then_inc(pT_done, 1)

            def attend(h, us):
                for u in us:
                    n, a = UNITS[u]
                    tiles, _ = span(n)
                    pe.wait_ge(pT_ready, 8 * h + u + 1)
                    if u == 0:
                        pe.wait_ge(vcur_ready, h + 1)
                        if not first(h):
                            pe.wait_ge(st_ready, 14 * h)
                    for i, t in enumerate(tiles):
                        last = nc.tensor.matmul(bank[7][:, n * P + a * DH:n * P + (a + 1) * DH], pTs[:, a, i, :],
                                                vcur[:, t, :], start=i == 0, stop=i == len(tiles) - 1)
                    last.then_inc(att_done, 1)

            def keys_and_chunk_scores(h, d):
                ki, qd = ((kiF, qdF), (kiB, qdB))[d]
                pe.wait_ge(qk_ready, 4 * h + 2 * d + 2)
                if d == 0:
                    pe.wait_ge(pT_ready, 8 * h + 8)
                else:
                    pe.wait_ge(kt_ready, 2 * h + 1)
                for j in range(NT):
                    last = nc.tensor.transpose(bank[2][:, j * P:(j + 1) * P], ki[:, j * P:(j + 1) * P], ident)
                last.then_inc(kT_done, 1)
                if d == 1:
                    pe.wait_ge(sc_ready, 2 * h + 1)
                for j in range(NT):
                    tok = slice(j * P, (j + 1) * P)
                    last = nc.tensor.matmul(bank[3][:, tok], ki[:, tok], qd[:, tok], start=True, stop=True)
                last.then_inc(sc_done, 1)

            def head(h, is_first, is_last):
                pg, pb = 8 * h + PRE_G, 8 * h + PRE_B
                if is_first:
                    project_cols(0, 0, None, pb + 1, av_ready, 3)
                else:
                    project_cols(0, 0, None, pb + 1, ts_free, 4 * h - 1)
                    updates(h - 1)
                project_cols(1, 1, None, pb + 2, av_ready if is_first else ts_free, 4 if is_first else 4 * h)
                scores(h, (0, 1))
                project_cols(2, 0, None, pb + 3, aq_ready, h + 1)
                if not is_first:
                    output(h - 1)
                turn(h, (0, 1))
                scores(h, (2, 3))
                project_cols(3, 1, None, pb + 4, th_ready, 3 * h + 1)
                attend(h, (0, 1))
                turn(h, (2, 3))
                scores(h, (4, 5))
                project_tokens(4, 0, 4, pb + 8, th_ready, 3 * h + 2)
                attend(h, (2, 3))
                turn(h, (4, 5))
                scores(h, (6, 7))
                project_tokens(5, 1, 4, pb + 8, q_ready, h + 1)
                attend(h, (4, 5))
                turn(h, (6, 7))
                project_tokens(6, 2, 4, pb + 8, ts_free, 4 * h + 1)
                attend(h, (6, 7))
                keys_and_chunk_scores(h, 0)
                project_tokens(7, 3, 4, pb + 8, ts_free, 4 * h + 2)
                keys_and_chunk_scores(h, 1)

            at_head(head, pe)
            updates(NH - 1)
            output(NH - 1)

            def half_piece(kk, n):
                return slice(kk * D + n * 512, kk * D + (n + 1) * 512)

            for k in range(KD):
                b_ = k % 6
                if k >= 6:
                    pe.wait_ge(ml_done, k - 5)
                elif k == 0:
                    pe.wait_ge(mg_ready, NH)
                for j in range(NT):
                    last = nc.tensor.transpose(bank[b_][:, j * P:(j + 1) * P], merged[:, j, k * P:(k + 1) * P], ident)
                last.then_inc(mT_done, 1)
            pe.wait_ge(ml_done, KD)
            def out_projection(j):
                for q in range(4):
                    if j == 0:
                        wait_split(pe, 0, q)
                    for kk in range(2):
                        k = 2 * q + kk
                        for n in range(2):
                            last = mm3(bank[2 * j + n], mTH[:, k, j * P:(j + 1) * P], mTL[:, k, j * P:(j + 1) * P],
                                       wH[:, q, half_piece(kk, n)], wL[:, q, half_piece(kk, n)], k == 0, k == KD - 1)
                    if j == NT - 1:
                        last.then_inc(p_used, 1)
                if j < NT - 1:
                    last.then_inc(wo_done, 1)

            def turn_rows(j):
                pe.wait_ge(xr_ready, j + 1)
                for half in range(2):
                    if j:
                        pe.wait_ge(rT_ready, 2 * (j - 1) + half + 1)
                    for k in range(4 * half, 4 * half + 4):
                        last = nc.tensor.transpose(bank[half][:, (k % 4) * P:(k % 4 + 1) * P], xr[:, j % 2, k * P:(k + 1) * P], ident)
                    last.then_inc(rT_done, 1)

            def logits(j):
                pe.wait_ge(rT_ready, 2 * j + 2)
                pe.wait_ge(wr_in, 32)
                pe.wait_ge(h_ready, 2 * (1 + j // 2) + 2)
                for k in range(KD):
                    last = nc.tensor.matmul(bank[2 + j][:, 0:NE], rT[:, k, j * P:(j + 1) * P], wr[:, k, :],
                                            start=k == 0, stop=k == KD - 1)
                last.then_inc(lg_done, 1)

            out_projection(0)
            out_projection(1)
            turn_rows(0)
            out_projection(2)
            logits(0)
            turn_rows(1)
            out_projection(3)
            logits(1)
            turn_rows(2)
            logits(2)
            turn_rows(3)
            logits(3)
            pe.wait_ge(mask_ready, 1)
            pe.wait_ge(tri_ready, 2)
            nc.tensor.matmul(bank[6][:, 0:(NT + 1) * NE], tri[:, 1, :], msk[:, NT:, :].to_broadcast([P, NT + 1, NE]),
                             start=True, stop=False)
            for t in range(NT):
                nc.tensor.matmul(bank[6][:, (t + 1) * NE:(NT + 1) * NE], tri[:, 1, :],
                                 msk[:, t:t + 1, :].to_broadcast([P, NT - t, NE]), start=False, stop=False,
                                 skip_group_check=True)
            last = nc.tensor.matmul(bank[6][:, 0:(NT + 1) * NE], tri[:, 0, :], msk[:, :, :], start=False, stop=True)
            last.then_inc(pos_done, 1)

            def x_part(i):
                pe.wait_ge(xg_in, 16 * i + 16)
                if first(i):
                    pe.wait_ge(xg_zero, 1)
                for b_ in range(2):
                    for k in range(4 * b_, 4 * b_ + 4):
                        last = nc.tensor.transpose(bank[6 + b_][:, (k % 4) * P:(k % 4 + 1) * P], xg[:, k * P:(k + 1) * P], ident)
                    last.then_inc(xT_done, 1)

            def up_part(i, over=False):
                k, b0 = up_at(i, over)
                if not first(i):
                    pe.wait_ge(ucl_ready, i)
                pe.wait_ge(sel_in[0], 16 * i + 16)
                if first(i):
                    pe.wait_ge(b_step, BIAS_STEPS)
                for n in range(4):
                    nc.tensor.matmul(bank[n], sel[:, 0, :], bias[:, n * 512:(n + 1) * 512], start=True, stop=False)
                pe.wait_ge(xTl_ready, 2 * i + 2)
                for p in range(8):
                    wait_split(pe, k, b0 + p)
                    slot = (b0 + p) % SPLIT
                    for n in range(4):
                        cols = slice(n * 512, (n + 1) * 512)
                        last = mm3(bank[n], xTH[:, p, :], xTL[:, p, :], wH[:, slot, cols], wL[:, slot, cols], False, p == 7)
                    last.then_inc(p_used, 1)

            def a_part(i, x_before):
                pe.wait_ge(act_ready, i + 1)
                pe.wait_ge(xTl_ready, x_before)
                for b_ in range(2):
                    for k in range(4 * b_, 4 * b_ + 4):
                        last = nc.tensor.transpose(bank[6 + b_][:, (k % 4) * P:(k % 4 + 1) * P], actv[:, k * P:(k + 1) * P], ident)
                    last.then_inc(aT_done, 1)

            def down_part(i, over=False):
                k, b0 = down_at(i, over)
                if not first(i):
                    pe.wait_ge(y_ready, i)
                pe.wait_ge(sel_in[1], 16 * i + 16)
                for n in range(2):
                    nc.tensor.matmul(bank[4 + n], sel[:, 1, :], bias[:, (4 + n) * 512:(5 + n) * 512], start=True, stop=False)
                pe.wait_ge(aTl_ready, 2 * i + 2)
                for q in range(4):
                    wait_split(pe, k, b0 + q)
                    slot = (b0 + q) % SPLIT
                    for kk in range(2):
                        for n in range(2):
                            last = mm3(bank[4 + n], aTH[:, 2 * q + kk, :], aTL[:, 2 * q + kk, :], wH[:, slot, half_piece(kk, n)],
                                       wL[:, slot, half_piece(kk, n)], False, 2 * q + kk == KD - 1)
                    last.then_inc(p_used, 1)

            x_part(0)
            up_part(0)
            x_part(1)
            a_part(0, 4)
            with pe.Fori(1, NE - 1) as i:
                up_part(i)
                pe.wait_ge(aTl_ready, 2 * i)
                x_part(i + 1)
                down_part(i - 1)
                a_part(i, 2 * i + 4)
            up_part(NE - 1)
            down_part(NE - 2)
            a_part(NE - 1, 2 * NE)
            down_part(NE - 1)

            def overflow(i):
                pe.wait_ge(aTl_ready, 2 * i)
                x_part(i)
                up_part(i, True)
                a_part(i, 2 * i + 2)
                down_part(i, True)
            run_overflow(pe, overflow)

        @block.scalar
        def _(act):
            A = nc.scalar.activation
            for j in range(NT):
                act.wait_ge(x_in[j], 16)
                if j:
                    act.wait_ge(sq0, j)
                A(junk[:, :], xt[:, j, :], ACT.Square, accum_out=stat[:, j:j + 1]).then_inc(sq0, 1)
            for j in range(NT):
                if j == 0:
                    act.wait_ge(cst_in, 16)
                act.wait_ge(sq0, j + 1)
                A(stat[:, 8 + j:9 + j], stat[:, j:j + 1], ACT.Sqrt, scale=1.0 / D, bias=eps).then_inc(sd0, 1)
            act.wait_ge(lb_step, 2)
            A(lbs[:, 2:4, :], lbs[:, 0:2, :], ACT.Exp).then_inc(lb_exp, 1)
            for k in range(KD):
                act.wait_ge(xt_done, k + 1)
                A(xnH[:, k, :], bank[k], ACT.Copy, scale=gain_mix[k]).then_inc(xh_done, 1)

            def split_ws(b, slot, raw_slot, raw_n, used):
                act.wait_ge(fraw_in[raw_slot], raw_n)
                if used is not None:
                    act.wait_ge(proj_done, used)
                A(wsH[:, slot, :, :], fraw[:, raw_slot, :, :], ACT.Copy).then_inc(w_hi, 1)

            def split_ts(b, col, raw_slot, raw_n, used):
                act.wait_ge(fraw_in[raw_slot], raw_n)
                if used is not None:
                    act.wait_ge(proj_done, used)
                A(tsH[:, :, col, :], fraw[:, raw_slot, :, :], ACT.Copy).then_inc(w_hi, 1)

            split_ws(0, 0, 0, 16, None)
            split_ws(1, 1, 1, 16, None)
            split_ts(2, 0, 2, 16, None)
            split_ts(3, 1, 3, 16, None)

            def split(h, b):
                raw_n = 16 * 2 * h + 16 * (2 + b // 4)
                if b < 4:
                    split_ws(b, b % 2, b % 4, raw_n, 8 * h + (1, 2, 7, 8)[b])
                else:
                    split_ts(b, b - 4, b % 4, raw_n, 8 * h + 6)

            def exps(h, us):
                for u in us:
                    tiles, _ = span(UNITS[u][0])
                    w = len(tiles) * P
                    act.wait_ge(nm_ready, 8 * h + u + 1)
                    if u >= 2:
                        act.wait_ge(pT_done, 8 * h + (u - 1))
                    elif not first(h):
                        act.wait_ge(pT_done, 8 * h)
                    a = UNITS[u][1]
                    A(sbuf_p[:, a, 0:w], sbuf_s[:, a, 0:w], ACT.Exp, bias=att[:, 8 + u:9 + u], scale=SCALE,
                      accum_out=att[:, 16 + u:17 + u]).then_inc(p_ready, 1)

            def evac_pT(h, us):
                for u in us:
                    tiles, _ = span(UNITS[u][0])
                    a = UNITS[u][1]
                    act.wait_ge(pT_done, 8 * h + u + 1)
                    if u >= 2:
                        act.wait_ge(att_done, 8 * h + (u - 1))
                    elif not first(h):
                        act.wait_ge(att_done, 8 * h)
                    A(pTs[:, a, 0:len(tiles), :], bank[2 + a][:, 0:len(tiles) * P].rearrange("p (i s) -> p i s", s=P),
                      ACT.Copy).then_inc(pT_ready, 1)

            def token_gates(h, j):
                act.wait_ge(proj_done, 8 * h + (PRE_G + 4 + j + 1))
                if j == 0 and not first(h):
                    act.wait_ge(att_step, 2 * h)
                A(tht[:, j, :, :], bank[j % 2][:, P:4 * P].rearrange("p (b n) -> p b n", b=3), ACT.Tanh,
                  scale=0.5).then_inc(tht_ready, 1)

            def norm_square(h):
                act.wait_ge(o_done, h + 1)
                A(ogt[:, :, :], bank[6].rearrange("p (j v) -> p j v", j=NT), ACT.Square).then_inc(osq_ready, 1)

            def norm_sqrt(h):
                act.wait_ge(oms_ready, h + 1)
                A(orow[:, 4:8], orow[:, 8:12], ACT.Sqrt, scale=1.0 / P, bias=eps).then_inc(osd_ready, 1)

            def exp_cum(h, d):
                cum, qd, ki = ((thF, qdF, kiF), (thB, qdB, kiB))[d]
                act.wait_ge(cum_ready, 2 * h + d + 1)
                A(qd[:, :], cum[:, :], ACT.Exp).then_inc(ec_ready, 1)
                A(ki[:, :], cum[:, :], ACT.Exp, scale=-1.0).then_inc(ec_ready, 1)

            def evac_kT(h, d):
                act.wait_ge(kT_done, 2 * h + d + 1)
                if d == 0 and not first(h):
                    act.wait_ge(U_done, 2 * h)
                A((ktF, ktB)[d][:, :, :], bank[2].rearrange("p (j s) -> p j s", j=NT), ACT.Copy).then_inc(kt_ready, 1)

            def head(h, is_first, is_last):
                pg = 8 * h + PRE_G
                if is_first:
                    split(h, 0)
                    split(h, 1)
                act.wait_ge(proj_done, pg + 1)
                if not is_first:
                    act.wait_ge(s_done, 8 * h)
                A(aqT[:, :], bank[0], ACT.Copy).then_inc(aq_ready, 1)
                split(h, 2)
                act.wait_ge(proj_done, pg + 2)
                if not is_first:
                    act.wait_ge(ec_ready, 4 * h)
                A(thF[:, :], bank[1], ACT.Tanh, scale=0.5).then_inc(th_ready, 1)
                split(h, 3)
                split(h, 4)
                split(h, 5)
                exps(h, (0, 1))
                act.wait_ge(proj_done, pg + 3)
                A(thB[:, :], bank[0], ACT.Tanh, scale=0.5).then_inc(th_ready, 1)
                split(h, 6)
                split(h, 7)
                if not is_first:
                    norm_square(h - 1)
                evac_pT(h, (0, 1))
                exps(h, (2, 3))
                if not is_first:
                    norm_sqrt(h - 1)
                act.wait_ge(proj_done, pg + 4)
                if not is_first:
                    act.wait_ge(qk_ready, 4 * h)
                A(qp[:, :], bank[1], ACT.Tanh, scale=0.5).then_inc(th_ready, 1)
                evac_pT(h, (2, 3))
                exps(h, (4, 5))
                act.wait_ge(f_ready, 2 * h + 2)
                act.wait_ge(k_ready, 2 * h + 2)
                A(fF[:, :], fF[:, :], ACT.Ln).then_inc(ln_ready, 1)
                A(fB[:, :], fB[:, :], ACT.Ln).then_inc(ln_ready, 1)
                token_gates(h, 0)
                if not is_last:
                    split(h + 1, 0)
                evac_pT(h, (4, 5))
                exps(h, (6, 7))
                if not is_first:
                    act.wait_ge(o_done, h)
                    act.wait_ge(dc_ready, 2 * h)
                exp_cum(h, 0)
                token_gates(h, 1)
                if not is_last:
                    split(h + 1, 1)
                evac_pT(h, (6, 7))
                exp_cum(h, 1)
                act.wait_ge(nm_ready, 8 * h + 8)
                act.wait_ge(l_step, 3 * h + 1)
                A(att[:, 32:40], att[:, 24:32], ACT.Exp).then_inc(se_ready, 1)
                token_gates(h, 2)
                evac_kT(h, 0)
                token_gates(h, 3)
                evac_kT(h, 1)

            at_head(head, act)
            norm_square(NH - 1)
            norm_sqrt(NH - 1)

            for q in range(4):
                high(act, 0, q)
            for k in range(KD):
                act.wait_ge(mT_done, k + 1)
                A(mTH[:, k, :], bank[k % 6], ACT.Copy).then_inc(mh_done, 1)
            def second_norm(j):
                act.wait_ge(h_ready, 2 * j + 2)
                if j >= 2:
                    act.wait_ge(x2_out[j % 2], 16)
                    act.wait_ge(rT_done, 2 * (j - 2) + 2)
                A(xr[:, j % 2, :], hres[:, j, :], ACT.Square, accum_out=stat[:, 16 + j:17 + j]).then_inc(sq1, 1)
                act.wait_ge(sq1, j + 1)
                A(stat[:, 24 + j:25 + j], stat[:, 16 + j:17 + j], ACT.Sqrt, scale=1.0 / D, bias=eps).then_inc(sd1, 1)

            def rows_turned(j):
                for half in range(2):
                    act.wait_ge(rT_done, 2 * j + half + 1)
                    A(rT[:, 4 * half:4 * half + 4, j * P:(j + 1) * P],
                      bank[half].rearrange("p (k t) -> p k t", k=4), ACT.Copy).then_inc(rT_ready, 1)

            second_norm(0)
            second_norm(1)
            rows_turned(0)
            second_norm(2)
            rows_turned(1)
            second_norm(3)
            rows_turned(2)
            rows_turned(3)
            for b in (4, 5, 6):
                high(act, 0, b)
            act.wait_ge(r_step, RS_MAX)
            for j in range(NT):
                A(gst[:, j, 0:4], v8[:, j, 0:4], ACT.Exp, bias=gst[:, j, 4:5], accum_out=gst[:, j, 5:6]).then_inc(rexp_ready, 1)

            def x_high(i, last_up):
                for b_ in range(2):
                    act.wait_ge(xT_done, 2 * i + b_ + 1)
                    if b_ == 0 and last_up is not None:
                        act.wait_ge(p_used, last_up)
                    A(xTH[:, 4 * b_:4 * b_ + 4, :], bank[6 + b_].rearrange("p (k s) -> p k s", k=4), ACT.Copy).then_inc(xTh_ready, 1)

            def a_high(i, last_down):
                for b_ in range(2):
                    act.wait_ge(aT_done, 2 * i + b_ + 1)
                    if b_ == 0 and last_down is not None:
                        act.wait_ge(p_used, last_down)
                    A(aTH[:, 4 * b_:4 * b_ + 4, :], bank[6 + b_].rearrange("p (k s) -> p k s", k=4), ACT.Copy).then_inc(aTh_ready, 1)

            def sigmoid(i):
                act.wait_ge(g_ready, i + 1)
                if not first(i):
                    act.wait_ge(act_ready, i)
                A(sg[:, :], gcl[:, :], ACT.Sigmoid, scale=ALPHA).then_inc(sg_ready, 1)

            def y_evac(i, over=False):
                act.wait_ge(p_used, used(down_at(i, over), 4))
                if not first(i):
                    act.wait_ge(y_out, 16 * i)
                A(ysb[:, :], ybank, ACT.Copy).then_inc(y_ready, 1)

            high(act, 0, 7)
            x_high(0, None)
            for p in range(4, 8):
                high(act, 0, 4 + p)
            high(act, 1, 0)
            x_high(1, used(up_at(0), 8))
            sigmoid(0)
            high(act, 1, 1)
            high(act, 1, 2)
            a_high(0, None)

            def body(i, prefetch):
                for b in range(3, 11):
                    high(act, i, b)
                high(act, i, 11)
                if prefetch:
                    x_high(i + 1, used((i, 0), 8))
                sigmoid(i)
                for b in range(3 if prefetch else 1):
                    high(act, i + 1, b)
                y_evac(i - 1)
                a_high(i, used((i, 8), 4))

            with act.Fori(1, NE - 1) as i:
                body(i, True)
            body(NE - 1, False)
            for q in range(1, 4):
                high(act, NE, q)
            y_evac(NE - 1)

            def overflow(i):
                x_high(i, used((i, 0), 0))
                for p in range(8):
                    high(act, i, 4 + p)
                sigmoid(i)
                a_high(i, used((i, 0), 4))
                for q in range(4):
                    high(act, i + 1, q)
                y_evac(i, True)
            run_overflow(act, overflow)

            for j in range(NT):
                act.wait_ge(acc_step, 4 * j + 4)
                if j >= 2:
                    act.wait_ge(out_done[j % 2], 16)
                A(fin[:, j % 2, :], acc[:, j % 2, :], ACT.Square, accum_out=stat[:, 32 + j:33 + j]).then_inc(sq2, 1)
                act.wait_ge(sq2, j + 1)
                A(stat[:, 40 + j:41 + j], stat[:, 32 + j:33 + j], ACT.Sqrt, scale=1.0 / D, bias=eps).then_inc(sd2, 1)

        @block.vector
        def _(dve):
            V = nc.vector
            dve.wait_ge(vecT_done, 1)
            V.tensor_copy(vecs[:, :], bank[0][:, 0:R_END]).then_inc(vec_ready, 1)
            dve.wait_ge(vec_ready, 1)
            lbv = vecs[:, 0:32].rearrange("p (d l h) -> p d l h", d=2, l=2)
            mx = lbs[:, 4, :].rearrange("p (d h) -> p d h", d=2)
            V.tensor_tensor(mx, lbv[:, :, 0, :], lbv[:, :, 1, :], ALU.max).then_inc(vec_ready, 1)
            dve.wait_ge(vec_ready, 2)
            for l in range(2):
                V.tensor_tensor(lbs[:, l, :].rearrange("p (d h) -> p d h", d=2), lbv[:, :, l, :], mx, ALU.subtract).then_inc(lb_step, 1)
            for j in range(NT):
                dve.wait_ge(sd0, j + 1)
                V.reciprocal(stat[:, 12 + j:13 + j], stat[:, 8 + j:9 + j]).then_inc(rs0, 1)
                dve.wait_ge(rs0, j + 1)
                V.tensor_scalar(xt[:, j, :], xt[:, j, :], stat[:, 12 + j:13 + j], None, ALU.mult).then_inc(xn0, 1)
            dve.wait_ge(lb_exp, 1)
            V.tensor_tensor(lbs[:, 5, :], lbs[:, 2, :], lbs[:, 3, :], ALU.add).then_inc(lb_step, 1)
            dve.wait_ge(lb_step, 3)
            V.reciprocal(lbs[:, 6, :], lbs[:, 5, :]).then_inc(lb_step, 1)
            dve.wait_ge(lb_step, 4)
            V.tensor_tensor(lbs[:, 7, :], lbs[:, 2, :], lbs[:, 6, :], ALU.mult).then_inc(lb_step, 1)
            dve.wait_ge(lb_step, 5)
            for t, (m, a) in ((fa, (-0.5, 0.5)), (fb_, (0.5, 0.5)), (fn, (0.25, -0.25)), (fk, (-0.25, 0.25))):
                V.tensor_scalar(t[:, :], lbs[:, 7, :], m, a, ALU.mult, ALU.add).then_inc(lb_step, 1)
            dve.wait_ge(bc_in, 32)
            V.tensor_scalar(gainq[:, :], gainq[:, :], 0.25, None, ALU.mult).then_inc(lb_step, 1)
            for k in range(KD):
                dve.wait_ge(xh_done, k + 1)
                V.scalar_tensor_tensor(out=xnL[:, k, :], in0=bank[k], scalar=gain_mix[k], in1=xnH[:, k, :].bitcast(F32),
                                       op0=ALU.mult, op1=ALU.subtract).then_inc(xl_done, 1)

            def low(n, out_, raw, high):
                dve.wait_ge(w_hi, n)
                V.tensor_tensor(out_, raw, high.bitcast(F32), ALU.subtract).then_inc(w_lo, 1)

            low(1, wsL[:, 0, :, :], fraw[:, 0, :, :], wsH[:, 0, :, :])
            low(2, wsL[:, 1, :, :], fraw[:, 1, :, :], wsH[:, 1, :, :])
            low(3, tsL[:, :, 0, :], fraw[:, 2, :, :], tsH[:, :, 0, :])
            low(4, tsL[:, :, 1, :], fraw[:, 3, :, :], tsH[:, :, 1, :])

            def split(h, b):
                n = 8 * h + (PRE_B + b + 1)
                if b < 4:
                    low(n, wsL[:, b % 2, :, :], fraw[:, b % 4, :, :], wsH[:, b % 2, :, :])
                else:
                    low(n, tsL[:, :, b - 4, :], fraw[:, b % 4, :, :], tsH[:, :, b - 4, :])

            split(0, 0)
            for kt_ in range(2):
                dve.wait_ge(proj_done, kt_ + 1)
                V.tensor_copy(kdup[0:DH, 2 * kt_, :], bank[kt_][0:DH, :]).then_inc(kd_ready, 1)
                V.tensor_copy(kdup[DH:P, 2 * kt_ + 1, :], bank[kt_][DH:P, :]).then_inc(kd_ready, 1)
            split(0, 1)
            for j in range(NT):
                dve.wait_ge(proj_done, 2 + j + 1)
                V.tensor_scalar(av[:, j, :], bank[j % 2][:, 0:KVH * DH], 0.5, None, ALU.mult).then_inc(av_ready, 1)

            def states(h, d):
                U, S, dc = ((nc_psum[:, 4 * 512:6 * 512], SF, dcF), (nc_psum[:, 6 * 512:8 * 512], SB, dcB))[d]
                U = U.rearrange("p (n v) -> p n v", n=NCH)
                n0 = 14 * h + 7 * d
                dve.wait_ge(U_done, 2 * h + d + 1)
                if not first(h):
                    dve.wait_ge(o_done, h)
                src, dst = ((0, 7), (1, 8)) if d == 0 else ((1, 8), (0, 7))
                V.tensor_tensor(S[:, dst[0]:dst[1], :], U[:, src[0]:src[1], :],
                                dc[:, src[0]:src[1]].unsqueeze(2).to_broadcast([P, 7, P]), ALU.mult).then_inc(st_ready, 1)
                for s in range(6):
                    n, b = (2 + s, 1 + s) if d == 0 else (5 - s, 6 - s)
                    dve.wait_ge(st_ready, n0 + (s + 1))
                    V.scalar_tensor_tensor(out=S[:, n, :], in0=S[:, b, :], scalar=dc[:, b:b + 1], in1=S[:, n, :],
                                           op0=ALU.mult, op1=ALU.add).then_inc(st_ready, 1)

            def softmax_front(h, us):
                for u in us:
                    n, a = UNITS[u]
                    tiles, c0 = span(n)
                    w = len(tiles) * P
                    dve.wait_ge(s_done, 8 * h + u + 1)
                    if u >= 2:
                        dve.wait_ge(p_ready, 8 * h + (u - 1))
                    elif not first(h):
                        dve.wait_ge(p_ready, 8 * h)
                    V.scalar_tensor_tensor(out=sbuf_s[:, a, 0:w], in0=cst[:, K_REL + c0:K_REL + c0 + w],
                                           scalar=cst[:, bass.ds(2 * h + (K_SL + a), 1)], in1=bank[4 + a][:, 0:w],
                                           op0=ALU.mult, op1=ALU.add).then_inc(s_ready, 1)
                for u in us:
                    n, a = UNITS[u]
                    w = len(span(n)[0]) * P
                    dve.wait_ge(s_ready, 8 * h + u + 1)
                    V.tensor_reduce(att[:, u:u + 1], sbuf_s[:, a, 0:w], AX.X, ALU.max).then_inc(mx_ready, 1)
                for u in us:
                    a = UNITS[u][1]
                    dve.wait_ge(mx_ready, 8 * h + u + 1)
                    if u == 0 and not first(h):
                        dve.wait_ge(l_step, 3 * h)
                    V.tensor_scalar(att[:, 8 + u:9 + u], att[:, u:u + 1], -SCALE, nsink[:, bass.ds(2 * h + a, 1)],
                                    ALU.mult, ALU.min).then_inc(nm_ready, 1)

            def gate(h, d):
                th, f, k = ((thF, fF, kF), (thB, fB, kB))[d]
                dve.wait_ge(th_ready, 3 * h + d + 1)
                if d == 0 and not first(h):
                    dve.wait_ge(qk_ready, 4 * h)
                col = bass.ds(h + 8 * d, 1)
                V.tensor_scalar(f[:, :], th[:, :], fa[:, col], fb_[:, col], ALU.mult, ALU.add).then_inc(f_ready, 1)
                V.tensor_scalar(k[:, :], th[:, :], fn[:, col], fk[:, col], ALU.mult, ALU.add).then_inc(k_ready, 1)

            def cumulate(h, d):
                th, f, keep = ((thF, fF, K_KF), (thB, fB, K_KB))[d]
                dve.wait_ge(ln_ready, 2 * h + d + 1)
                dve.wait_ge(f_ready, 2 * h + 2)
                dve.wait_ge(k_ready, 2 * h + 2)
                step = 1 if d == 0 else -1
                V.tensor_tensor_scan(th[:, ::step], cst[:, K_KF:K_KB] if d == 0 else cst[:, K_KB:K_REL][:, ::-1],
                                     f[:, ::step], 0.0, ALU.mult, ALU.add).then_inc(cum_ready, 1)

            def chunk_decay(h, d):
                qd, dc, c = ((qdF, dcF, CH - 1), (qdB, dcB, 0))[d]
                dve.wait_ge(ec_ready, 4 * h + 2 * d + 2)
                V.tensor_copy(dc[:, :], qd[:, :].rearrange("p (n c) -> p n c", c=CH)[:, :, c]).then_inc(dc_ready, 1)

            def token_tile(h, j):
                dve.wait_ge(tht_ready, 4 * h + j + 1)
                if j == 0 and not first(h):
                    dve.wait_ge(mg_ready, h)
                    dve.wait_ge(U_done, 2 * h)
                V.tensor_copy(vv[:, j, :], bank[j % 2][:, 0:P]).then_inc(v_ready, 1)
                V.scalar_tensor_tensor(out=G1[:, j, :], in0=tht[:, j, 0, :], scalar=1.0, in1=bank[j % 2][:, P:2 * P],
                                       op0=ALU.add, op1=ALU.mult).then_inc(ts_free, 1)
                dve.wait_ge(ts_free, 4 * h + j + 1)
                V.scalar_tensor_tensor(out=G1[:, j, :], in0=tht[:, j, 1, :], scalar=1.0, in1=G1[:, j, :],
                                       op0=ALU.add, op1=ALU.mult).then_inc(G1_step, 1)

            def mask_scores(h, d):
                sc, m = ((scF, K_TF), (scB, K_TB))[d]
                dve.wait_ge(zeroed, 3)
                dve.wait_ge(sc_done, 2 * h + d + 1)
                V.copy_predicated(sc[:, :, :], cst[:, m:m + P].bitcast(I32).unsqueeze(1).to_broadcast([P, NT, P]),
                                  bank[3].rearrange("p (j c) -> p j c", j=NT)).then_inc(sc_ready, 1)

            def norm_stats(h):
                dve.wait_ge(osq_ready, h + 1)
                V.tensor_reduce(orow[:, 8:12], ogt[:, :, :], AX.X, ALU.add).then_inc(oms_ready, 1)

            def gated_output(h):
                dve.wait_ge(osd_ready, h + 1)
                V.reciprocal(orow[:, 12:16], orow[:, 4:8]).then_inc(ors_ready, 1)
                dve.wait_ge(ors_ready, h + 1)
                dve.wait_ge(G1_ready, 4 * h + 4)
                for j in range(NT):
                    V.scalar_tensor_tensor(out=ogt[:, j, :], in0=bank[6][:, j * P:(j + 1) * P], scalar=orow[:, 12 + j:13 + j],
                                           in1=G1[:, j, :], op0=ALU.mult, op1=ALU.mult).then_inc(og_ready, 1)
                dve.wait_ge(og_ready, 4 * h + 4)
                dve.wait_ge(ma_ready, h + 1)
                m = merged[:, :, bass.ds(h * P, P)]
                V.tensor_tensor(m, m, ogt[:, :, :], ALU.add).then_inc(mg_ready, 1)

            def sink_sum(h, part):
                if part == 0:
                    dve.wait_ge(nm_ready, 8 * h + 8)
                    V.tensor_tensor(att[:, 24:32].rearrange("p (n a) -> p n a", a=2),
                                    att[:, 8:16].rearrange("p (n a) -> p n a", a=2),
                                    sinkb[:, bass.ds(2 * h, 2)].unsqueeze(1).to_broadcast([P, NT, 2]), ALU.add).then_inc(l_step, 1)
                else:
                    dve.wait_ge(se_ready, h + 1)
                    dve.wait_ge(p_ready, 8 * h + 8)
                    V.tensor_tensor(att[:, 40:48], att[:, 32:40], att[:, 16:24], ALU.add).then_inc(l_step, 1)
                    dve.wait_ge(l_step, 3 * h + 2)
                    V.reciprocal(att[:, 48:56], att[:, 40:48]).then_inc(l_step, 1)

            def gated_attention(h):
                dve.wait_ge(l_step, 3 * h + 3)
                dve.wait_ge(att_done, 8 * h + 8)
                V.tensor_tensor(attn1[:, :, :].rearrange("p j (a d) -> p (j a) d", a=2),
                                bank[7].rearrange("p (g d) -> p g d", d=DH),
                                att[:, 48:56].unsqueeze(2).to_broadcast([P, 8, DH]), ALU.mult).then_inc(att_step, 1)
                dve.wait_ge(att_step, 2 * h + 1)
                dve.wait_ge(tht_ready, 4 * h + 4)
                V.scalar_tensor_tensor(out=attn1[:, :, :], in0=tht[:, :, 2, :], scalar=1.0, in1=attn1[:, :, :],
                                       op0=ALU.add, op1=ALU.mult).then_inc(att_step, 1)
                dve.wait_ge(att_step, 2 * h + 2)
                V.tensor_copy(merged[:, :, bass.ds(h * P, P)], attn1[:, :, :]).then_inc(ma_ready, 1)

            def head(h, is_first, is_last):
                split(h, 2)
                if not is_first:
                    states(h - 1, 0)
                    states(h - 1, 1)
                split(h, 3)
                softmax_front(h, (0, 1))
                gate(h, 0)
                split(h, 4)
                split(h, 5)
                if not is_first:
                    norm_stats(h - 1)
                softmax_front(h, (2, 3))
                gate(h, 1)
                split(h, 6)
                split(h, 7)
                if not is_first:
                    gated_output(h - 1)
                dve.wait_ge(th_ready, 3 * h + 3)
                V.scalar_tensor_tensor(out=qp[:, :], in0=qp[:, :], scalar=1.0, in1=bank[1], op0=ALU.add,
                                       op1=ALU.mult).then_inc(q_ready, 1)
                softmax_front(h, (4, 5))
                cumulate(h, 0)
                cumulate(h, 1)
                token_tile(h, 0)
                if not is_last:
                    split(h + 1, 0)
                softmax_front(h, (6, 7))
                sink_sum(h, 0)
                chunk_decay(h, 0)
                token_tile(h, 1)
                if not is_last:
                    split(h + 1, 1)
                chunk_decay(h, 1)
                sink_sum(h, 1)
                token_tile(h, 2)
                mask_scores(h, 0)
                token_tile(h, 3)
                gated_attention(h)
                mask_scores(h, 1)

            dve.wait_ge(nsink_ready, 1)
            at_head(head, dve)
            states(NH - 1, 0)
            states(NH - 1, 1)
            norm_stats(NH - 1)
            gated_output(NH - 1)

            def low_piece(k, b):
                low_part(dve, V, k, b, p_lo)

            low_piece(0, 0)
            for k in range(KD):
                dve.wait_ge(mh_done, k + 1)
                V.tensor_tensor(mTL[:, k, :], bank[k % 6], mTH[:, k, :].bitcast(F32), ALU.subtract).then_inc(ml_done, 1)
            low_piece(0, 2)
            low_piece(0, 3)
            dve.wait_ge(h_in, 16 * NT)
            step = [0]

            def chain(ins):
                ins.then_inc(r_step, 1)
                step[0] += 1
                dve.wait_ge(r_step, step[0])

            def second_norm(j):
                if j < NT - 1:
                    dve.wait_ge(wo_done, j + 1)
                else:
                    dve.wait_ge(p_used, 4)
                for n in range(2):
                    hs = hres[:, j, n * 512:(n + 1) * 512]
                    V.tensor_tensor(hs, hs, bank[2 * j + n], ALU.add).then_inc(h_ready, 1)
                dve.wait_ge(sd1, j + 1)
                V.reciprocal(stat[:, 28 + j:29 + j], stat[:, 24 + j:25 + j]).then_inc(rs1, 1)
                dve.wait_ge(rs1, j + 1)
                dve.wait_ge(ng_in, 16)
                V.scalar_tensor_tensor(out=xr[:, j % 2, :], in0=hres[:, j, :], scalar=stat[:, 28 + j:29 + j], in1=ngain[:, :],
                                       op0=ALU.mult, op1=ALU.mult).then_inc(xr_ready, 1)

            def largest(j):
                dve.wait_ge(lg_done, j + 1)
                chain(V.tensor_tensor(lg[:, j, :], bank[2 + j][:, 0:NE], brb[:, :], ALU.add))
                chain(V.max(v8[:, j, :], lg[:, j, :]))
                V.max_index(i8[:, j, :], v8[:, j, :], lg[:, j, :]).then_inc(mi_ready, 1)

            dve.wait_ge(wr_in, 32)
            second_norm(0)
            second_norm(1)
            second_norm(2)
            largest(0)
            second_norm(3)
            for j in range(1, NT):
                largest(j)
            dve.wait_ge(mi_ready, NT)
            chain(V.tensor_copy(idf[:, :, :], i8[:, :, :]))
            chain(V.tensor_scalar(gst[:, :, 4], v8[:, :, 0], -1.0, None, ALU.mult))
            assert step[0] == RS_MAX
            chain(V.tensor_tensor(oh[:, :, :, :],
                                  cst[:, K_IO:K_IO + NE].unsqueeze(1).unsqueeze(1).to_broadcast([P, NT, TOPK, NE]),
                                  idf[:, :, 0:TOPK].unsqueeze(3).to_broadcast([P, NT, TOPK, NE]), ALU.is_equal))
            with nc.allow_low_precision(reason="a sum of zeros and at most one one"):
                V.tensor_reduce(msk[:, 0:NT, :], oh[:, :, :, :].rearrange("p j k e -> p j e k"), AX.X, ALU.add).then_inc(mask_ready, 1)
            dve.wait_ge(pos_done, 1)
            chain(V.tensor_tensor(pk[:, :, :, :], oh[:, :, :, :],
                                  bank[6][:, 0:NT * NE].rearrange("p (j e) -> p j e", j=NT).unsqueeze(2).to_broadcast([P, NT, TOPK, NE]),
                                  ALU.mult))
            chain(V.tensor_reduce(posk[:, :], pk[:, :, :, :].rearrange("p j k e -> p (j k) e"), AX.X, ALU.add))
            for b in range(1, NB):
                chain(V.tensor_scalar(blk_[:, b - 1, :], posk[:, :], float(BLK * b), None, ALU.is_ge))
            chain(V.tensor_tensor(blk_[:, 0, :], blk_[:, 0, :], blk_[:, 1, :], ALU.add))
            chain(V.tensor_tensor(blk_[:, 0, :], blk_[:, 0, :], blk_[:, 2, :], ALU.add))
            chain(V.tensor_scalar(rowf[:, :], posk[:, :], float(NE * NB), None, ALU.mult))
            chain(V.scalar_tensor_tensor(out=rowf[:, :], in0=blk_[:, 0, :], scalar=float(1 - BLK * NE * NB), in1=rowf[:, :],
                                         op0=ALU.mult, op1=ALU.add))
            chain(V.scalar_tensor_tensor(out=rowf[:, :].rearrange("p (j k) -> p j k", j=NT), in0=idf[:, :, 0:TOPK], scalar=float(NB),
                                         in1=rowf[:, :].rearrange("p (j k) -> p j k", j=NT), op0=ALU.mult, op1=ALU.add))
            V.tensor_copy(rowi[:, :], rowf[:, :]).then_inc(row_ready, 1)
            low_piece(0, 4)
            low_piece(0, 6)
            chain(V.tensor_copy(msum[:, :], bank[6][:, NT * NE:(NT + 1) * NE]))
            for j in range(NT):
                dve.wait_ge(rexp_ready, j + 1)
            chain(V.reciprocal(gst[:, :, 6], gst[:, :, 5]))
            chain(V.tensor_tensor(gates[:, :, :], gst[:, :, 0:4], gst[:, :, 6:7].to_broadcast([P, NT, TOPK]), ALU.mult))
            for b in range(1, NB):
                chain(V.tensor_scalar(ovf[:, 0, :].rearrange("p (e b) -> p e b", b=NB - 1)[:, :, b - 1], msum[:, :],
                                      float(BLK * b), None, ALU.is_gt))
            chain(V.memset(ovf[:, 1, :], 1.0))
            chain(V.tensor_tensor_scan(ovf[:, 2, :], ovf[:, 1, :], ovf[:, 0, :], 0.0, ALU.mult, ALU.add))
            chain(V.tensor_copy(ovc[:, 0:1], ovf[:, 2, NE * (NB - 1) - 1:]))
            chain(V.scalar_tensor_tensor(out=ovf[:, 3, :], in0=ovf[:, 2, :], scalar=cst[:, K_P1:K_P1 + 1], in1=ovf[:, 0, :],
                                         op0=ALU.is_equal, op1=ALU.mult))
            chain(V.tensor_tensor(ovf[:, 1, :], ovf[:, 3, :], cst[:, K_CD:K_CD + NE * (NB - 1)], ALU.mult))
            chain(V.tensor_reduce(ovc[:, 1:2], ovf[:, 1, :], AX.X, ALU.add))
            chain(V.tensor_copy(ovi[:, 0:1], ovc[:, 1:2]))
            V.tensor_copy(regs_in[:, 0:1], ovc[:, 0:1]).then_inc(over_ready, 1)

            def x_low(i):
                for b_ in range(2):
                    dve.wait_ge(xTh_ready, 2 * i + b_ + 1)
                    V.tensor_tensor(xTL[:, 4 * b_:4 * b_ + 4, :], bank[6 + b_].rearrange("p (k s) -> p k s", k=4),
                                    xTH[:, 4 * b_:4 * b_ + 4, :].bitcast(F32), ALU.subtract).then_inc(xTl_ready, 1)

            def a_low(i):
                for b_ in range(2):
                    dve.wait_ge(aTh_ready, 2 * i + b_ + 1)
                    V.tensor_tensor(aTL[:, 4 * b_:4 * b_ + 4, :], bank[6 + b_].rearrange("p (k s) -> p k s", k=4),
                                    aTH[:, 4 * b_:4 * b_ + 4, :].bitcast(F32), ALU.subtract).then_inc(aTl_ready, 1)

            def clamp(i, over=False):
                dve.wait_ge(p_used, used(up_at(i, over), 8))
                if not first(i):
                    dve.wait_ge(act_ready, i)
                V.tensor_scalar(gcl[:, :], hu[:, 0:FF], LIMIT, None, ALU.min).then_inc(g_ready, 1)
                V.tensor_scalar(ucl[:, :], hu[:, FF:2 * FF], LIMIT, -LIMIT, ALU.min, ALU.max).then_inc(ucl_ready, 1)

            def swiglu(i):
                dve.wait_ge(g_ready, i + 1)
                dve.wait_ge(ucl_ready, i + 1)
                V.scalar_tensor_tensor(out=ucl[:, :], in0=ucl[:, :], scalar=1.0, in1=gcl[:, :], op0=ALU.add,
                                       op1=ALU.mult).then_inc(t_ready, 1)
                dve.wait_ge(t_ready, i + 1)
                dve.wait_ge(sg_ready, i + 1)
                if not first(i):
                    dve.wait_ge(aT_done, 2 * i)
                V.tensor_tensor(actv[:, :], ucl[:, :], sg[:, :], ALU.mult).then_inc(act_ready, 1)

            low_piece(0, 7)
            x_low(0)
            for b in (8, 10, 11):
                low_piece(0, b)
            low_piece(1, 0)
            clamp(0)
            x_low(1)
            swiglu(0)
            low_piece(1, 2)
            a_low(0)

            def body(i, prefetch):
                for b in (3, 4, 6, 7, 8, 10):
                    low_piece(i, b)
                clamp(i)
                low_piece(i, 11)
                if prefetch:
                    x_low(i + 1)
                swiglu(i)
                low_piece(i + 1, 0)
                if prefetch:
                    low_piece(i + 1, 2)
                a_low(i)

            with dve.Fori(1, NE - 1) as i:
                body(i, True)
            body(NE - 1, False)
            for q in (2, 3):
                low_piece(NE, q)

            def overflow(i):
                x_low(i)
                for b in (4, 6, 7, 8, 10, 11):
                    low_piece(i, b)
                clamp(i, True)
                swiglu(i)
                a_low(i)
                for q in (0, 2, 3):
                    low_piece(i + 1, q)
            run_overflow(dve, overflow)

            def gather_sum(j):
                if j >= 2:
                    dve.wait_ge(fin_ready, j - 1)
                dve.wait_ge(yk_in[j], 64)
                for k in range(TOPK):
                    if k:
                        dve.wait_ge(acc_step, 4 * j + k)
                    V.scalar_tensor_tensor(out=acc[:, j % 2, :], in0=yk[:, j, k, :], scalar=gates[:, j, k:k + 1],
                                           in1=acc[:, j % 2, :] if k else hres[:, j, :], op0=ALU.mult, op1=ALU.add).then_inc(acc_step, 1)

            def final_norm(j):
                dve.wait_ge(sd2, j + 1)
                V.reciprocal(stat[:, 44 + j:45 + j], stat[:, 40 + j:41 + j]).then_inc(rs2, 1)
                dve.wait_ge(rs2, j + 1)
                dve.wait_ge(fg_in, 16)
                V.scalar_tensor_tensor(out=fin[:, j % 2, :], in0=acc[:, j % 2, :], scalar=stat[:, 44 + j:45 + j], in1=fgain[:, :],
                                       op0=ALU.mult, op1=ALU.mult).then_inc(fin_ready, 1)

            for j in range(NT):
                gather_sum(j)
                if j:
                    final_norm(j - 1)
            final_norm(NT - 1)

        @block.gpsimd
        def _(gp):
            G = nc.gpsimd
            G.memset(scF[:, :, :], 0.0).then_inc(zeroed, 1)
            G.memset(scB[:, :, :], 0.0).then_inc(zeroed, 1)
            G.memset(vab[:, :, :, :], 0.0).then_inc(zeroed, 1)
            gp.wait_ge(bc_in, 32)
            G.tensor_scalar(nsink[:, :], sinkb[:, :], -1.0, None, ALU.mult).then_inc(nsink_ready, 1)
            for kv in range(KVH):
                src, dst = (slice(0, DH), slice(DH, P)) if kv % 2 == 0 else (slice(DH, P), slice(0, DH))
                gp.wait_ge(kd_ready, 2 * (kv // 2) + 2)
                gp.dma_start(kdup[dst, kv, :], kdup[src, kv, :]).then_inc(kdup_in, 16)
            gp.wait_ge(kdup_in, 16 * KVH)
            gp.wait_ge(av_ready, NT)

            def decayed(h, d):
                qd, ki, k = ((qdF, kiF, kF), (qdB, kiB, kB))[d]
                gp.wait_ge(ec_ready, 4 * h + 2 * d + 2)
                gp.wait_ge(dc_ready, 2 * h + d + 1)
                gp.wait_ge(q_ready, h + 1)
                gp.wait_ge(k_ready, 2 * h + 2)
                G.tensor_tensor(qd[:, :], qp[:, :], qd[:, :], ALU.mult).then_inc(qk_ready, 1)
                G.tensor_tensor(ki[:, :], k[:, :], ki[:, :], ALU.mult).then_inc(qk_ready, 1)

            def kv_of(h):
                kv = h // 2
                if not first(h):
                    gp.wait_ge(s_done, 8 * h)
                src = kdup[:, kv, :] if isinstance(h, int) else kdup[:, bass.ds(kv, 1), :].rearrange("p o t -> p (o t)")
                G.tensor_copy(kcur[:, :], src).then_inc(kcur_ready, 1)
                if not first(h):
                    gp.wait_ge(att_done, 8 * h)
                G.tensor_copy(vcur[:, :, :], av[:, :, bass.ds(kv * DH, DH)]).then_inc(vcur_ready, 1)

            def head(h, is_first, is_last):
                decayed(h, 0)
                decayed(h, 1)
                for j in range(NT):
                    gp.wait_ge(G1_step, 4 * h + j + 1)
                    G.tensor_tensor(G1[:, j, :], G1[:, j, :], gainq[:, :], ALU.mult).then_inc(G1_ready, 1)
                gp.wait_ge(zeroed, 3)
                gp.wait_ge(v_ready, 4 * h + 4)
                if not is_first:
                    gp.wait_ge(U_done, 2 * h)
                gp.wait_ge(G1_ready, 4 * h + 4)
                G.tensor_copy(vab[0:CH, :, 0, :], vv[0:CH, :, :]).then_inc(vab_ready, 1)
                gp.wait_ge(zeroed, 3)
                gp.wait_ge(vab_ready, 2 * h + 1)
                G.tensor_copy(vab[CH:P, :, 1, :], vv[CH:P, :, :]).then_inc(vab_ready, 1)
                if not is_last:
                    gp.wait_ge(vab_ready, 2 * h + 2)
                    kv_of(h + 1)

            gp.wait_ge(zeroed, 3)
            gp.wait_ge(lb_step, 10)
            kv_of(0)
            at_head(head, gp)

            def low_piece(k, b):
                low_part(gp, G, k, b, p_lop)

            low_piece(0, 1)
            gp.wait_ge(mg_ready, NH)
            G.memset(msk[:, NT, :], 0.0).then_inc(tri_ready, 1)
            G.tensor_copy(tri[:, :, :], cst[:, K_LT:K_CD].rearrange("p (a s) -> p a s", a=2)).then_inc(tri_ready, 1)

            gp.wait_ge(b_in, 16 * 6)
            step = [0]

            def chain(ins):
                ins.then_inc(b_step, 1)
                step[0] += 1
                gp.wait_ge(b_step, step[0])

            chain(G.tensor_copy(bias[:, :], braw[:, :]))
            for left in (2 * NE, NE):
                chain(G.tensor_tensor(braw[0:left, :], braw[0:left, :], bias[0:left, :], ALU.subtract))
                chain(G.tensor_copy(bias[0:left, :], braw[0:left, :]))
            assert step[0] == BIAS_STEPS
            low_piece(0, 5)
            G.memset(fill[:, :], NONE).then_inc(fill_ready, 1)
            for k in range(TOPK):
                pv = pay[:, :, :].rearrange("p (j k) c -> p j k c", k=TOPK)
                G.iota(pv[:, :, k, 0], pattern=[[P, NT]], base=0, channel_multiplier=1).then_inc(pay_ready, 1)
                G.iota(pv[:, :, k, 1], pattern=[[P, NT]], base=k * T, channel_multiplier=1).then_inc(pay_ready, 1)
            gp.wait_ge(pay_ready, 2 * TOPK)
            gp.wait_ge(fill_out, 16)
            gp.wait_ge(row_ready, 1)
            for n in range(NT * TOPK):
                gp.indirect_dma_start(slots, bass.IndirectOffsetOnAxis(ap=rowi[:, n:n + 1], axis=0),
                                      pay[:, n, :], None).then_inc(slot_out, 16)
            gp.wait_ge(lg_done, NT)
            gp.wait_ge(rT_ready, 2 * NT)
            G.memset(xg[:, :], 0.0).then_inc(xg_zero, 1)
            gp.wait_ge(xg_zero, 1)
            gp.wait_ge(tab_in, 16)
            gp.wait_ge(x2_out[0], 32)
            gp.wait_ge(x2_out[1], 32)
            gp.wait_ge(over_ready, 1)

            last_token, last_assignment = gp.to_reg(T - 1), gp.to_reg(TOPK * T - 1)

            def gather(i, code):
                if not first(i):
                    gp.wait_ge(xT_done, 2 * i)
                src = tab[:, code, :] if isinstance(code, int) else tab[:, bass.ds(code, 1), :].rearrange("p o c -> p (o c)")
                G.tensor_copy(ixg[:, :], src).then_inc(ix_ready, 1)
                n = i + 1 if isinstance(i, int) else gp.to_reg(i + 1)
                gp.wait_ge(x2_out[0], 32)
                gp.wait_ge(ix_ready, n)
                gp.indirect_dma_start(xg[:, :], None, x2d, bass.IndirectOffsetOnAxis(ap=ixg[:, 0:1], axis=0),
                                      bounds_check=last_token, oob_is_err=False).then_inc(xg_in, 16)

            def scatter(i, code):
                src = tab[:, code, :] if isinstance(code, int) else tab[:, bass.ds(code, 1), :].rearrange("p o c -> p (o c)")
                n, last = (i + 1, 16 * i) if isinstance(i, int) else (gp.to_reg(i + 1), gp.to_reg(16 * i))
                gp.wait_ge(tab_in, 16)
                gp.wait_ge(y_ready, n)
                if not first(i):
                    gp.wait_ge(y_out, last)
                G.tensor_copy(ixs[:, :], src).then_inc(ixs_ready, 1)
                gp.wait_ge(tab_in, 16)
                gp.wait_ge(ixs_ready, i + 1)
                gp.indirect_dma_start(yd, bass.IndirectOffsetOnAxis(ap=ixs[:, 1:2], axis=0), ysb[:, :], None,
                                      bounds_check=last_assignment, oob_is_err=False).then_inc(y_out, 16)

            gather(0, 0)
            low_piece(0, 9)
            gather(1, NB)

            def body(i, prefetch, is_second):
                low_piece(i, 1)
                if prefetch:
                    gather(i + 1, NB * (i + 1))
                if not is_second:
                    scatter(i - 2, NB * (i - 2))
                low_piece(i, 5)
                low_piece(i, 9)

            body(1, True, True)
            body(2, True, False)
            with gp.Fori(3, NE - 1) as i:
                body(i, True, False)
            body(NE - 1, False, False)
            low_piece(NE, 1)
            scatter(NE - 2, NB * (NE - 2))
            scatter(NE - 1, NB * (NE - 1))
            gp.wait_ge(y_out, 16 * NE)

            def overflow(i, code):
                code = gp.snap(code)
                gather(i, code)
                low_piece(i, 5)
                low_piece(i, 9)
                low_piece(i + 1, 1)
                scatter(i, code)
                gp.wait_ge(y_out, 16 * i + 16)
            run_overflow(gp, overflow, needs_code=True)
            G.memset(done[:, :], 0.0).then_inc(experts_done, 1)


_INS = ['x', 'norm_mix_gain', 'w_in', 'hg_lb_fwd', 'hg_lb_bwd', 'hg_norm_gain', 'attn_sink', 'w_out',
        'norm_ffn_gain', 'w_router', 'b_router', 'w_up_gate', 'b_up_gate', 'w_down', 'b_down', 'final_norm_gain']


def kernel(**inputs):
    import concourse.bacc as bacc
    from concourse.bass_utils import run_bass_kernel_spmd

    nc = bacc.Bacc("TRN2", target_bir_lowering=False, num_devices=1)
    arrays = {n: np.ascontiguousarray(inputs[n]) for n in _INS}
    arrays["consts"] = constants()
    arrays["selectors"] = bias_selectors()
    args = [nc.dram_tensor(f"in_{n}", a.shape, mybir.dt.from_np(a.dtype), kind="ExternalInput").ap()
            for n, a in arrays.items()]
    out = nc.dram_tensor("out_0", (1, T, D), F32, kind="ExternalOutput").ap()
    build(nc, *args, out)
    r = run_bass_kernel_spmd(nc, [{f"in_{n}": a for n, a in arrays.items()}], core_ids=[0])
    return r.results[0]["out_0"]
```

```python
from contextlib import ExitStack

import numpy as np

import concourse.bass as bass
from concourse import mybir

F32, F32R, BF16 = mybir.dt.float32, mybir.dt.float32r, mybir.dt.bfloat16
I32, U32 = mybir.dt.int32, mybir.dt.uint32
ALU, ACT, AX = mybir.AluOpType, mybir.ActivationFunctionType, mybir.AxisListType

P = 128
T, D = 512, 1024
NT, KD = T // P, D // P
NH = 8
CH = 64
NCH = T // CH
QH, KVH, DH = 16, 4, 64
WIN = 128
NE, TOPK, FF = 32, 4, 1024
RS_MAX = 2 * NT + 2
RAW, SPLIT = 6, 4
BODY = 12
BIAS_STEPS = 5
BLK = 96
NB = -(-T // BLK)
NBC_BITS = (NB - 1).bit_length()
NBC = 1 << NBC_BITS
MAXOVER = (T * TOPK - 1) // BLK
LIMIT, ALPHA = 7.0, 1.702
EPS = 1e-5
NONE = 1 << 20
SCALE = DH ** -0.5

C_Q, C_FF, C_FB, C_V, C_G = 0, D, 2 * D, 3 * D, 4 * D
C_AQ = 5 * D
C_AK = C_AQ + QH * DH
C_AV = C_AK + KVH * DH
C_GA = C_AV + KVH * DH
C_GB = C_GA + D

K_ID, K_TF, K_TB, K_KF, K_KB, K_REL, K_SL, K_IO, K_LT, K_ON, K_CD, K_P1, K_EPS, K_SE, K_AS, K_TH, K_END = np.cumsum(
    [0, P, P, P, T, T, 3 * P, QH, NE * NBC, P, P, NE * (NB - 1), 1, 1, NE, NT * TOPK, NB - 1]).tolist()
R_LF, R_LB, R_NG, R_END = 0, 16, 32, 40


def constants():
    c = np.zeros((P, K_END), np.float32)
    i, s = np.arange(P), np.arange(P)[:, None]
    c[:, K_ID:K_TF] = np.eye(P)
    same = (i[None] // CH) == (s // CH)
    c[:, K_TF:K_TB] = same & (s <= i[None])
    c[:, K_TB:K_KF] = same & (s >= i[None])
    t = np.arange(T)
    c[:, K_KF:K_KB] = t % CH != 0
    c[:, K_KB:K_REL] = t % CH != CH - 1
    rel = np.abs(s + WIN - np.arange(3 * P)[None])
    c[:, K_REL:K_SL] = np.where(rel <= WIN, -rel, -1e30)
    c[:, K_SL:K_IO] = 2.0 ** (-8.0 * np.arange(1, QH + 1) / QH) / SCALE
    c[:, K_IO:K_LT] = np.arange(NE * NBC)
    c[:, K_LT:K_ON] = s < i[None]
    c[:, K_ON:K_CD] = 1.0
    c[:, K_CD:K_P1] = (np.arange(NE)[:, None] * NBC + np.arange(1, NB)[None]).ravel()
    c[:, K_P1] = np.arange(P) + 1
    c[:, K_EPS] = EPS
    c[:, K_SE:K_AS] = s % NE == np.arange(NE)[None]
    j, k = np.arange(NT * TOPK) // TOPK, np.arange(NT * TOPK) % TOPK
    c[:, K_AS:K_TH] = k * T + j * P + s + 1
    c[:, K_TH:K_END] = BLK * np.arange(1, NB)
    return c


def build(nc, x, norm_mix_gain, w_in, hg_lb_fwd, hg_lb_bwd, hg_norm_gain, attn_sink, w_out,
          norm_ffn_gain, w_router, b_router, w_up_gate, b_up_gate, w_down, b_down,
          final_norm_gain, consts, out):
    w_in, w_out = w_in[0], w_out[0]
    over_list = nc.dram_tensor("over_list", [P, 1], I32, kind="Internal").ap()
    x2d = nc.dram_tensor("x2d", [T, D], F32, kind="Internal").ap()
    yd = nc.dram_tensor("yd", [TOPK * T, D], F32, kind="Internal").ap()

    BASE = 16512
    at = [BASE]

    def sb(name, shape, dt=F32):
        size = int(np.prod(shape[1:])) * (2 if dt == BF16 else 4)
        t = nc.alloc_sbuf_tensor_at(name, shape, dt, offset=at[0])
        at[0] += -(-size // 32) * 32
        return t

    cst = sb("cst", [P, K_END])
    vecs = sb("vecs", [P, R_END])
    rows = sb("rows", [R_END, P])
    lbs = sb("lbs", [P, 8, 16])
    fa = sb("fa", [P, 16])
    fb_ = sb("fb_", [P, 16])
    fn = sb("fn", [P, 16])
    fk = sb("fk", [P, 16])
    stat = sb("stat", [P, 64])
    small_top = at[0]

    xnH = sb("xnH", [P, KD, T], F32R)
    xnL = sb("xnL", [P, KD, T], F32R)
    fraw = sb("fraw", [P, 4, KD, P])
    tsH = sb("tsH", [P, KD, 4, P], F32R)
    tsL = sb("tsL", [P, KD, 4, P], F32R)
    wsH = sb("wsH", [P, 2, KD, P], F32R)
    wsL = sb("wsL", [P, 2, KD, P], F32R)
    front_w_top = at[0]
    merged = sb("merged", [P, NT, D])
    front_work = at[0]
    thF = sb("thF", [P, T]); thB = sb("thB", [P, T])
    qp = sb("qp", [P, T])
    fF = sb("fF", [P, T]); fB = sb("fB", [P, T])
    kF = sb("kF", [P, T]); kB = sb("kB", [P, T])
    qdF = sb("qdF", [P, T]); qdB = sb("qdB", [P, T])
    kiF = sb("kiF", [P, T]); kiB = sb("kiB", [P, T])
    dcF = sb("dcF", [P, NCH]); dcB = sb("dcB", [P, NCH])
    ktF = sb("ktF", [P, NT, P]); ktB = sb("ktB", [P, NT, P])
    scF = sb("scF", [P, NT, P]); scB = sb("scB", [P, NT, P])
    SF = sb("SF", [P, NCH, P]); SB = sb("SB", [P, NCH, P])
    vv = sb("vv", [P, NT, P])
    vab = sb("vab", [P, NT, 2, P])
    tht = sb("tht", [P, NT, 3, P])
    G1 = sb("G1", [P, NT, P])
    aqT = sb("aqT", [P, T])
    kdup = sb("kdup", [P, KVH, T])
    kcur = sb("kcur", [P, T])
    av = sb("av", [P, NT, KVH * DH])
    vcur = sb("vcur", [P, NT, DH])
    sbuf_s = sb("sbuf_s", [P, 2, 3 * P])
    sbuf_p = sb("sbuf_p", [P, 2, 3 * P])
    pTs = sb("pTs", [P, 2, 3, P])
    gainq = sb("gainq", [P, P])
    sinkb = sb("sinkb", [P, QH])
    nsink = sb("nsink", [P, QH])
    att = sb("att", [P, 64])
    orow = sb("orow", [P, 16])
    ogt = sb("ogt", [P, NT, P])
    attn1 = sb("attn1", [P, NT, P])
    assert at[0] <= 229368, at[0]
    at[0] = front_work
    xt = sb("xt", [P, NT, D])
    junk = sb("junk", [P, D])

    at[0] = small_top
    wraw = sb("wraw", [P, RAW, 2 * FF])
    wH = sb("wH", [P, SPLIT, 2 * FF], F32R)
    wL = sb("wL", [P, SPLIT, 2 * FF], F32R)
    moe_w_top = at[0]
    at[0] = max(moe_w_top, front_w_top)
    at[0] = max(at[0], front_work)
    hres = sb("hres", [P, NT, D])
    bias = sb("bias", [3 * NE, 3 * D], BF16)
    tab = sb("tab", [P, NE * NBC, 2], I32)
    sel = sb("sel", [3 * NE, 2, P], BF16)
    ixg = sb("ixg", [P, 2], I32)
    ixs = sb("ixs", [P, 2], I32)
    gates = sb("gates", [P, NT, TOPK])
    regs_in = sb("regs_in", [P, 4], I32)
    done = sb("done", [P, 1])
    fgain = sb("fgain", [P, D])
    moe_work = at[0]
    mTH = sb("mTH", [P, KD, T], F32R)
    mTL = sb("mTL", [P, KD, T], F32R)
    ngain = sb("ngain", [P, D])
    xr = sb("xr", [P, 2, D])
    mid_top = at[0]
    at[0] = mid_top - 3 * D * 4
    ovf = sb("ovf", [P, 4, NE * (NB - 1)])
    at[0] = moe_work
    rT = sb("rT", [P, KD, T])
    at[0] = mid_top
    wr = sb("wr", [P, KD, NE])
    brb = sb("brb", [P, NE])
    lg = sb("lg", [P, NT, NE])
    v8 = sb("v8", [P, NT, 8])
    i8 = sb("i8", [P, NT, 8], U32)
    idf = sb("idf", [P, NT, 8])
    oh = sb("oh", [P, NT, TOPK, NE])
    msk = sb("msk", [P, NT + 1, NE], BF16)
    tri = sb("tri", [P, 2, P], BF16)
    msum = sb("msum", [P, NE])
    pk = sb("pk", [P, NT, TOPK, NE])
    posk = sb("posk", [P, NT * TOPK])
    past = sb("past", [P, NT * TOPK, NB - 1])
    blk_ = sb("blk_", [P, NT * TOPK])
    slotf = sb("slotf", [P, NT * TOPK])
    colf = sb("colf", [P, NT * TOPK])
    empty = sb("empty", [P, NE * NBC])
    tabf = sb("tabf", [P, NE * NBC])
    gst = sb("gst", [P, NT, 8])
    ovc = sb("ovc", [P, 4])
    ovi = sb("ovi", [P, 2], I32)
    assert at[0] <= 229368, at[0]
    at[0] = moe_work + 8192
    hot_slot = sb("hot_slot", [P, NT * TOPK, P])
    hot_col = sb("hot_col", [P, NT * TOPK, NE * NBC])
    assert at[0] <= mid_top
    at[0] = moe_work
    xg = sb("xg", [P, D])
    xTH = sb("xTH", [P, KD, BLK], F32R)
    xTL = sb("xTL", [P, KD, BLK], F32R)
    gcl = sb("gcl", [P, FF]); ucl = sb("ucl", [P, FF]); sg = sb("sg", [P, FF]); actv = sb("actv", [P, FF])
    aTH = sb("aTH", [P, KD, BLK], F32R)
    aTL = sb("aTL", [P, KD, BLK], F32R)
    ysb = sb("ysb", [P, D])
    at[0] = small_top + 4 * 2 * FF * 4
    braw = sb("braw", [3 * NE, 3 * D])
    assert at[0] <= small_top + RAW * 2 * FF * 4
    at[0] = small_top
    yk = sb("yk", [P, NT, TOPK, D])
    acc = sb("acc", [P, 2, D])
    fin = sb("fin", [P, 2, D])

    nc_psum = nc.alloc_psum_tensor("psum", [P, 8 * 512], F32)
    bank = [nc_psum[:, i * 512:(i + 1) * 512] for i in range(8)]

    def sem(name):
        return nc.alloc_semaphore(name)

    def sems(name, n):
        return [sem(f"{name}{i}") for i in range(n)]

    ident = cst[:, K_ID:K_TF]
    eps = cst[:, K_EPS:K_EPS + 1]
    gain_mix = [vecs[:, R_NG + k:R_NG + k + 1] for k in range(KD)]

    def mm3(ps, lh, ll, rh, rl, start, stop):
        nc.tensor.matmul(ps, lh, rh, start=start, stop=False)
        nc.tensor.matmul(ps, lh, rl, start=False, stop=False)
        return nc.tensor.matmul(ps, ll, rh, start=False, stop=stop)

    id_in, eps_in, cst_in, vec_in, bc_in = sem("id_in"), sem("eps_in"), sem("cst_in"), sem("vec_in"), sem("bc_in")
    x_in = sems("x_in", NT)
    fraw_in, wraw_in = sems("fraw_in", 4), sems("wraw_in", RAW)
    kdup_in = sem("kdup_in")
    sq0, sd0, rs0, xn0 = sem("sq0"), sem("sd0"), sem("rs0"), sem("xn0")
    xt_done, xh_done, xl_done = sem("xt_done"), sem("xh_done"), sem("xl_done")
    vecT_done, vec_ready, lb_step, lb_exp = sem("vecT_done"), sem("vec_ready"), sem("lb_step"), sem("lb_exp")
    zeroed = sem("zeroed")
    w_hi, w_lo, proj_done = sem("w_hi"), sem("w_lo"), sem("proj_done")
    kd_ready, av_ready = sem("kd_ready"), sem("av_ready")
    th_ready, f_ready, k_ready, ln_ready, cum_ready = sem("th_ready"), sem("f_ready"), sem("k_ready"), sem("ln_ready"), sem("cum_ready")
    q_ready, ec_ready, dc_ready, qk_ready = sem("q_ready"), sem("ec_ready"), sem("dc_ready"), sem("qk_ready")
    kT_done, kt_ready, sc_done, sc_ready = sem("kT_done"), sem("kt_ready"), sem("sc_done"), sem("sc_ready")
    U_done, st_ready, o_done = sem("U_done"), sem("st_ready"), sem("o_done")
    tht_ready, v_ready, ts_free, G1_step, G1_ready, vab_ready = sem("tht_ready"), sem("v_ready"), sem("ts_free"), sem("G1_step"), sem("G1_ready"), sem("vab_ready")
    osq_ready, oms_ready, osd_ready, ors_ready, og_ready, mg_ready = sem("osq_ready"), sem("oms_ready"), sem("osd_ready"), sem("ors_ready"), sem("og_ready"), sem("mg_ready")
    aq_ready, kcur_ready, vcur_ready = sem("aq_ready"), sem("kcur_ready"), sem("vcur_ready")
    s_done, s_ready, mx_ready, nm_ready, p_ready = sem("s_done"), sem("s_ready"), sem("mx_ready"), sem("nm_ready"), sem("p_ready")
    pT_done, pT_ready, att_done = sem("pT_done"), sem("pT_ready"), sem("att_done")
    se_ready, l_step, att_step, ma_ready = sem("se_ready"), sem("l_step"), sem("att_step"), sem("ma_ready")
    mT_done, mh_done, ml_done = sem("mT_done"), sem("mh_done"), sem("ml_done")
    wo_done, h_in, h_ready = sem("wo_done"), sem("h_in"), sem("h_ready")
    sq1, sd1, rs1, xr_ready, x2_out = sem("sq1"), sem("sd1"), sem("rs1"), sem("xr_ready"), sems("x2_out", 2)
    b_in, b_step = sem("b_in"), sem("b_step")
    mi_ready, rT_done, rT_ready, wr_in, lg_done, r_step, rexp_ready = sem("mi_ready"), sem("rT_done"), sem("rT_ready"), sem("wr_in"), sem("lg_done"), sem("r_step"), sem("rexp_ready")
    tri_ready, mask_ready, pos_done, place_ready = sem("tri_ready"), sem("mask_ready"), sem("pos_done"), sem("place_ready")
    hot_slot_ready, hot_col_ready, hot_col_p_ready, tabT_done, tab_ready = sem("hot_slot_ready"), sem("hot_col_ready"), sem("hot_col_p_ready"), sem("tabT_done"), sem("tab_ready")
    over_ready, over_out = sem("over_ready"), sem("over_out")
    p_hi, p_lo, p_lop, p_used = sem("p_hi"), sem("p_lo"), sem("p_lop"), sem("p_used")
    sel_ready = sems("sel_ready", 2)
    ix_ready, xg_in, xg_zero = sem("ix_ready"), sem("xg_in"), sem("xg_zero")
    xT_done, xTh_ready, xTl_ready = sem("xT_done"), sem("xTh_ready"), sem("xTl_ready")
    g_ready, ucl_ready, sg_ready, t_ready, act_ready = sem("g_ready"), sem("ucl_ready"), sem("sg_ready"), sem("t_ready"), sem("act_ready")
    aT_done, aTh_ready, aTl_ready = sem("aT_done"), sem("aTh_ready"), sem("aTl_ready")
    y_ready, y_out, experts_done = sem("y_ready"), sem("y_out"), sem("experts_done")
    yk_in, yk_edge, acc_step, sq2, sd2, rs2, fs_ready, fin_p_ready, fin_ready, out_done = sems("yk_in", NT - 2), sems("yk_edge", 2 * TOPK), sem("acc_step"), sem("sq2"), sem("sd2"), sem("rs2"), sem("fs_ready"), sem("fin_p_ready"), sem("fin_ready"), sems("out_done", 2)
    nsink_ready, ixs_ready = sem("nsink_ready"), sem("ixs_ready")
    gains_in = sem("gains_in")

    PRE_B, PRE_G = 4, 6
    UNITS = [(n, a) for n in range(NT) for a in range(2)]

    def span(n):
        tiles = [t for t in (n - 1, n, n + 1) if 0 <= t < NT]
        return tiles, (tiles[0] - (n - 1)) * P

    block_cols = [C_AQ, C_FF, C_FB, C_Q, C_V, C_G, C_GA, C_GB]
    w_in_t = w_in.rearrange("(k p) n -> p k n", p=P)

    def at_head(fn, eng):
        fn(0, True, False)
        with eng.Fori(1, NH - 1) as h:
            fn(h, False, False)
        fn(NH - 1, False, True)

    POOL_B = (1, 5, 9)
    VEC_B = tuple(b for b in range(BODY) if b not in POOL_B)

    POOL_HOT = tuple(range(NT * TOPK - 3, NT * TOPK))

    def first(i):
        return isinstance(i, int) and i == 0

    def wait_split(eng, k, b):
        if b in POOL_B:
            eng.wait_ge(p_lop, len(POOL_B) * k + (POOL_B.index(b) + 1))
        else:
            eng.wait_ge(p_lo, len(VEC_B) * k + (VEC_B.index(b) + 1))

    def high(act, k, b):
        act.wait_ge(wraw_in[b % RAW], 16 * BODY // RAW * k + 16 * (b // RAW + 1))
        if not (first(k) and b < SPLIT):
            act.wait_ge(p_used, BODY * k + (b + 1 - SPLIT))
        nc.scalar.activation(wH[:, b % SPLIT, :], wraw[:, b % RAW, :], ACT.Copy).then_inc(p_hi, 1)

    def low_part(eng, engine, k, b, done):
        eng.wait_ge(p_hi, BODY * k + (b + 1))
        engine.tensor_tensor(wL[:, b % SPLIT, :], wraw[:, b % RAW, :], wH[:, b % SPLIT, :].bitcast(F32),
                             ALU.subtract).then_inc(done, 1)

    def up_at(i, over=False):
        return (i, 4) if over or first(i) else (i, 0)

    def down_at(i, over=False):
        return (i + 1, 0) if over or (isinstance(i, int) and i == NE - 1) else (i + 1, 8)

    def used(at_, n):
        return BODY * at_[0] + (at_[1] + n)

    def run_overflow(eng, item, needs_code=False):
        eng.wait_ge(over_ready, 1)
        if needs_code:
            eng.wait_ge(over_out, 16)
        n = eng.value_load(regs_in[0:1, 0:1], min_val=0, max_val=MAXOVER)
        with eng.If(n > 0):
            with eng.Fori(0, MAXOVER) as j:
                with eng.If(n > j):
                    if needs_code:
                        code = eng.value_load(over_list[bass.ds(j, 1), 0:1], min_val=0, max_val=NE * NBC - 1)
                        item(j + NE, code)
                    else:
                        item(j + NE)

    hu = nc_psum[:, 0:4 * 512]
    ybank = nc_psum[:, 4 * 512:6 * 512]
    with nc.Block() as block:

        @block.sync
        def _(sp):
            sp.dma_start(cst[:, K_ID:K_TF], consts[:, K_ID:K_TF]).then_inc(id_in, 16)
            for r, a in ((R_LF, hg_lb_fwd), (R_LB, hg_lb_bwd)):
                sp.dma_start(rows[r:r + 16, :], a.rearrange("a (k p) -> (a k) p", p=P)).then_inc(vec_in, 16)
            sp.dma_start(rows[R_NG:R_END, :], norm_mix_gain.rearrange("a (k p) -> (a k) p", p=P)).then_inc(vec_in, 16)
            for j in range(NT):
                sp.dma_start(xt[:, j, :], x[0, j * P:(j + 1) * P, :]).then_inc(x_in[j], 16)
                if j == 0:
                    sp.dma_start(cst[:, K_P1:], consts[:, K_P1:]).then_inc(eps_in, 16)

            def load_block(slot, col, free):
                src = w_in_t[:, :, bass.ds(col, P)] if not isinstance(col, int) else w_in_t[:, :, col:col + P]
                if free is not None:
                    sp.wait_ge(fraw_in[slot], 16)
                    sp.wait_ge(w_lo, free)
                sp.dma_start(fraw[:, slot, :, :], src).then_inc(fraw_in[slot], 16)

            for b, col in enumerate((C_AK, C_AK + P, C_AV, C_AV + P)):
                load_block(b, col, None)
            sp.dma_start(gainq[:, :], hg_norm_gain.to_broadcast([P, P])).then_inc(bc_in, 16)
            sp.dma_start(sinkb[:, :], attn_sink.to_broadcast([P, QH])).then_inc(bc_in, 16)
            sp.dma_start(cst[:, K_TF:K_P1], consts[:, K_TF:K_P1]).then_inc(cst_in, 16)
            for b in range(8):
                load_block(b % 4, block_cols[b], PRE_B + b - 3)
            with sp.Fori(1, NH) as h:
                for b in range(8):
                    col = sp.snap(h * P + block_cols[b])
                    load_block(b % 4, col, sp.to_reg(8 * h + (PRE_B + b - 3)))

            sp.wait_ge(w_lo, PRE_B + 8 * NH)
            sp.wait_ge(proj_done, PRE_G + 8 * NH)
            d_src0 = w_out.rearrange("(q k p) n -> q p k n", p=P, k=2)

            def load_piece(k, b, src):
                if b >= RAW:
                    wait_split(sp, k, b - RAW)
                elif not first(k):
                    wait_split(sp, k - 1, b + BODY - RAW)
                sp.dma_start(wraw[:, b % RAW, :] if len(src.shape) == 2 else
                             wraw[:, b % RAW, :].rearrange("p (k n) -> p k n", k=2), src).then_inc(wraw_in[b % RAW], 16)

            def up_src(e, p):
                return w_up_gate[0][bass.ds(e, 1), p * P:(p + 1) * P, :].rearrange("o p n -> (o p) n")

            def down_src(e, q):
                return w_down[0][bass.ds(e, 1), q * 2 * P:(q + 1) * 2 * P, :].rearrange("o (k p) n -> p (o k) n", p=P)

            for q in range(4):
                load_piece(0, q, d_src0[q])
            for r in range(3):
                sp.dma_start(braw[r * NE:(r + 1) * NE, 0:2 * FF], b_up_gate[0]).then_inc(b_in, 16)
                sp.dma_start(braw[r * NE:(r + 1) * NE, 2 * FF:], b_down[0]).then_inc(b_in, 16)
            sp.wait_ge(mg_ready, NH)
            for j in range(NT):
                sp.dma_start(hres[:, j, :], x[0, j * P:(j + 1) * P, :]).then_inc(h_in, 16)
            sp.dma_start(ngain[:, :], norm_ffn_gain.to_broadcast([P, D])).then_inc(gains_in, 16)
            sp.dma_start(wr[:, :, :], w_router[0].rearrange("(k p) n -> p k n", p=P)).then_inc(wr_in, 16)
            sp.dma_start(brb[:, :], b_router.to_broadcast([P, NE])).then_inc(wr_in, 16)
            sp.dma_start(fgain[:, :], final_norm_gain.rearrange("(a n) -> a n", a=1).to_broadcast([P, D])).then_inc(gains_in, 16)
            for p in range(2, 6):
                load_piece(0, 4 + p, up_src(0, p))
            for j in range(NT):
                sp.wait_ge(xr_ready, j + 1)
                sp.dma_start(x2d[j * P:(j + 1) * P, :], xr[:, j % 2, :]).then_inc(x2_out[j % 2], 16)
            sp.wait_ge(b_step, BIAS_STEPS)
            for p in range(2):
                load_piece(0, 4 + p, up_src(0, p))
            def load_body(e):
                for p in range(8):
                    load_piece(e, p, up_src(e, p))
                for q in range(4):
                    load_piece(e, 8 + q, down_src(e - 1, q))

            for p in range(6, 8):
                load_piece(0, 4 + p, up_src(0, p))
            load_body(1)
            sp.wait_ge(over_ready, 1)
            sp.dma_start(over_list[:, :], ovi[:, 0:1]).then_inc(over_out, 16)
            with sp.Fori(2, NE) as e:
                load_body(e)
            for q in range(4):
                load_piece(NE, q, down_src(NE - 1, q))

            def overflow(i, code):
                e = nc.s_assert_within(code >> NBC_BITS, 0, NE - 1, skip_runtime_bounds_check_because="codes are below NE * NBC")
                for p in range(8):
                    load_piece(i, 4 + p, up_src(e, p))
                for q in range(4):
                    load_piece(i + 1, q, down_src(e, q))
            run_overflow(sp, overflow, needs_code=True)

            sp.wait_ge(experts_done, 1)
            for j in range(NT):
                for k in range(TOPK):
                    r = k * T + j * P
                    sp.dma_start(yk[:, j, k, :], yd[r:r + P, :]).then_inc(yk_in[j - 1] if 0 < j < NT - 1 else yk_edge[min(j, 1) * TOPK + k], 16)
            for j in range(NT):
                if j < NT - 1:
                    sp.wait_ge(fin_p_ready, j + 1)
                else:
                    sp.wait_ge(fin_ready, 1)
                sp.dma_start(out[0, j * P:(j + 1) * P, :], fin[:, j % 2, :]).then_inc(out_done[j % 2], 16)
            sp.wait_ge(out_done[0], 32)
            sp.wait_ge(out_done[1], 32)
            for s_, n_ in ((x2_out[0], 32), (x2_out[1], 32), (over_out, 16)):
                sp.wait_ge(s_, n_)

        @block.tensor
        def _(pe):
            pe.wait_ge(id_in, 16)
            pe.wait_ge(vec_in, 48)
            nc.tensor.transpose(bank[0][:, 0:R_END], rows[:, :], cst[0:R_END, K_ID:K_ID + R_END]).then_inc(vecT_done, 1)
            pe.wait_ge(vec_ready, 1)
            for k in range(KD):
                for j in range(NT):
                    if k == 0:
                        pe.wait_ge(xn0, j + 1)
                    last = nc.tensor.transpose(bank[k][:, j * P:(j + 1) * P], xt[:, j, k * P:(k + 1) * P], ident)
                last.then_inc(xt_done, 1)

            def project_cols(g, slot, by_tile, ready, bank_sem, bank_n):
                pe.wait_ge(w_lo, ready)
                if bank_sem is not None:
                    pe.wait_ge(bank_sem, bank_n)
                for k in range(KD):
                    if by_tile:
                        pe.wait_ge(xl_done, k + 1)
                    last = mm3(bank[g % 2], wsH[:, slot, k, :], wsL[:, slot, k, :], xnH[:, k, :], xnL[:, k, :],
                               k == 0, k == KD - 1)
                last.then_inc(proj_done, 1)

            def project_tokens(g, j, nblk, ready, bank_sem, bank_n):
                pe.wait_ge(w_lo, ready)
                pe.wait_ge(bank_sem, bank_n)
                ps = bank[g % 2][:, 0:nblk * P].rearrange("p (b n) -> p b n", b=nblk)
                tok = slice(j * P, (j + 1) * P)
                for k in range(KD):
                    last = mm3(ps, xnH[:, k, tok], xnL[:, k, tok], tsH[:, k, 0:nblk, :], tsL[:, k, 0:nblk, :],
                               k == 0, k == KD - 1)
                last.then_inc(proj_done, 1)

            project_cols(0, 0, True, 1, None, None)
            project_cols(1, 1, False, 2, None, None)
            for j, (s_, n_) in enumerate(((kd_ready, 2), (kd_ready, 4), (av_ready, 1), (av_ready, 2))):
                project_tokens(2 + j, j, 2, 4, s_, n_)

            U4 = nc_psum[:, 4 * 512:6 * 512].rearrange("p (n v) -> p n v", n=NCH)
            U6 = nc_psum[:, 6 * 512:8 * 512].rearrange("p (n v) -> p n v", n=NCH)

            def updates(h):
                pe.wait_ge(vab_ready, 2 * h + 2)
                for d, (kt, U) in enumerate(((ktF, U4), (ktB, U6))):
                    pe.wait_ge(kt_ready, 2 * h + d + 1)
                    if d == 0:
                        pe.wait_ge(s_ready, 8 * h + 8)
                    else:
                        pe.wait_ge(att_step, 2 * h + 1)
                        if not first(h):
                            pe.wait_ge(og_ready, 4 * h)
                    for j in range(NT):
                        last = nc.tensor.matmul(U[:, 2 * j:2 * j + 2, :], kt[:, j, :], vab[:, j, :, :],
                                                start=True, stop=True)
                    last.then_inc(U_done, 1)

            def output(h):
                pe.wait_ge(st_ready, 14 * h + 14)
                pe.wait_ge(sc_ready, 2 * h + 2)
                for j in range(NT):
                    ps = bank[6][:, j * P:(j + 1) * P]
                    nc.tensor.matmul(ps, scF[:, j, :], vv[:, j, :], start=True, stop=False, skip_group_check=True)
                    nc.tensor.matmul(ps, scB[:, j, :], vv[:, j, :], start=False, stop=False, skip_group_check=True)
                    for c in range(2):
                        n = 2 * j + c
                        tok, half = slice(n * CH, (n + 1) * CH), bank[6][c * CH:(c + 1) * CH, j * P:(j + 1) * P]
                        for qd, S, has in ((qdF, SF, n > 0), (qdB, SB, n < NCH - 1)):
                            if has:
                                last = nc.tensor.matmul(half, qd[:, tok], S[:, n, :], start=False, stop=True,
                                                        skip_group_check=True)
                last.then_inc(o_done, 1)

            def scores(h, us):
                if us[0] == 0:
                    pe.wait_ge(aq_ready, h + 1)
                    pe.wait_ge(kcur_ready, h + 1)
                for u in us:
                    n, a = UNITS[u]
                    if u >= 2:
                        pe.wait_ge(s_ready, 8 * h + (u - 1))
                    elif not first(h):
                        pe.wait_ge(st_ready, 14 * (h - 1) + 1)
                    tiles, c0 = span(n)
                    half = slice(a * DH, (a + 1) * DH)
                    nc.tensor.matmul(bank[4 + a][:, 0:len(tiles) * P], aqT[half, n * P:(n + 1) * P],
                                     kcur[half, tiles[0] * P:(tiles[-1] + 1) * P], start=True, stop=True).then_inc(s_done, 1)

            def turn(h, us):
                for u in us:
                    n, a = UNITS[u]
                    tiles, _ = span(n)
                    pe.wait_ge(p_ready, 8 * h + u + 1)
                    if u >= 2:
                        pe.wait_ge(pT_ready, 8 * h + (u - 1))
                    elif not first(h):
                        pe.wait_ge(kt_ready, 2 * h)
                        pe.wait_ge(sc_ready, 2 * h)
                    for i in range(len(tiles)):
                        last = nc.tensor.transpose(bank[2 + a][:, i * P:(i + 1) * P], sbuf_p[:, a, i * P:(i + 1) * P], ident)
                    last.then_inc(pT_done, 1)

            def attend(h, us):
                for u in us:
                    n, a = UNITS[u]
                    tiles, _ = span(n)
                    pe.wait_ge(pT_ready, 8 * h + u + 1)
                    if u == 0:
                        pe.wait_ge(vcur_ready, h + 1)
                        if not first(h):
                            pe.wait_ge(st_ready, 14 * h)
                    for i, t in enumerate(tiles):
                        last = nc.tensor.matmul(bank[7][:, n * P + a * DH:n * P + (a + 1) * DH], pTs[:, a, i, :],
                                                vcur[:, t, :], start=i == 0, stop=i == len(tiles) - 1)
                    last.then_inc(att_done, 1)

            def keys_and_chunk_scores(h, d):
                ki, qd = ((kiF, qdF), (kiB, qdB))[d]
                pe.wait_ge(qk_ready, 4 * h + 2 * d + 2)
                if d == 0:
                    pe.wait_ge(pT_ready, 8 * h + 8)
                else:
                    pe.wait_ge(kt_ready, 2 * h + 1)
                for j in range(NT):
                    last = nc.tensor.transpose(bank[2][:, j * P:(j + 1) * P], ki[:, j * P:(j + 1) * P], ident)
                last.then_inc(kT_done, 1)
                if d == 1:
                    pe.wait_ge(sc_ready, 2 * h + 1)
                for j in range(NT):
                    tok = slice(j * P, (j + 1) * P)
                    last = nc.tensor.matmul(bank[3][:, tok], ki[:, tok], qd[:, tok], start=True, stop=True)
                last.then_inc(sc_done, 1)

            def head(h, is_first, is_last):
                pg, pb = 8 * h + PRE_G, 8 * h + PRE_B
                if is_first:
                    project_cols(0, 0, False, pb + 1, av_ready, 3)
                else:
                    project_cols(0, 0, False, pb + 1, ts_free, 4 * h - 1)
                    updates(h - 1)
                project_cols(1, 1, False, pb + 2, av_ready if is_first else ts_free, 4 if is_first else 4 * h)
                scores(h, (0, 1))
                project_cols(2, 0, False, pb + 3, aq_ready, h + 1)
                if not is_first:
                    output(h - 1)
                turn(h, (0, 1))
                scores(h, (2, 3))
                project_cols(3, 1, False, pb + 4, th_ready, 3 * h + 1)
                attend(h, (0, 1))
                turn(h, (2, 3))
                scores(h, (4, 5))
                project_tokens(4, 0, 4, pb + 8, th_ready, 3 * h + 2)
                attend(h, (2, 3))
                turn(h, (4, 5))
                scores(h, (6, 7))
                project_tokens(5, 1, 4, pb + 8, q_ready, h + 1)
                attend(h, (4, 5))
                turn(h, (6, 7))
                project_tokens(6, 2, 4, pb + 8, ts_free, 4 * h + 1)
                attend(h, (6, 7))
                keys_and_chunk_scores(h, 0)
                project_tokens(7, 3, 4, pb + 8, ts_free, 4 * h + 2)
                keys_and_chunk_scores(h, 1)

            at_head(head, pe)
            updates(NH - 1)
            output(NH - 1)

            def half_piece(kk, n):
                return slice(kk * D + n * 512, kk * D + (n + 1) * 512)

            for k in range(KD):
                b_ = 2 + k % 6
                if k >= 6:
                    pe.wait_ge(ml_done, k - 5)
                elif k == 0:
                    pe.wait_ge(mg_ready, NH)
                for j in range(NT):
                    last = nc.tensor.transpose(bank[b_][:, j * P:(j + 1) * P], merged[:, j, k * P:(k + 1) * P], ident)
                last.then_inc(mT_done, 1)
            def out_projection(j):
                for q in range(4):
                    if j == 0:
                        wait_split(pe, 0, q)
                    for kk in range(2):
                        k = 2 * q + kk
                        if j == 0:
                            pe.wait_ge(ml_done, k + 1)
                        for n in range(2):
                            last = mm3(bank[2 * j + n], mTH[:, k, j * P:(j + 1) * P], mTL[:, k, j * P:(j + 1) * P],
                                       wH[:, q, half_piece(kk, n)], wL[:, q, half_piece(kk, n)], k == 0, k == KD - 1)
                    if j == NT - 1:
                        last.then_inc(p_used, 1)
                if j < NT - 1:
                    last.then_inc(wo_done, 1)

            def turn_rows(j):
                pe.wait_ge(xr_ready, j + 1)
                for half in range(2):
                    if j:
                        pe.wait_ge(rT_ready, 2 * (j - 1) + half + 1)
                    for k in range(4 * half, 4 * half + 4):
                        last = nc.tensor.transpose(bank[half][:, (k % 4) * P:(k % 4 + 1) * P], xr[:, j % 2, k * P:(k + 1) * P], ident)
                    last.then_inc(rT_done, 1)

            def logits(j):
                pe.wait_ge(rT_ready, 2 * j + 2)
                pe.wait_ge(wr_in, 32)
                pe.wait_ge(h_ready, 2 * (1 + j // 2) + 2)
                for k in range(KD):
                    last = nc.tensor.matmul(bank[2 + j][:, 0:NE], rT[:, k, j * P:(j + 1) * P], wr[:, k, :],
                                            start=k == 0, stop=k == KD - 1)
                last.then_inc(lg_done, 1)

            out_projection(0)
            out_projection(1)
            turn_rows(0)
            out_projection(2)
            logits(0)
            turn_rows(1)
            out_projection(3)
            logits(1)
            turn_rows(2)
            logits(2)
            turn_rows(3)
            logits(3)
            pe.wait_ge(mask_ready, 1)
            pe.wait_ge(tri_ready, 2)
            nc.tensor.matmul(bank[6][:, 0:(NT + 1) * NE], tri[:, 1, :], msk[:, NT:, :].to_broadcast([P, NT + 1, NE]),
                             start=True, stop=False)
            for t in range(NT):
                nc.tensor.matmul(bank[6][:, (t + 1) * NE:(NT + 1) * NE], tri[:, 1, :],
                                 msk[:, t:t + 1, :].to_broadcast([P, NT - t, NE]), start=False, stop=False,
                                 skip_group_check=True)
            last = nc.tensor.matmul(bank[6][:, 0:(NT + 1) * NE], tri[:, 0, :], msk[:, :, :], start=False, stop=True)
            last.then_inc(pos_done, 1)
            for n in range(NT * TOPK):
                pe.wait_ge(hot_slot_ready, n + 1)
                if n in POOL_HOT:
                    pe.wait_ge(hot_col_p_ready, POOL_HOT.index(n) + 1)
                else:
                    pe.wait_ge(hot_col_ready, n + 1)
                last = nc.tensor.matmul(bank[7][:, 0:NE * NBC], hot_slot[:, n, :], hot_col[:, n, :], start=n == 0,
                                        stop=n == NT * TOPK - 1)
            last.then_inc(tabT_done, 1)

            def x_part(i):
                pe.wait_ge(xg_in, 16 * i + 16)
                for b_ in range(2):
                    for k in range(4 * b_, 4 * b_ + 4):
                        last = nc.tensor.transpose(bank[6 + b_][:, (k % 4) * BLK:(k % 4 + 1) * BLK], xg[0:BLK, k * P:(k + 1) * P], ident[0:BLK, 0:BLK])
                    last.then_inc(xT_done, 1)

            def up_part(i, over=False, turn_last=False):
                k, b0 = up_at(i, over)
                if not first(i):
                    pe.wait_ge(ucl_ready, i)
                pe.wait_ge(sel_ready[0], i + 1)
                if first(i):
                    pe.wait_ge(b_step, BIAS_STEPS)
                for n in range(4):
                    nc.tensor.matmul(bank[n][0:BLK, :], sel[:, 0, 0:BLK], bias[:, n * 512:(n + 1) * 512], start=True, stop=False)
                pe.wait_ge(xTl_ready, 2 * i + 2)
                for p in range(8):
                    wait_split(pe, k, b0 + p)
                    slot = (b0 + p) % SPLIT
                    for n in range(4):
                        cols = slice(n * 512, (n + 1) * 512)
                        last = mm3(bank[n][0:BLK, :], xTH[:, p, :], xTL[:, p, :], wH[:, slot, cols], wL[:, slot, cols], False, p == 7)
                    last.then_inc(p_used, 1)
                    if turn_last and p == 1:
                        a_part(i - 1, 2 * i + 2)

            def a_part(i, x_before):
                pe.wait_ge(act_ready, i + 1)
                pe.wait_ge(xTl_ready, x_before)
                for b_ in range(2):
                    for k in range(4 * b_, 4 * b_ + 4):
                        last = nc.tensor.transpose(bank[6 + b_][:, (k % 4) * BLK:(k % 4 + 1) * BLK], actv[0:BLK, k * P:(k + 1) * P], ident[0:BLK, 0:BLK])
                    last.then_inc(aT_done, 1)

            def down_part(i, over=False):
                k, b0 = down_at(i, over)
                if not first(i):
                    pe.wait_ge(y_ready, i)
                pe.wait_ge(sel_ready[1], i + 1)
                for n in range(2):
                    nc.tensor.matmul(bank[4 + n][0:BLK, :], sel[:, 1, 0:BLK], bias[:, (4 + n) * 512:(5 + n) * 512], start=True, stop=False)
                pe.wait_ge(aTl_ready, 2 * i + 2)
                for q in range(4):
                    wait_split(pe, k, b0 + q)
                    slot = (b0 + q) % SPLIT
                    for kk in range(2):
                        for n in range(2):
                            last = mm3(bank[4 + n][0:BLK, :], aTH[:, 2 * q + kk, :], aTL[:, 2 * q + kk, :], wH[:, slot, half_piece(kk, n)],
                                       wL[:, slot, half_piece(kk, n)], False, 2 * q + kk == KD - 1)
                    last.then_inc(p_used, 1)

            x_part(0)
            up_part(0)
            x_part(1)
            with pe.Fori(1, NE - 1) as i:
                up_part(i, turn_last=True)
                pe.wait_ge(aTl_ready, 2 * i)
                x_part(i + 1)
                down_part(i - 1)
            up_part(NE - 1, turn_last=True)
            down_part(NE - 2)
            a_part(NE - 1, 2 * NE)
            down_part(NE - 1)

            def overflow(i):
                pe.wait_ge(aTl_ready, 2 * i)
                x_part(i)
                up_part(i, True)
                a_part(i, 2 * i + 2)
                down_part(i, True)
            run_overflow(pe, overflow)

        @block.scalar
        def _(act):
            A = nc.scalar.activation
            act.wait_ge(lb_step, 2)
            A(lbs[:, 2:4, :], lbs[:, 0:2, :], ACT.Exp).then_inc(lb_exp, 1)
            for j in range(NT):
                act.wait_ge(x_in[j], 16)
                if j:
                    act.wait_ge(sq0, j)
                A(junk[:, :], xt[:, j, :], ACT.Square, accum_out=stat[:, j:j + 1]).then_inc(sq0, 1)
            for j in range(NT):
                if j == 0:
                    act.wait_ge(eps_in, 16)
                act.wait_ge(sq0, j + 1)
                A(stat[:, 8 + j:9 + j], stat[:, j:j + 1], ACT.Sqrt, scale=1.0 / D, bias=eps).then_inc(sd0, 1)
            def split_ws(b, slot, raw_slot, raw_n, used):
                act.wait_ge(fraw_in[raw_slot], raw_n)
                if used is not None:
                    act.wait_ge(proj_done, used)
                A(wsH[:, slot, :, :], fraw[:, raw_slot, :, :], ACT.Copy).then_inc(w_hi, 1)

            def split_ts(b, col, raw_slot, raw_n, used):
                act.wait_ge(fraw_in[raw_slot], raw_n)
                if used is not None:
                    act.wait_ge(proj_done, used)
                A(tsH[:, :, col, :], fraw[:, raw_slot, :, :], ACT.Copy).then_inc(w_hi, 1)

            split_ws(0, 0, 0, 16, None)
            split_ws(1, 1, 1, 16, None)
            for k in range(KD):
                act.wait_ge(xt_done, k + 1)
                A(xnH[:, k, :], bank[k], ACT.Copy, scale=gain_mix[k]).then_inc(xh_done, 1)
            split_ts(2, 0, 2, 16, None)
            split_ts(3, 1, 3, 16, None)

            def split(h, b):
                raw_n = 16 * 2 * h + 16 * (2 + b // 4)
                if b < 4:
                    split_ws(b, b % 2, b % 4, raw_n, 8 * h + (1, 2, 7, 8)[b])
                else:
                    split_ts(b, b - 4, b % 4, raw_n, 8 * h + 6)

            def exps(h, us):
                for u in us:
                    tiles, _ = span(UNITS[u][0])
                    w = len(tiles) * P
                    act.wait_ge(nm_ready, 8 * h + u + 1)
                    if u >= 2:
                        act.wait_ge(pT_done, 8 * h + (u - 1))
                    elif not first(h):
                        act.wait_ge(pT_done, 8 * h)
                    a = UNITS[u][1]
                    A(sbuf_p[:, a, 0:w], sbuf_s[:, a, 0:w], ACT.Exp, bias=att[:, 8 + u:9 + u], scale=SCALE,
                      accum_out=att[:, 16 + u:17 + u]).then_inc(p_ready, 1)

            def evac_pT(h, us):
                for u in us:
                    tiles, _ = span(UNITS[u][0])
                    a = UNITS[u][1]
                    act.wait_ge(pT_done, 8 * h + u + 1)
                    if u >= 2:
                        act.wait_ge(att_done, 8 * h + (u - 1))
                    elif not first(h):
                        act.wait_ge(att_done, 8 * h)
                    A(pTs[:, a, 0:len(tiles), :], bank[2 + a][:, 0:len(tiles) * P].rearrange("p (i s) -> p i s", s=P),
                      ACT.Copy).then_inc(pT_ready, 1)

            def token_gates(h, j):
                act.wait_ge(proj_done, 8 * h + (PRE_G + 4 + j + 1))
                if j == 0 and not first(h):
                    act.wait_ge(att_step, 2 * h)
                A(tht[:, j, :, :], bank[j % 2][:, P:4 * P].rearrange("p (b n) -> p b n", b=3), ACT.Tanh,
                  scale=0.5).then_inc(tht_ready, 1)

            def table_ahead(func, n):
                A(stat[:, 48 + n:49 + n], eps, func)

            def norm_square(h):
                act.wait_ge(o_done, h + 1)
                A(ogt[:, :, :], bank[6].rearrange("p (j v) -> p j v", j=NT), ACT.Square).then_inc(osq_ready, 1)

            def norm_sqrt(h):
                act.wait_ge(oms_ready, h + 1)
                A(orow[:, 4:8], orow[:, 8:12], ACT.Sqrt, scale=1.0 / P, bias=eps).then_inc(osd_ready, 1)

            def exp_cum(h, d):
                cum, qd, ki = ((thF, qdF, kiF), (thB, qdB, kiB))[d]
                act.wait_ge(cum_ready, 2 * h + d + 1)
                A(qd[:, :], cum[:, :], ACT.Exp).then_inc(ec_ready, 1)
                A(ki[:, :], cum[:, :], ACT.Exp, scale=-1.0).then_inc(ec_ready, 1)

            def evac_kT(h, d):
                act.wait_ge(kT_done, 2 * h + d + 1)
                if d == 0 and not first(h):
                    act.wait_ge(U_done, 2 * h)
                A((ktF, ktB)[d][:, :, :], bank[2].rearrange("p (j s) -> p j s", j=NT), ACT.Copy).then_inc(kt_ready, 1)

            def values_by_chunk(h):
                act.wait_ge(v_ready, 4 * h + 4)
                act.wait_ge(U_done, 2 * h)
                A(vab[0:CH, :, 0, :], vv[0:CH, :, :], ACT.Copy).then_inc(vab_ready, 1)
                A(vab[CH:P, :, 1, :], vv[CH:P, :, :], ACT.Copy).then_inc(vab_ready, 1)

            def head(h, is_first, is_last):
                pg = 8 * h + PRE_G
                if is_first:
                    split(h, 0)
                    split(h, 1)
                act.wait_ge(proj_done, pg + 1)
                if not is_first:
                    act.wait_ge(s_done, 8 * h)
                A(aqT[:, :], bank[0], ACT.Copy).then_inc(aq_ready, 1)
                split(h, 2)
                act.wait_ge(proj_done, pg + 2)
                if not is_first:
                    act.wait_ge(ec_ready, 4 * h)
                A(thF[:, :], bank[1], ACT.Tanh, scale=0.5).then_inc(th_ready, 1)
                split(h, 3)
                split(h, 4)
                split(h, 5)
                exps(h, (0, 1))
                act.wait_ge(proj_done, pg + 3)
                A(thB[:, :], bank[0], ACT.Tanh, scale=0.5).then_inc(th_ready, 1)
                split(h, 6)
                split(h, 7)
                if not is_first:
                    norm_square(h - 1)
                evac_pT(h, (0, 1))
                exps(h, (2, 3))
                if not is_first:
                    norm_sqrt(h - 1)
                act.wait_ge(proj_done, pg + 4)
                if not is_first:
                    act.wait_ge(qk_ready, 4 * h)
                A(qp[:, :], bank[1], ACT.Tanh, scale=0.5).then_inc(th_ready, 1)
                evac_pT(h, (2, 3))
                exps(h, (4, 5))
                act.wait_ge(f_ready, 2 * h + 2)
                act.wait_ge(k_ready, 2 * h + 2)
                A(fF[:, :], fF[:, :], ACT.Ln).then_inc(ln_ready, 1)
                A(fB[:, :], fB[:, :], ACT.Ln).then_inc(ln_ready, 1)
                token_gates(h, 0)
                if not is_last:
                    split(h + 1, 0)
                evac_pT(h, (4, 5))
                exps(h, (6, 7))
                if not is_first:
                    act.wait_ge(o_done, h)
                    act.wait_ge(dc_ready, 2 * h)
                exp_cum(h, 0)
                token_gates(h, 1)
                if not is_last:
                    split(h + 1, 1)
                evac_pT(h, (6, 7))
                exp_cum(h, 1)
                act.wait_ge(nm_ready, 8 * h + 8)
                act.wait_ge(l_step, 3 * h + 1)
                A(att[:, 32:40], att[:, 24:32], ACT.Exp).then_inc(se_ready, 1)
                token_gates(h, 2)
                evac_kT(h, 0)
                token_gates(h, 3)
                evac_kT(h, 1)

            at_head(head, act)
            values_by_chunk(NH - 1)
            for q in range(3):
                high(act, 0, q)
            table_ahead(ACT.Sqrt, 0)
            norm_square(NH - 1)
            norm_sqrt(NH - 1)

            for k in range(KD):
                act.wait_ge(mT_done, k + 1)
                A(mTH[:, k, :], bank[2 + k % 6], ACT.Copy).then_inc(mh_done, 1)
            high(act, 0, 3)

            def second_norm(j):
                act.wait_ge(h_ready, 2 * j + 2)
                if j >= 2:
                    act.wait_ge(x2_out[j % 2], 16)
                    act.wait_ge(rT_done, 2 * (j - 2) + 2)
                A(xr[:, j % 2, :], hres[:, j, :], ACT.Square, accum_out=stat[:, 16 + j:17 + j]).then_inc(sq1, 1)
                act.wait_ge(sq1, j + 1)
                A(stat[:, 24 + j:25 + j], stat[:, 16 + j:17 + j], ACT.Sqrt, scale=1.0 / D, bias=eps).then_inc(sd1, 1)

            def rows_turned(j):
                for half in range(2):
                    act.wait_ge(rT_done, 2 * j + half + 1)
                    A(rT[:, 4 * half:4 * half + 4, j * P:(j + 1) * P],
                      bank[half].rearrange("p (k t) -> p k t", k=4), ACT.Copy).then_inc(rT_ready, 1)

            second_norm(0)
            second_norm(1)
            rows_turned(0)
            second_norm(2)
            rows_turned(1)
            second_norm(3)
            rows_turned(2)
            rows_turned(3)
            for b in (4, 5, 6):
                high(act, 0, b)
            act.wait_ge(r_step, RS_MAX)
            for j in range(NT):
                A(gst[:, j, 0:4], v8[:, j, 0:4], ACT.Exp, bias=gst[:, j, 4:5], accum_out=gst[:, j, 5:6]).then_inc(rexp_ready, 1)

            def x_high(i, last_up):
                for b_ in range(2):
                    act.wait_ge(xT_done, 2 * i + b_ + 1)
                    if b_ == 0 and last_up is not None:
                        act.wait_ge(p_used, last_up)
                    A(xTH[:, 4 * b_:4 * b_ + 4, :], bank[6 + b_][:, 0:4 * BLK].rearrange("p (k s) -> p k s", k=4), ACT.Copy).then_inc(xTh_ready, 1)

            def a_high(i, last_down):
                for b_ in range(2):
                    act.wait_ge(aT_done, 2 * i + b_ + 1)
                    if b_ == 0 and last_down is not None:
                        act.wait_ge(p_used, last_down)
                    A(aTH[:, 4 * b_:4 * b_ + 4, :], bank[6 + b_][:, 0:4 * BLK].rearrange("p (k s) -> p k s", k=4), ACT.Copy).then_inc(aTh_ready, 1)

            def sigmoid(i):
                act.wait_ge(g_ready, i + 1)
                if not first(i):
                    act.wait_ge(act_ready, i)
                A(sg[0:BLK, :], gcl[0:BLK, :], ACT.Sigmoid, scale=ALPHA).then_inc(sg_ready, 1)

            def y_evac(i, over=False):
                act.wait_ge(p_used, used(down_at(i, over), 4))
                if not first(i):
                    act.wait_ge(y_out, 16 * i)
                A(ysb[0:BLK, :], ybank[0:BLK, :], ACT.Copy).then_inc(y_ready, 1)

            high(act, 0, 7)
            x_high(0, None)
            for p in range(4, 8):
                high(act, 0, 4 + p)
            high(act, 1, 0)
            table_ahead(ACT.Sigmoid, 1)
            x_high(1, used(up_at(0), 8))
            sigmoid(0)
            high(act, 1, 1)
            high(act, 1, 2)

            def body(i, prefetch, is_second):
                high(act, i, 3)
                a_high(i - 1, None if is_second else used((i, 0), 0))
                for b in range(4, 12):
                    high(act, i, b)
                if prefetch:
                    x_high(i + 1, used((i, 0), 8))
                sigmoid(i)
                high(act, i + 1, 0)
                high(act, i + 1, 1)
                if prefetch:
                    high(act, i + 1, 2)
                y_evac(i - 1)

            body(1, True, True)
            with act.Fori(2, NE - 1) as i:
                body(i, True, False)
            body(NE - 1, False, False)
            a_high(NE - 1, used((NE - 1, 8), 4))
            high(act, NE, 2)
            high(act, NE, 3)
            y_evac(NE - 1)

            def overflow(i):
                x_high(i, used((i, 0), 0))
                for p in range(8):
                    high(act, i, 4 + p)
                sigmoid(i)
                a_high(i, used((i, 0), 4))
                for q in range(4):
                    high(act, i + 1, q)
                y_evac(i, True)
            run_overflow(act, overflow)

            table_ahead(ACT.Sqrt, 2)
            for j in range(NT):
                act.wait_ge(acc_step, 4 * j + 4)
                if j >= 2:
                    act.wait_ge(out_done[j % 2], 16)
                A(fin[:, j % 2, :], acc[:, j % 2, :], ACT.Square, accum_out=stat[:, 32 + j:33 + j]).then_inc(sq2, 1)
                act.wait_ge(sq2, j + 1)
                A(stat[:, 40 + j:41 + j], stat[:, 32 + j:33 + j], ACT.Sqrt, scale=1.0 / D, bias=eps).then_inc(sd2, 1)
                if j < NT - 1:
                    act.wait_ge(rs2, j + 1)
                    A(fin[:, j % 2, :], acc[:, j % 2, :], ACT.Copy, scale=stat[:, 44 + j:45 + j]).then_inc(fs_ready, 1)

        @block.vector
        def _(dve):
            V = nc.vector
            dve.wait_ge(vecT_done, 1)
            V.tensor_copy(vecs[:, :], bank[0][:, 0:R_END]).then_inc(vec_ready, 1)
            dve.wait_ge(vec_ready, 1)
            lbv = vecs[:, 0:32].rearrange("p (d l h) -> p d l h", d=2, l=2)
            mx = lbs[:, 4, :].rearrange("p (d h) -> p d h", d=2)
            V.tensor_tensor(mx, lbv[:, :, 0, :], lbv[:, :, 1, :], ALU.max).then_inc(vec_ready, 1)
            dve.wait_ge(vec_ready, 2)
            for l in range(2):
                V.tensor_tensor(lbs[:, l, :].rearrange("p (d h) -> p d h", d=2), lbv[:, :, l, :], mx, ALU.subtract).then_inc(lb_step, 1)
            for j in range(NT):
                dve.wait_ge(sd0, j + 1)
                V.reciprocal(stat[:, 12 + j:13 + j], stat[:, 8 + j:9 + j]).then_inc(rs0, 1)
                dve.wait_ge(rs0, j + 1)
                V.tensor_scalar(xt[:, j, :], xt[:, j, :], stat[:, 12 + j:13 + j], None, ALU.mult).then_inc(xn0, 1)
            dve.wait_ge(lb_exp, 1)
            V.tensor_tensor(lbs[:, 5, :], lbs[:, 2, :], lbs[:, 3, :], ALU.add).then_inc(lb_step, 1)
            dve.wait_ge(lb_step, 3)
            V.reciprocal(lbs[:, 6, :], lbs[:, 5, :]).then_inc(lb_step, 1)
            dve.wait_ge(lb_step, 4)
            V.tensor_tensor(lbs[:, 7, :], lbs[:, 2, :], lbs[:, 6, :], ALU.mult).then_inc(lb_step, 1)
            dve.wait_ge(lb_step, 5)
            for t, (m, a) in ((fa, (-0.5, 0.5)), (fb_, (0.5, 0.5)), (fn, (0.25, -0.25)), (fk, (-0.25, 0.25))):
                V.tensor_scalar(t[:, :], lbs[:, 7, :], m, a, ALU.mult, ALU.add).then_inc(lb_step, 1)
            dve.wait_ge(bc_in, 32)
            V.tensor_scalar(gainq[:, :], gainq[:, :], 0.25, None, ALU.mult).then_inc(lb_step, 1)

            def low(n, out_, raw, high):
                dve.wait_ge(w_hi, n)
                V.tensor_tensor(out_, raw, high.bitcast(F32), ALU.subtract).then_inc(w_lo, 1)

            low(1, wsL[:, 0, :, :], fraw[:, 0, :, :], wsH[:, 0, :, :])
            for k in range(KD):
                dve.wait_ge(xh_done, k + 1)
                V.scalar_tensor_tensor(out=xnL[:, k, :], in0=bank[k], scalar=gain_mix[k], in1=xnH[:, k, :].bitcast(F32),
                                       op0=ALU.mult, op1=ALU.subtract).then_inc(xl_done, 1)
            low(2, wsL[:, 1, :, :], fraw[:, 1, :, :], wsH[:, 1, :, :])
            low(3, tsL[:, :, 0, :], fraw[:, 2, :, :], tsH[:, :, 0, :])
            low(4, tsL[:, :, 1, :], fraw[:, 3, :, :], tsH[:, :, 1, :])

            def split(h, b):
                n = 8 * h + (PRE_B + b + 1)
                if b < 4:
                    low(n, wsL[:, b % 2, :, :], fraw[:, b % 4, :, :], wsH[:, b % 2, :, :])
                else:
                    low(n, tsL[:, :, b - 4, :], fraw[:, b % 4, :, :], tsH[:, :, b - 4, :])

            split(0, 0)
            for kt_ in range(2):
                dve.wait_ge(proj_done, kt_ + 1)
                V.tensor_copy(kdup[0:DH, 2 * kt_, :], bank[kt_][0:DH, :]).then_inc(kd_ready, 1)
                V.tensor_copy(kdup[DH:P, 2 * kt_ + 1, :], bank[kt_][DH:P, :]).then_inc(kd_ready, 1)
            split(0, 1)
            for j in range(NT):
                dve.wait_ge(proj_done, 2 + j + 1)
                V.tensor_scalar(av[:, j, :], bank[j % 2][:, 0:KVH * DH], 0.5, None, ALU.mult).then_inc(av_ready, 1)

            def states(h, d):
                U, S, dc = ((nc_psum[:, 4 * 512:6 * 512], SF, dcF), (nc_psum[:, 6 * 512:8 * 512], SB, dcB))[d]
                U = U.rearrange("p (n v) -> p n v", n=NCH)
                n0 = 14 * h + 7 * d
                dve.wait_ge(U_done, 2 * h + d + 1)
                if not first(h):
                    dve.wait_ge(o_done, h)
                src, dst = ((0, 7), (1, 8)) if d == 0 else ((1, 8), (0, 7))
                V.tensor_tensor(S[:, dst[0]:dst[1], :], U[:, src[0]:src[1], :],
                                dc[:, src[0]:src[1]].unsqueeze(2).to_broadcast([P, 7, P]), ALU.mult).then_inc(st_ready, 1)
                for s in range(6):
                    n, b = (2 + s, 1 + s) if d == 0 else (5 - s, 6 - s)
                    dve.wait_ge(st_ready, n0 + (s + 1))
                    V.scalar_tensor_tensor(out=S[:, n, :], in0=S[:, b, :], scalar=dc[:, b:b + 1], in1=S[:, n, :],
                                           op0=ALU.mult, op1=ALU.add).then_inc(st_ready, 1)

            def softmax_front(h, us):
                for u in us:
                    n, a = UNITS[u]
                    tiles, c0 = span(n)
                    w = len(tiles) * P
                    dve.wait_ge(s_done, 8 * h + u + 1)
                    if u >= 2:
                        dve.wait_ge(p_ready, 8 * h + (u - 1))
                    elif not first(h):
                        dve.wait_ge(p_ready, 8 * h)
                    V.scalar_tensor_tensor(out=sbuf_s[:, a, 0:w], in0=cst[:, K_REL + c0:K_REL + c0 + w],
                                           scalar=cst[:, bass.ds(2 * h + (K_SL + a), 1)], in1=bank[4 + a][:, 0:w],
                                           op0=ALU.mult, op1=ALU.add).then_inc(s_ready, 1)
                for u in us:
                    n, a = UNITS[u]
                    w = len(span(n)[0]) * P
                    dve.wait_ge(s_ready, 8 * h + u + 1)
                    V.tensor_reduce(att[:, u:u + 1], sbuf_s[:, a, 0:w], AX.X, ALU.max).then_inc(mx_ready, 1)
                for u in us:
                    a = UNITS[u][1]
                    dve.wait_ge(mx_ready, 8 * h + u + 1)
                    if u == 0 and not first(h):
                        dve.wait_ge(l_step, 3 * h)
                    V.tensor_scalar(att[:, 8 + u:9 + u], att[:, u:u + 1], -SCALE, nsink[:, bass.ds(2 * h + a, 1)],
                                    ALU.mult, ALU.min).then_inc(nm_ready, 1)

            def gate(h, d):
                th, f, k = ((thF, fF, kF), (thB, fB, kB))[d]
                dve.wait_ge(th_ready, 3 * h + d + 1)
                if d == 0 and not first(h):
                    dve.wait_ge(qk_ready, 4 * h)
                col = bass.ds(h + 8 * d, 1)
                V.tensor_scalar(f[:, :], th[:, :], fa[:, col], fb_[:, col], ALU.mult, ALU.add).then_inc(f_ready, 1)
                V.tensor_scalar(k[:, :], th[:, :], fn[:, col], fk[:, col], ALU.mult, ALU.add).then_inc(k_ready, 1)

            def cumulate(h, d):
                th, f, keep = ((thF, fF, K_KF), (thB, fB, K_KB))[d]
                dve.wait_ge(ln_ready, 2 * h + d + 1)
                dve.wait_ge(f_ready, 2 * h + 2)
                dve.wait_ge(k_ready, 2 * h + 2)
                step = 1 if d == 0 else -1
                V.tensor_tensor_scan(th[:, ::step], cst[:, K_KF:K_KB] if d == 0 else cst[:, K_KB:K_REL][:, ::-1],
                                     f[:, ::step], 0.0, ALU.mult, ALU.add).then_inc(cum_ready, 1)

            def chunk_decay(h, d):
                qd, dc, c = ((qdF, dcF, CH - 1), (qdB, dcB, 0))[d]
                dve.wait_ge(ec_ready, 4 * h + 2 * d + 2)
                V.tensor_copy(dc[:, :], qd[:, :].rearrange("p (n c) -> p n c", c=CH)[:, :, c]).then_inc(dc_ready, 1)

            def token_tile(h, j):
                dve.wait_ge(tht_ready, 4 * h + j + 1)
                if j == 0 and not first(h):
                    dve.wait_ge(mg_ready, h)
                    dve.wait_ge(U_done, 2 * h)
                V.tensor_copy(vv[:, j, :], bank[j % 2][:, 0:P]).then_inc(v_ready, 1)
                V.scalar_tensor_tensor(out=G1[:, j, :], in0=tht[:, j, 0, :], scalar=1.0, in1=bank[j % 2][:, P:2 * P],
                                       op0=ALU.add, op1=ALU.mult).then_inc(ts_free, 1)
                dve.wait_ge(ts_free, 4 * h + j + 1)
                V.scalar_tensor_tensor(out=G1[:, j, :], in0=tht[:, j, 1, :], scalar=1.0, in1=G1[:, j, :],
                                       op0=ALU.add, op1=ALU.mult).then_inc(G1_step, 1)

            def mask_scores(h, d):
                sc, m = ((scF, K_TF), (scB, K_TB))[d]
                dve.wait_ge(zeroed, 3)
                dve.wait_ge(sc_done, 2 * h + d + 1)
                V.copy_predicated(sc[:, :, :], cst[:, m:m + P].bitcast(I32).unsqueeze(1).to_broadcast([P, NT, P]),
                                  bank[3].rearrange("p (j c) -> p j c", j=NT)).then_inc(sc_ready, 1)

            def norm_stats(h):
                dve.wait_ge(osq_ready, h + 1)
                V.tensor_reduce(orow[:, 8:12], ogt[:, :, :], AX.X, ALU.add).then_inc(oms_ready, 1)

            def gated_output(h):
                dve.wait_ge(osd_ready, h + 1)
                V.reciprocal(orow[:, 12:16], orow[:, 4:8]).then_inc(ors_ready, 1)
                dve.wait_ge(ors_ready, h + 1)
                dve.wait_ge(G1_ready, 4 * h + 4)
                for j in range(NT):
                    V.scalar_tensor_tensor(out=ogt[:, j, :], in0=bank[6][:, j * P:(j + 1) * P], scalar=orow[:, 12 + j:13 + j],
                                           in1=G1[:, j, :], op0=ALU.mult, op1=ALU.mult).then_inc(og_ready, 1)
                dve.wait_ge(og_ready, 4 * h + 4)
                dve.wait_ge(ma_ready, h + 1)
                m = merged[:, :, bass.ds(h * P, P)]
                V.tensor_tensor(m, m, ogt[:, :, :], ALU.add).then_inc(mg_ready, 1)

            def sink_sum(h, part):
                if part == 0:
                    dve.wait_ge(nm_ready, 8 * h + 8)
                    V.tensor_tensor(att[:, 24:32].rearrange("p (n a) -> p n a", a=2),
                                    att[:, 8:16].rearrange("p (n a) -> p n a", a=2),
                                    sinkb[:, bass.ds(2 * h, 2)].unsqueeze(1).to_broadcast([P, NT, 2]), ALU.add).then_inc(l_step, 1)
                else:
                    dve.wait_ge(se_ready, h + 1)
                    dve.wait_ge(p_ready, 8 * h + 8)
                    V.tensor_tensor(att[:, 40:48], att[:, 32:40], att[:, 16:24], ALU.add).then_inc(l_step, 1)
                    dve.wait_ge(l_step, 3 * h + 2)
                    V.reciprocal(att[:, 48:56], att[:, 40:48]).then_inc(l_step, 1)

            def gated_attention(h):
                dve.wait_ge(l_step, 3 * h + 3)
                dve.wait_ge(att_done, 8 * h + 8)
                V.tensor_tensor(attn1[:, :, :].rearrange("p j (a d) -> p (j a) d", a=2),
                                bank[7].rearrange("p (g d) -> p g d", d=DH),
                                att[:, 48:56].unsqueeze(2).to_broadcast([P, 8, DH]), ALU.mult).then_inc(att_step, 1)
                dve.wait_ge(att_step, 2 * h + 1)
                dve.wait_ge(tht_ready, 4 * h + 4)
                V.scalar_tensor_tensor(out=attn1[:, :, :], in0=tht[:, :, 2, :], scalar=1.0, in1=attn1[:, :, :],
                                       op0=ALU.add, op1=ALU.mult).then_inc(att_step, 1)
                dve.wait_ge(att_step, 2 * h + 2)
                V.tensor_copy(merged[:, :, bass.ds(h * P, P)], attn1[:, :, :]).then_inc(ma_ready, 1)

            def head(h, is_first, is_last):
                split(h, 2)
                if not is_first:
                    states(h - 1, 0)
                    states(h - 1, 1)
                split(h, 3)
                softmax_front(h, (0, 1))
                gate(h, 0)
                split(h, 4)
                split(h, 5)
                if not is_first:
                    norm_stats(h - 1)
                softmax_front(h, (2, 3))
                gate(h, 1)
                split(h, 6)
                split(h, 7)
                if not is_first:
                    gated_output(h - 1)
                dve.wait_ge(th_ready, 3 * h + 3)
                V.scalar_tensor_tensor(out=qp[:, :], in0=qp[:, :], scalar=1.0, in1=bank[1], op0=ALU.add,
                                       op1=ALU.mult).then_inc(q_ready, 1)
                softmax_front(h, (4, 5))
                cumulate(h, 0)
                cumulate(h, 1)
                token_tile(h, 0)
                if not is_last:
                    split(h + 1, 0)
                softmax_front(h, (6, 7))
                sink_sum(h, 0)
                chunk_decay(h, 0)
                token_tile(h, 1)
                if not is_last:
                    split(h + 1, 1)
                chunk_decay(h, 1)
                sink_sum(h, 1)
                token_tile(h, 2)
                mask_scores(h, 0)
                token_tile(h, 3)
                gated_attention(h)
                mask_scores(h, 1)

            def low_piece(k, b):
                low_part(dve, V, k, b, p_lo)

            dve.wait_ge(nsink_ready, 1)
            dve.wait_ge(cst_in, 16)
            at_head(head, dve)
            states(NH - 1, 0)
            states(NH - 1, 1)
            low_piece(0, 0)
            norm_stats(NH - 1)
            gated_output(NH - 1)

            for k in range(KD):
                dve.wait_ge(mh_done, k + 1)
                V.tensor_tensor(mTL[:, k, :], bank[2 + k % 6], mTH[:, k, :].bitcast(F32), ALU.subtract).then_inc(ml_done, 1)
            low_piece(0, 2)
            low_piece(0, 3)
            dve.wait_ge(h_in, 16 * NT)
            step = [0]

            def chain(ins):
                ins.then_inc(r_step, 1)
                step[0] += 1
                dve.wait_ge(r_step, step[0])

            def second_norm(j):
                if j < NT - 1:
                    dve.wait_ge(wo_done, j + 1)
                else:
                    dve.wait_ge(p_used, 4)
                for n in range(2):
                    hs = hres[:, j, n * 512:(n + 1) * 512]
                    V.tensor_tensor(hs, hs, bank[2 * j + n], ALU.add).then_inc(h_ready, 1)
                dve.wait_ge(sd1, j + 1)
                V.reciprocal(stat[:, 28 + j:29 + j], stat[:, 24 + j:25 + j]).then_inc(rs1, 1)
                dve.wait_ge(rs1, j + 1)
                dve.wait_ge(gains_in, 32)
                V.scalar_tensor_tensor(out=xr[:, j % 2, :], in0=hres[:, j, :], scalar=stat[:, 28 + j:29 + j], in1=ngain[:, :],
                                       op0=ALU.mult, op1=ALU.mult).then_inc(xr_ready, 1)

            def largest(j):
                dve.wait_ge(lg_done, j + 1)
                chain(V.tensor_tensor(lg[:, j, :], bank[2 + j][:, 0:NE], brb[:, :], ALU.add))
                chain(V.max(v8[:, j, :], lg[:, j, :]))
                V.max_index(i8[:, j, :], v8[:, j, :], lg[:, j, :]).then_inc(mi_ready, 1)

            dve.wait_ge(wr_in, 32)
            second_norm(0)
            second_norm(1)
            second_norm(2)
            largest(0)
            second_norm(3)
            for j in range(1, NT):
                largest(j)
            dve.wait_ge(mi_ready, NT)
            chain(V.tensor_copy(idf[:, :, :], i8[:, :, :]))
            chain(V.tensor_scalar(gst[:, :, 4], v8[:, :, 0], -1.0, None, ALU.mult))
            assert step[0] == RS_MAX
            chain(V.tensor_tensor(oh[:, :, :, :],
                                  cst[:, K_IO:K_IO + NE].unsqueeze(1).unsqueeze(1).to_broadcast([P, NT, TOPK, NE]),
                                  idf[:, :, 0:TOPK].unsqueeze(3).to_broadcast([P, NT, TOPK, NE]), ALU.is_equal))
            with nc.allow_low_precision(reason="a sum of zeros and at most one one"):
                V.tensor_reduce(msk[:, 0:NT, :], oh[:, :, :, :].rearrange("p j k e -> p j e k"), AX.X, ALU.add).then_inc(mask_ready, 1)
            dve.wait_ge(pos_done, 1)
            chain(V.tensor_tensor(pk[:, :, :, :], oh[:, :, :, :],
                                  bank[6][:, 0:NT * NE].rearrange("p (j e) -> p j e", j=NT).unsqueeze(2).to_broadcast([P, NT, TOPK, NE]),
                                  ALU.mult))
            chain(V.tensor_reduce(posk[:, :], pk[:, :, :, :].rearrange("p j k e -> p (j k) e"), AX.X, ALU.add))
            chain(V.tensor_tensor(past[:, :, :], posk[:, :].unsqueeze(2).to_broadcast([P, NT * TOPK, NB - 1]),
                                  cst[:, K_TH:K_END].unsqueeze(1).to_broadcast([P, NT * TOPK, NB - 1]), ALU.is_ge))
            chain(V.tensor_reduce(blk_[:, :], past[:, :, :], AX.X, ALU.add))
            V.scalar_tensor_tensor(out=colf[:, :].rearrange("p (j k) -> p j k", j=NT), in0=idf[:, :, 0:TOPK], scalar=float(NBC),
                                   in1=blk_[:, :].rearrange("p (j k) -> p j k", j=NT), op0=ALU.mult,
                                   op1=ALU.add).then_inc(place_ready, 1)
            chain(V.scalar_tensor_tensor(out=slotf[:, :], in0=blk_[:, :], scalar=float(-BLK), in1=posk[:, :],
                                         op0=ALU.mult, op1=ALU.add))
            dve.wait_ge(place_ready, 1)
            for n in range(NT * TOPK):
                V.tensor_scalar(hot_slot[:, n, :], cst[:, K_IO:K_IO + P], slotf[:, n:n + 1], None,
                                ALU.is_equal).then_inc(hot_slot_ready, 1)
                if n not in POOL_HOT:
                    V.tensor_scalar(hot_col[:, n, :], cst[:, K_IO:K_LT], colf[:, n:n + 1], cst[:, K_AS + n:K_AS + n + 1],
                                    ALU.is_equal, ALU.mult).then_inc(hot_col_ready, 1)
            chain(V.tensor_copy(msum[:, :], bank[6][:, NT * NE:(NT + 1) * NE]))
            table = bank[7][:, 0:NE * NBC]
            dve.wait_ge(tabT_done, 1)
            chain(V.tensor_scalar(empty[:, :], table, 0.0, float(NONE + 1), ALU.is_equal, ALU.mult))
            chain(V.scalar_tensor_tensor(out=tabf[:, :], in0=table, scalar=-1.0, in1=empty[:, :], op0=ALU.add, op1=ALU.add))
            V.tensor_copy(tab[:, :, 1], tabf[:, :]).then_inc(tab_ready, 1)
            dve.wait_ge(tab_ready, 1)
            V.tensor_scalar(tab[:, :, 0], tab[:, :, 1], NONE | (T - 1), None, ALU.bitwise_and).then_inc(tab_ready, 1)
            low_piece(0, 4)
            low_piece(0, 6)

            def gates_and_overflow():
                for j in range(NT):
                    dve.wait_ge(rexp_ready, j + 1)
                chain(V.reciprocal(gst[:, :, 6], gst[:, :, 5]))
                chain(V.tensor_tensor(gates[:, :, :], gst[:, :, 0:4], gst[:, :, 6:7].to_broadcast([P, NT, TOPK]), ALU.mult))
                chain(V.tensor_tensor(ovf[:, 0, :].rearrange("p (e b) -> p e b", b=NB - 1),
                                      msum[:, :].unsqueeze(2).to_broadcast([P, NE, NB - 1]),
                                      cst[:, K_TH:K_END].unsqueeze(1).to_broadcast([P, NE, NB - 1]), ALU.is_gt))
                chain(V.memset(ovf[:, 1, :], 1.0))
                chain(V.tensor_tensor_scan(ovf[:, 2, :], ovf[:, 1, :], ovf[:, 0, :], 0.0, ALU.mult, ALU.add))
                chain(V.tensor_copy(ovc[:, 0:1], ovf[:, 2, NE * (NB - 1) - 1:]))
                chain(V.scalar_tensor_tensor(out=ovf[:, 3, :], in0=ovf[:, 2, :], scalar=cst[:, K_P1:K_P1 + 1], in1=ovf[:, 0, :],
                                             op0=ALU.is_equal, op1=ALU.mult))
                chain(V.tensor_tensor(ovf[:, 1, :], ovf[:, 3, :], cst[:, K_CD:K_CD + NE * (NB - 1)], ALU.mult))
                chain(V.tensor_reduce(ovc[:, 1:2], ovf[:, 1, :], AX.X, ALU.add))
                chain(V.tensor_copy(ovi[:, 0:1], ovc[:, 1:2]))
                V.tensor_copy(regs_in[:, 0:1], ovc[:, 0:1]).then_inc(over_ready, 1)

            def x_low(i):
                for b_ in range(2):
                    dve.wait_ge(xTh_ready, 2 * i + b_ + 1)
                    V.tensor_tensor(xTL[:, 4 * b_:4 * b_ + 4, :], bank[6 + b_][:, 0:4 * BLK].rearrange("p (k s) -> p k s", k=4),
                                    xTH[:, 4 * b_:4 * b_ + 4, :].bitcast(F32), ALU.subtract).then_inc(xTl_ready, 1)

            def a_low(i):
                for b_ in range(2):
                    dve.wait_ge(aTh_ready, 2 * i + b_ + 1)
                    V.tensor_tensor(aTL[:, 4 * b_:4 * b_ + 4, :], bank[6 + b_][:, 0:4 * BLK].rearrange("p (k s) -> p k s", k=4),
                                    aTH[:, 4 * b_:4 * b_ + 4, :].bitcast(F32), ALU.subtract).then_inc(aTl_ready, 1)

            def select(s_, e, after):
                if after is not None:
                    dve.wait_ge(p_used, after)
                V.tensor_scalar(sel[:, s_, :], cst[0:3 * NE, bass.ds(K_SE + e, 1)].to_broadcast([3 * NE, P]), 1.0, None,
                                ALU.mult).then_inc(sel_ready[s_], 1)

            def clamp(i, over=False):
                dve.wait_ge(p_used, used(up_at(i, over), 8))
                if not first(i):
                    dve.wait_ge(act_ready, i)
                V.tensor_scalar(gcl[0:BLK, :], hu[0:BLK, 0:FF], LIMIT, None, ALU.min).then_inc(g_ready, 1)
                V.tensor_scalar(ucl[0:BLK, :], hu[0:BLK, FF:2 * FF], LIMIT, -LIMIT, ALU.min, ALU.max).then_inc(ucl_ready, 1)

            def swiglu(i):
                dve.wait_ge(g_ready, i + 1)
                dve.wait_ge(ucl_ready, i + 1)
                V.scalar_tensor_tensor(out=ucl[0:BLK, :], in0=ucl[0:BLK, :], scalar=1.0, in1=gcl[0:BLK, :], op0=ALU.add,
                                       op1=ALU.mult).then_inc(t_ready, 1)
                dve.wait_ge(t_ready, i + 1)
                dve.wait_ge(sg_ready, i + 1)
                if not first(i):
                    dve.wait_ge(aT_done, 2 * i)
                V.tensor_tensor(actv[0:BLK, :], ucl[0:BLK, :], sg[0:BLK, :], ALU.mult).then_inc(act_ready, 1)

            select(0, 0, None)
            x_low(0)
            low_piece(0, 7)
            low_piece(0, 8)
            gates_and_overflow()
            for b in (10, 11):
                low_piece(0, b)
            low_piece(1, 0)
            clamp(0)
            select(0, 1, None)
            select(1, 0, None)
            x_low(1)
            swiglu(0)
            low_piece(1, 2)

            def body(i, prefetch):
                low_piece(i, 3)
                a_low(i - 1)
                for b in (4, 6, 7, 8, 10):
                    low_piece(i, b)
                clamp(i)
                if prefetch:
                    select(0, i + 1, None)
                low_piece(i, 11)
                if prefetch:
                    x_low(i + 1)
                swiglu(i)
                low_piece(i + 1, 0)
                if prefetch:
                    low_piece(i + 1, 2)
                select(1, i, BODY * i + 9)

            with dve.Fori(1, NE - 1) as i:
                body(i, True)
            body(NE - 1, False)
            a_low(NE - 1)
            low_piece(NE, 2)
            low_piece(NE, 3)

            def overflow(i, code):
                e = nc.s_assert_within(code >> NBC_BITS, 0, NE - 1, skip_runtime_bounds_check_because="codes are below NE * NBC")
                select(0, e, None)
                select(1, e, BODY * i + 1)
                x_low(i)
                for b in (4, 6, 7, 8, 10, 11):
                    low_piece(i, b)
                clamp(i, True)
                swiglu(i)
                a_low(i)
                for q in (0, 2, 3):
                    low_piece(i + 1, q)
            run_overflow(dve, overflow, needs_code=True)

            def gather_sum(j):
                if j >= 2:
                    dve.wait_ge(fs_ready, j - 1)
                if 0 < j < NT - 1:
                    dve.wait_ge(yk_in[j - 1], 16 * TOPK)
                for k in range(TOPK):
                    if j in (0, NT - 1):
                        dve.wait_ge(yk_edge[min(j, 1) * TOPK + k], 16)
                    if k:
                        dve.wait_ge(acc_step, 4 * j + k)
                    V.scalar_tensor_tensor(out=acc[:, j % 2, :], in0=yk[:, j, k, :], scalar=gates[:, j, k:k + 1],
                                           in1=acc[:, j % 2, :] if k else hres[:, j, :], op0=ALU.mult, op1=ALU.add).then_inc(acc_step, 1)

            def final_norm(j):
                dve.wait_ge(sd2, j + 1)
                V.reciprocal(stat[:, 44 + j:45 + j], stat[:, 40 + j:41 + j]).then_inc(rs2, 1)
                if j < NT - 1:
                    return
                dve.wait_ge(rs2, j + 1)
                dve.wait_ge(gains_in, 32)
                V.scalar_tensor_tensor(out=fin[:, j % 2, :], in0=acc[:, j % 2, :], scalar=stat[:, 44 + j:45 + j], in1=fgain[:, :],
                                       op0=ALU.mult, op1=ALU.mult).then_inc(fin_ready, 1)

            for j in range(NT):
                gather_sum(j)
                if j:
                    final_norm(j - 1)
            final_norm(NT - 1)

        @block.gpsimd
        def _(gp):
            G = nc.gpsimd
            G.memset(scF[:, :, :], 0.0).then_inc(zeroed, 1)
            G.memset(scB[:, :, :], 0.0).then_inc(zeroed, 1)
            G.memset(vab[:, :, :, :], 0.0).then_inc(zeroed, 1)
            gp.wait_ge(bc_in, 32)
            G.tensor_scalar(nsink[:, :], sinkb[:, :], -1.0, None, ALU.mult).then_inc(nsink_ready, 1)
            for kv in range(KVH):
                src, dst = (slice(0, DH), slice(DH, P)) if kv % 2 == 0 else (slice(DH, P), slice(0, DH))
                gp.wait_ge(kd_ready, 2 * (kv // 2) + 2)
                gp.dma_start(kdup[dst, kv, :], kdup[src, kv, :]).then_inc(kdup_in, 16)
            gp.wait_ge(kdup_in, 16 * KVH)
            gp.wait_ge(av_ready, NT)

            def decayed(h, d):
                qd, ki, k = ((qdF, kiF, kF), (qdB, kiB, kB))[d]
                gp.wait_ge(ec_ready, 4 * h + 2 * d + 2)
                gp.wait_ge(dc_ready, 2 * h + d + 1)
                gp.wait_ge(q_ready, h + 1)
                gp.wait_ge(k_ready, 2 * h + 2)
                G.tensor_tensor(qd[:, :], qp[:, :], qd[:, :], ALU.mult).then_inc(qk_ready, 1)
                G.tensor_tensor(ki[:, :], k[:, :], ki[:, :], ALU.mult).then_inc(qk_ready, 1)

            def kv_of(h):
                kv = h // 2
                if not first(h):
                    gp.wait_ge(s_done, 8 * h)
                src = kdup[:, kv, :] if isinstance(h, int) else kdup[:, bass.ds(kv, 1), :].rearrange("p o t -> p (o t)")
                G.tensor_copy(kcur[:, :], src).then_inc(kcur_ready, 1)
                if not first(h):
                    gp.wait_ge(att_done, 8 * h)
                G.tensor_copy(vcur[:, :, :], av[:, :, bass.ds(kv * DH, DH)]).then_inc(vcur_ready, 1)

            def head(h, is_first, is_last):
                decayed(h, 0)
                decayed(h, 1)
                for j in range(NT):
                    gp.wait_ge(G1_step, 4 * h + j + 1)
                    G.tensor_tensor(G1[:, j, :], G1[:, j, :], gainq[:, :], ALU.mult).then_inc(G1_ready, 1)
                if is_last:
                    return
                gp.wait_ge(zeroed, 3)
                gp.wait_ge(v_ready, 4 * h + 4)
                if not is_first:
                    gp.wait_ge(U_done, 2 * h)
                gp.wait_ge(G1_ready, 4 * h + 4)
                G.tensor_copy(vab[0:CH, :, 0, :], vv[0:CH, :, :]).then_inc(vab_ready, 1)
                gp.wait_ge(zeroed, 3)
                gp.wait_ge(vab_ready, 2 * h + 1)
                G.tensor_copy(vab[CH:P, :, 1, :], vv[CH:P, :, :]).then_inc(vab_ready, 1)
                gp.wait_ge(vab_ready, 2 * h + 2)
                kv_of(h + 1)

            gp.wait_ge(zeroed, 3)
            gp.wait_ge(lb_step, 10)
            kv_of(0)
            at_head(head, gp)

            def low_piece(k, b):
                low_part(gp, G, k, b, p_lop)

            low_piece(0, 1)
            gp.wait_ge(mg_ready, NH)
            G.memset(msk[:, NT, :], 0.0).then_inc(tri_ready, 1)
            G.tensor_copy(tri[:, :, :], cst[:, K_LT:K_CD].rearrange("p (a s) -> p a s", a=2)).then_inc(tri_ready, 1)

            gp.wait_ge(b_in, 16 * 6)
            step = [0]

            def chain(ins):
                ins.then_inc(b_step, 1)
                step[0] += 1
                gp.wait_ge(b_step, step[0])

            chain(G.tensor_copy(bias[:, :], braw[:, :]))
            for left in (2 * NE, NE):
                chain(G.tensor_tensor(braw[0:left, :], braw[0:left, :], bias[0:left, :], ALU.subtract))
                chain(G.tensor_copy(bias[0:left, :], braw[0:left, :]))
            assert step[0] == BIAS_STEPS
            gp.wait_ge(lg_done, NT)
            G.memset(xg[:, :], 0.0).then_inc(xg_zero, 1)
            gp.wait_ge(p_used, 4)
            gp.wait_ge(place_ready, 1)
            for n in POOL_HOT:
                G.tensor_scalar(hot_col[:, n, :], cst[:, K_IO:K_LT], colf[:, n:n + 1], cst[:, K_AS + n:K_AS + n + 1],
                                ALU.is_equal, ALU.mult).then_inc(hot_col_p_ready, 1)
            gp.wait_ge(xg_zero, 1)
            gp.wait_ge(tab_ready, 2)
            gp.wait_ge(x2_out[0], 32)
            gp.wait_ge(x2_out[1], 32)

            last_token, last_assignment = gp.to_reg(T - 1), gp.to_reg(TOPK * T - 1)

            def gather(i, code):
                if not first(i):
                    gp.wait_ge(xT_done, 2 * i)
                src = tab[:, code, :] if isinstance(code, int) else tab[:, bass.ds(code, 1), :].rearrange("p o c -> p (o c)")
                G.tensor_copy(ixg[:, :], src).then_inc(ix_ready, 1)
                n = i + 1 if isinstance(i, int) else gp.to_reg(i + 1)
                gp.wait_ge(x2_out[0], 32)
                gp.wait_ge(ix_ready, n)
                gp.indirect_dma_start(xg[0:BLK, :], None, x2d, bass.IndirectOffsetOnAxis(ap=ixg[0:BLK, 0:1], axis=0),
                                      bounds_check=last_token, oob_is_err=False).then_inc(xg_in, 16)

            def scatter(i, code):
                src = tab[:, code, :] if isinstance(code, int) else tab[:, bass.ds(code, 1), :].rearrange("p o c -> p (o c)")
                n, last = (i + 1, 16 * i) if isinstance(i, int) else (gp.to_reg(i + 1), gp.to_reg(16 * i))
                gp.wait_ge(tab_ready, 2)
                gp.wait_ge(y_ready, n)
                if not first(i):
                    gp.wait_ge(y_out, last)
                G.tensor_copy(ixs[:, :], src).then_inc(ixs_ready, 1)
                gp.wait_ge(tab_ready, 2)
                gp.wait_ge(ixs_ready, i + 1)
                gp.indirect_dma_start(yd, bass.IndirectOffsetOnAxis(ap=ixs[0:BLK, 1:2], axis=0), ysb[0:BLK, :], None,
                                      bounds_check=last_assignment, oob_is_err=False).then_inc(y_out, 16)

            gather(0, 0)
            low_piece(0, 5)
            low_piece(0, 9)
            gather(1, NBC)

            def body(i, prefetch, is_second):
                low_piece(i, 1)
                if prefetch:
                    gather(i + 1, NBC * (i + 1))
                if not is_second:
                    scatter(i - 2, NBC * (i - 2))
                low_piece(i, 5)
                low_piece(i, 9)

            body(1, True, True)
            body(2, True, False)
            with gp.Fori(3, NE - 1) as i:
                body(i, True, False)
            body(NE - 1, False, False)
            low_piece(NE, 1)
            scatter(NE - 2, NBC * (NE - 2))
            scatter(NE - 1, NBC * (NE - 1))
            gp.wait_ge(y_out, 16 * NE)

            def overflow(i, code):
                code = gp.snap(code)
                gather(i, code)
                low_piece(i, 5)
                low_piece(i, 9)
                low_piece(i + 1, 1)
                scatter(i, code)
                gp.wait_ge(y_out, 16 * i + 16)
            run_overflow(gp, overflow, needs_code=True)
            G.memset(done[:, :], 0.0).then_inc(experts_done, 1)

            gp.wait_ge(gains_in, 32)
            for j in range(NT - 1):
                gp.wait_ge(fs_ready, j + 1)
                G.tensor_tensor(fin[:, j % 2, :], fin[:, j % 2, :], fgain[:, :], ALU.mult).then_inc(fin_p_ready, 1)


_INS = ['x', 'norm_mix_gain', 'w_in', 'hg_lb_fwd', 'hg_lb_bwd', 'hg_norm_gain', 'attn_sink', 'w_out',
        'norm_ffn_gain', 'w_router', 'b_router', 'w_up_gate', 'b_up_gate', 'w_down', 'b_down', 'final_norm_gain']


def kernel(**inputs):
    import concourse.bacc as bacc
    from concourse.bass_utils import run_bass_kernel_spmd

    nc = bacc.Bacc("TRN2", target_bir_lowering=False, num_devices=1)
    arrays = {n: np.ascontiguousarray(inputs[n]) for n in _INS}
    arrays["consts"] = constants()
    args = [nc.dram_tensor(f"in_{n}", a.shape, mybir.dt.from_np(a.dtype), kind="ExternalInput").ap()
            for n, a in arrays.items()]
    out = nc.dram_tensor("out_0", (1, T, D), F32, kind="ExternalOutput").ap()
    build(nc, *args, out)
    r = run_bass_kernel_spmd(nc, [{f"in_{n}": a for n, a in arrays.items()}], core_ids=[0])
    return r.results[0]["out_0"]
```
